# Optimizing a Trainium2 kernel written in Bass

```python
import math
import jax, jax.numpy as jnp
from jax import lax
import numpy as np

D_MODEL = 2048
BATCH = 1
SEQ = 256
DEPTH = 2
DEC_BATCH = 8
DEC_SEQ = 4
PAST_LEN = 2048
PAGE_SIZE = 128

N_MIXERS = 2
N_A_LAYERS = (DEPTH + 1) // 2
N_B_LAYERS = DEPTH // 2
A_HEADS = 8
A_DK = D_MODEL // (2 * A_HEADS)
A_DV = D_MODEL // A_HEADS
A_CHUNK = 64
B_EXPAND = 2
B_DINNER = B_EXPAND * D_MODEL
B_HEADDIM = 64
B_HEADS = B_DINNER // B_HEADDIM
B_GROUPS = 8
B_DSTATE = 128
B_DCONV = 4
B_CONV_DIM = B_DINNER + 2 * B_GROUPS * B_DSTATE
B_CHUNK = 128
D_FF = 5632
FFN_CONV = 3
EPS = 1e-6

kernel_name = 'hybrid_mlstm_mamba2_convffn_step'

F32 = jnp.float32

def _rmsnorm(x, w):
    xf = x.astype(F32)
    y = xf * lax.rsqrt(jnp.mean(xf * xf, axis=-1, keepdims=True) + EPS)
    return (y * w.astype(F32)).astype(x.dtype)

def _chunk_len(L, c):
    c = min(c, L)
    while L % c:
        c -= 1
    return c

def _causal_dwconv(x, buf, w, b):
    K = w.shape[0]
    L = x.shape[1]
    xp = jnp.concatenate([buf.astype(x.dtype), x], axis=1)
    y = xp[:, 0:L] * w[0]
    for j in range(1, K):
        y = y + xp[:, j:j + L] * w[j]
    return y + b, xp[:, L:]

def _mlstm_chunk_scan(q, k, v, ig, lf, C0, n0, m0):
    Bn, H, L, _ = q.shape
    DV = v.shape[-1]
    c = _chunk_len(L, A_CHUNK)
    nc = L // c

    def to_chunks(a):
        return jnp.moveaxis(a.reshape(a.shape[:2] + (nc, c) + a.shape[3:]), 2, 0)

    causal = jnp.tril(jnp.ones((c, c), dtype=bool))

    def step(carry, inp):
        C, n, m = carry
        qc, kc, vc, ic, fc = inp
        b = jnp.cumsum(fc, axis=-1)
        logD = jnp.where(causal, b[..., :, None] - b[..., None, :] + ic[..., None, :], -jnp.inf)
        inter = b + m[..., None]
        m_t = jnp.maximum(inter, jnp.max(logD, axis=-1))
        Dm = jnp.exp(logD - m_t[..., None])
        w_inter = jnp.exp(inter - m_t)
        s = jnp.einsum('bhtd,bhsd->bhts', qc, kc) * Dm
        num = w_inter[..., None] * jnp.einsum('bhtd,bhde->bhte', qc, C) + jnp.einsum('bhts,bhse->bhte', s, vc)
        den = w_inter * jnp.einsum('bhtd,bhd->bht', qc, n) + jnp.sum(s, axis=-1)
        h = num / jnp.maximum(jnp.abs(den), jnp.exp(-m_t))[..., None]
        m_new = m_t[..., -1]
        w_state = jnp.exp(b[..., -1:] - b + ic - m_new[..., None])
        decay = jnp.exp(inter[..., -1] - m_new)
        C_new = decay[..., None, None] * C + jnp.einsum('bhs,bhsd,bhse->bhde', w_state, kc, vc)
        n_new = decay[..., None] * n + jnp.einsum('bhs,bhsd->bhd', w_state, kc)
        return (C_new, n_new, m_new), h

    (C, n, m), hs = lax.scan(step, (C0, n0, m0), tuple(map(to_chunks, (q, k, v, ig, lf))))
    h = jnp.moveaxis(hs, 0, 2).reshape(Bn, H, L, DV)
    return h, C, n, m

def _mlstm_mixer(h, C0, n0, m0, w_in, b_if, w_out):
    Bn, L, _ = h.shape
    HK, HV = A_HEADS * A_DK, A_HEADS * A_DV
    proj = h @ w_in
    q, k, v, o, gates = jnp.split(proj, [HK, 2 * HK, 2 * HK + HV, 2 * HK + 2 * HV], axis=-1)

    def heads(a, d):
        return a.reshape(Bn, L, A_HEADS, d).transpose(0, 2, 1, 3).astype(F32)

    q = heads(q, A_DK)
    k = heads(k, A_DK) * (A_DK ** -0.5)
    v = heads(v, A_DV)
    gates = (gates.astype(F32) + b_if.astype(F32)).transpose(0, 2, 1)
    ig = gates[:, :A_HEADS]
    lf = jax.nn.log_sigmoid(gates[:, A_HEADS:])
    ht, C, n, m = _mlstm_chunk_scan(q, k, v, ig, lf, C0.astype(F32), n0.astype(F32), m0.astype(F32))
    ht = ht.transpose(0, 2, 1, 3).reshape(Bn, L, HV)
    out = (jax.nn.sigmoid(o.astype(F32)) * ht).astype(h.dtype) @ w_out
    return out, C, n, m

def _ssd_chunk_scan(x, dt, A, Bm, Cm, h0):
    Bn, L, H, P = x.shape
    G, N = Bm.shape[2], Bm.shape[3]
    R = H // G
    c = _chunk_len(L, B_CHUNK)
    nc = L // c
    xs = jnp.moveaxis(x.reshape(Bn, nc, c, G, R, P), 1, 0)
    dts = jnp.moveaxis(dt.reshape(Bn, nc, c, G, R), 1, 0)
    Bs = jnp.moveaxis(Bm.reshape(Bn, nc, c, G, N), 1, 0)
    Cs = jnp.moveaxis(Cm.reshape(Bn, nc, c, G, N), 1, 0)
    A_gr = A.reshape(G, R)
    causal = jnp.tril(jnp.ones((c, c), dtype=bool))[None, :, :, None, None]

    def step(hs, inp):
        xc, dtc, Bc, Cc = inp
        acum = jnp.cumsum(dtc * A_gr, axis=1)
        seg = acum[:, :, None] - acum[:, None, :]
        decay = jnp.exp(jnp.where(causal, seg, -jnp.inf))
        cb = jnp.einsum('btgn,bsgn->btsg', Cc, Bc)
        wts = cb[..., None] * decay * dtc[:, None]
        y = jnp.einsum('btsgr,bsgrp->btgrp', wts, xc)
        y = y + jnp.einsum('btgn,bgrpn->btgrp', Cc, hs) * jnp.exp(acum)[..., None]
        to_end = jnp.exp(acum[:, -1:] - acum) * dtc
        hs = jnp.exp(acum[:, -1])[..., None, None] * hs + jnp.einsum('bsgr,bsgrp,bsgn->bgrpn', to_end, xc, Bc)
        return hs, y

    hT, ys = lax.scan(step, h0.reshape(Bn, G, R, P, N), (xs, dts, Bs, Cs))
    y = jnp.moveaxis(ys, 0, 1).reshape(Bn, L, H, P)
    return y, hT.reshape(Bn, H, P, N)

def _gated_group_rmsnorm(y, z, w):
    g = y * jax.nn.silu(z)
    g = g.reshape(y.shape[:-1] + (B_GROUPS, B_DINNER // B_GROUPS))
    g = g * lax.rsqrt(jnp.mean(g * g, axis=-1, keepdims=True) + EPS)
    return g.reshape(y.shape) * w

def _mamba_mixer(h, ssm0, conv0, w_in, conv_w, conv_b, dt_bias, A_log, D_skip, norm_w, w_out):
    Bn, L, _ = h.shape
    proj = h @ w_in
    z, xBC, dt = jnp.split(proj, [B_DINNER, B_DINNER + B_CONV_DIM], axis=-1)
    xBC, conv_new = _causal_dwconv(xBC, conv0, conv_w, conv_b)
    xBC = jax.nn.silu(xBC.astype(F32))
    xs, Bm, Cm = jnp.split(xBC, [B_DINNER, B_DINNER + B_GROUPS * B_DSTATE], axis=-1)
    xs = xs.reshape(Bn, L, B_HEADS, B_HEADDIM)
    Bm = Bm.reshape(Bn, L, B_GROUPS, B_DSTATE)
    Cm = Cm.reshape(Bn, L, B_GROUPS, B_DSTATE)
    dt = jax.nn.softplus(dt.astype(F32) + dt_bias.astype(F32))
    A = -jnp.exp(A_log.astype(F32))
    y, ssm_new = _ssd_chunk_scan(xs, dt, A, Bm, Cm, ssm0.astype(F32))
    y = y + D_skip.astype(F32)[:, None] * xs
    y = _gated_group_rmsnorm(y.reshape(Bn, L, B_DINNER), z.astype(F32), norm_w.astype(F32))
    return y.astype(h.dtype) @ w_out, ssm_new, conv_new

def _conv_ffn(h, buf, w_up, conv_w, conv_b, w_down):
    u = h @ w_up
    u, buf_new = _causal_dwconv(u, buf, conv_w, conv_b)
    g, val = jnp.split(u, 2, axis=-1)
    return (jax.nn.silu(g) * val) @ w_down, buf_new

def _forward(x, mC, mn, mm, ssm, sconv, fconv, p):
    nC, nn_, nm, nssm, nsconv, nfconv = [], [], [], [], [], []
    for i in range(DEPTH):
        j = i // N_MIXERS
        hn = _rmsnorm(x, p['norm_mix'][i])
        if i % N_MIXERS == 0:
            out, C, n, m = _mlstm_mixer(hn, mC[j], mn[j], mm[j], p['a_w_in'][j], p['a_b_if'][j], p['a_w_out'][j])
            nC.append(C)
            nn_.append(n)
            nm.append(m)
        else:
            out, s_new, c_new = _mamba_mixer(hn, ssm[j], sconv[j], p['b_w_in'][j], p['b_conv_w'][j], p['b_conv_b'][j],
                                             p['b_dt_bias'][j], p['b_A_log'][j], p['b_D'][j], p['b_norm_w'][j], p['b_w_out'][j])
            nssm.append(s_new)
            nsconv.append(c_new)
        x = x + out.astype(x.dtype)
        hn = _rmsnorm(x, p['norm_ffn'][i])
        out, fb = _conv_ffn(hn, fconv[i], p['f_w_up'][i], p['f_conv_w'][i], p['f_conv_b'][i], p['f_w_down'][i])
        nfconv.append(fb)
        x = x + out.astype(x.dtype)
    y = _rmsnorm(x, p['norm_final'])
    return (y, jnp.stack(nC), jnp.stack(nn_), jnp.stack(nm), jnp.stack(nssm), jnp.stack(nsconv), jnp.stack(nfconv))

def setup_inputs(seed: int = 0) -> dict:
    key = jax.random.key(seed)
    ks = iter(jax.random.split(key, 48))

    def nrm(shape, scale):
        return scale * jax.random.normal(next(ks), shape, F32)

    a_cols = 2 * A_HEADS * A_DK + 2 * A_HEADS * A_DV + 2 * A_HEADS
    b_cols = B_DINNER + B_CONV_DIM + B_HEADS
    i_bias = nrm((N_A_LAYERS, A_HEADS), 0.1)
    f_bias = jnp.linspace(3.0, 6.0, A_HEADS, dtype=F32)[None] + nrm((N_A_LAYERS, A_HEADS), 0.1)
    dt0 = jnp.exp(jax.random.uniform(next(ks), (N_B_LAYERS, B_HEADS), F32, math.log(1e-3), math.log(1e-1)))
    b_dt_bias = dt0 + jnp.log(-jnp.expm1(-dt0))
    b_A_log = jnp.log(jax.random.uniform(next(ks), (N_B_LAYERS, B_HEADS), F32, 1.0, 16.0))
    return {
        'x_prompt': nrm((BATCH, SEQ, D_MODEL), 1.0),
        'x_sample': nrm((DEC_BATCH, DEC_SEQ, D_MODEL), 1.0),
        'state_mlstm_C': nrm((N_A_LAYERS, DEC_BATCH, A_HEADS, A_DK, A_DV), 0.3),
        'state_mlstm_n': nrm((N_A_LAYERS, DEC_BATCH, A_HEADS, A_DK), 0.3),
        'state_mlstm_m': nrm((N_A_LAYERS, DEC_BATCH, A_HEADS), 1.0),
        'state_ssm': nrm((N_B_LAYERS, DEC_BATCH, B_HEADS, B_HEADDIM, B_DSTATE), 0.5),
        'state_ssm_conv': nrm((N_B_LAYERS, DEC_BATCH, B_DCONV - 1, B_CONV_DIM), 1.0),
        'state_ffn_conv': nrm((DEPTH, DEC_BATCH, FFN_CONV - 1, 2 * D_FF), 1.0),
        'norm_mix': 1.0 + nrm((DEPTH, D_MODEL), 0.05),
        'norm_ffn': 1.0 + nrm((DEPTH, D_MODEL), 0.05),
        'norm_final': 1.0 + nrm((D_MODEL,), 0.05),
        'a_w_in': nrm((N_A_LAYERS, D_MODEL, a_cols), D_MODEL ** -0.5),
        'a_b_if': jnp.concatenate([i_bias, f_bias], axis=-1),
        'a_w_out': nrm((N_A_LAYERS, A_HEADS * A_DV, D_MODEL), (A_HEADS * A_DV) ** -0.5),
        'b_w_in': nrm((N_B_LAYERS, D_MODEL, b_cols), D_MODEL ** -0.5),
        'b_conv_w': nrm((N_B_LAYERS, B_DCONV, B_CONV_DIM), B_DCONV ** -0.5),
        'b_conv_b': nrm((N_B_LAYERS, B_CONV_DIM), 0.02),
        'b_dt_bias': b_dt_bias,
        'b_A_log': b_A_log,
        'b_D': 1.0 + nrm((N_B_LAYERS, B_HEADS), 0.1),
        'b_norm_w': 1.0 + nrm((N_B_LAYERS, B_DINNER), 0.05),
        'b_w_out': nrm((N_B_LAYERS, B_DINNER, D_MODEL), B_DINNER ** -0.5),
        'f_w_up': nrm((DEPTH, D_MODEL, 2 * D_FF), D_MODEL ** -0.5),
        'f_conv_w': nrm((DEPTH, FFN_CONV, 2 * D_FF), FFN_CONV ** -0.5),
        'f_conv_b': nrm((DEPTH, 2 * D_FF), 0.02),
        'f_w_down': nrm((DEPTH, D_FF, D_MODEL), D_FF ** -0.5),
    }

def reference(x_prompt, x_sample, state_mlstm_C, state_mlstm_n, state_mlstm_m, state_ssm, state_ssm_conv,
              state_ffn_conv, norm_mix, norm_ffn, norm_final, a_w_in, a_b_if, a_w_out, b_w_in, b_conv_w,
              b_conv_b, b_dt_bias, b_A_log, b_D, b_norm_w, b_w_out, f_w_up, f_conv_w, f_conv_b, f_w_down):
    p = {'norm_mix': norm_mix, 'norm_ffn': norm_ffn, 'norm_final': norm_final,
         'a_w_in': a_w_in, 'a_b_if': a_b_if, 'a_w_out': a_w_out,
         'b_w_in': b_w_in, 'b_conv_w': b_conv_w, 'b_conv_b': b_conv_b, 'b_dt_bias': b_dt_bias,
         'b_A_log': b_A_log, 'b_D': b_D, 'b_norm_w': b_norm_w, 'b_w_out': b_w_out,
         'f_w_up': f_w_up, 'f_conv_w': f_conv_w, 'f_conv_b': f_conv_b, 'f_w_down': f_w_down}
    Bp = x_prompt.shape[0]
    z_C = jnp.zeros((N_A_LAYERS, Bp, A_HEADS, A_DK, A_DV), F32)
    z_n = jnp.zeros((N_A_LAYERS, Bp, A_HEADS, A_DK), F32)
    z_m = jnp.zeros((N_A_LAYERS, Bp, A_HEADS), F32)
    z_ssm = jnp.zeros((N_B_LAYERS, Bp, B_HEADS, B_HEADDIM, B_DSTATE), F32)
    z_sconv = jnp.zeros((N_B_LAYERS, Bp, B_DCONV - 1, B_CONV_DIM), x_prompt.dtype)
    z_fconv = jnp.zeros((DEPTH, Bp, FFN_CONV - 1, 2 * D_FF), x_prompt.dtype)
    y_prompt, pC, pn, pm, pssm, psconv, pfconv = _forward(x_prompt, z_C, z_n, z_m, z_ssm, z_sconv, z_fconv, p)
    y_sample, sC, sn, sm, sssm, ssconv, sfconv = _forward(x_sample, state_mlstm_C, state_mlstm_n, state_mlstm_m,
                                                          state_ssm, state_ssm_conv, state_ffn_conv, p)
    return (y_prompt, y_sample, pC, sC, pn, sn, pm, sm, pssm, sssm, psconv, ssconv, pfconv, sfconv)


_drawn_inputs = setup_inputs


def setup_inputs(seed=0):
    import zlib

    import numpy as np

    out = dict(_drawn_inputs(seed))
    spreads = {}
    factors = {'f_conv_b': 3.875}
    for name, (base, spread) in spreads.items():
        noise = np.random.default_rng([zlib.crc32(name.encode()), seed]).standard_normal(out[name].shape)
        drawn = base * np.exp(spread * noise) if base else spread * noise
        out[name] = __import__('jax').numpy.asarray(drawn.astype(out[name].dtype))
    for name, factor in factors.items():
        out[name] = (out[name] * factor).astype(out[name].dtype)
    return out
```

```python
from contextlib import ExitStack, contextmanager

import numpy as np

import concourse.bass as bass
from concourse import mybir

F32 = mybir.dt.float32
F32R = mybir.dt.float32r
ACT = mybir.ActivationFunctionType
ALU = mybir.AluOpType

P = 128
D_MODEL = 2048
KT = D_MODEL // P
TP, NB, SL = 256, 8, 4
TS = NB * SL
T = TP + TS
A_HEADS, A_DK, A_DV = 8, 128, 256
B_HEADS, B_GROUPS = 64, 8
B_DINNER = 4096
D_FF = 5632
FT = D_FF // P
FH = FT // 2
EPS = 1e-6
BIG = 1e30
CH = 16 * P
DCH = FH // 2 * P
SC = TP + P + TS

C_AIN = 1
C_AOUT = C_AIN + 6 * A_HEADS
C_F0 = C_AOUT + KT
C_FHALF = 2 * FH + 2 * KT
C_BGATE = C_F0 + 2 * C_FHALF
C_BIN = C_BGATE + 1
C_BHALF = 40 + KT
C_F1 = C_BIN + 2 * C_BHALF
C_END = C_F1 + 2 * C_FHALF
N_AOUT = C_AOUT
N_F0 = C_F0
N_FHALF = 2 * FH + KT
N_BIN = N_F0 + 2 * N_FHALF + 1
N_F1 = N_BIN + 2 * C_BHALF
EA_F0 = 1 + 48
EA_BGATE = EA_F0 + 4 * FH
EA_BIN = EA_BGATE + 1
EA_F1 = EA_BIN + 80
ED_F0 = KT
ED_BIN = ED_F0 + 2 * KT
ED_F1 = ED_BIN + 2 * KT


SQ_RUNS = [1, 2, 4, 6, 8]


class Count:

    def __init__(self, base, *terms):
        self.base, self.terms = base, terms

    def plus(self, n):
        return Count(self.base + n, *self.terms)

    def times(self, n):
        return Count(self.base * n, *[(r, s * n) for r, s in self.terms])

    def add(self, reg, step):
        if isinstance(reg, int):
            return Count(self.base + reg * step, *self.terms)
        return Count(self.base, *self.terms, (reg, step))

    def half(self):
        return Count(self.base // 2, *[(r, s // 2) for r, s in self.terms])

    @property
    def value(self):
        v = self.base
        for r, s in self.terms:
            v = r * s + v
        return v


def wait(eng, sem, count):
    if isinstance(count, int):
        count = Count(count)
    if count.base <= 0:
        return
    eng.wait_ge(sem, count.value)


class Own:

    def __init__(self, eng, sem):
        self.eng, self.sem, self.n, self.terms = eng, sem, 0, []

    def mark(self, ins):
        ins.then_inc(self.sem, 1)
        self.n += 1

    def sync(self):
        wait(self.eng, self.sem, Count(self.n, *self.terms))

    def link(self, ins):
        self.mark(ins)
        self.sync()

    @contextmanager
    def loop(self, times, per):
        start = self.n
        with self.eng.Fori(0, times) as i:
            self.terms.append((i, per))
            yield i
            self.terms.pop()
        assert self.n - start == per, f"a turn of this loop counts {self.n - start}, not {per}"
        self.n = start + times * per


def trunk(nc, d, o):
    with ExitStack() as ctx:
        def sb(name, shape, dt=F32, stack=ctx):
            return stack.enter_context(nc.sbuf_tensor(name, shape, dt))

        def sem(name):
            return ctx.enter_context(nc.semaphore(name))

        x = sb("x", [P, KT, T])
        hn_hi = sb("hn_hi", [P, KT, T], F32R)
        hn_lo = sb("hn_lo", [P, KT, T], F32R)
        w_raw = sb("w_raw", [P, 2, CH])
        w_hi = sb("w_hi", [P, 2, CH], F32R)
        w_lo = sb("w_lo", [P, 2, CH], F32R)
        ident = sb("ident", [P, P])
        mean_mat = sb("mean_mat", [P, P])
        ones = sb("ones", [P, P])
        future = sb("future", [P, SC])
        seg_keep = sb("seg_keep", [64, T])
        seg_drop = sb("seg_drop", [8, T])
        in_batch = sb("in_batch", [TS, NB])
        norm_w = sb("norm_w", [P, 5, KT])
        f_conv = sb("f_conv", [P, 2, 2 * FT, 4])
        b_conv = sb("b_conv", [P, 48, 5])
        b_normw = sb("b_normw", [P, 32, 1])
        b_skip = sb("b_skip", [P, 32, 1])
        b_small = sb("b_small", [64, 2])
        a_small = sb("a_small", [8, 2 + NB])
        rstd = sb("rstd", [P, T])
        sumsq = sb("sumsq", [P, T])
        work = sb("work", [P, 2, T])

        with ExitStack() as st:
            a_out_hi = sb("a_out_hi", [P, KT, T], F32R, st)
            a_out_lo = sb("a_out_lo", [P, KT, T], F32R, st)
            a_io = sb("a_io", [P, 2, 6, T], F32, st)
            a_c = sb("a_c", [P, 2, NB, A_DV], F32, st)
            a_cp = sb("a_cp", [P, A_DV], F32, st)
            a_n = sb("a_n", [P, A_HEADS, NB], F32, st)
            a_nnew = sb("a_nnew", [P, A_HEADS, 1 + NB], F32, st)
            a_mnew = sb("a_mnew", [8, 1 + NB], F32, st)
            a_rows = sb("a_rows", [8, 9, T], F32, st)
            a_acol = sb("a_acol", [P, 8, 3], F32, st)
            a_wcol = sb("a_wcol", [P, 8, 3], F32, st)
            a_sel = sb("a_sel", [8, P], F32, st)
            a_dec = sb("a_dec", [P, SC], F32, st)
            a_prob = sb("a_prob", [P, SC], F32, st)
            a_kw = sb("a_kw", [P, 3, P], F32, st)
            a_vt = sb("a_vt", [P, 3, A_DV], F32, st)
            a_vm = sb("a_vm", [TS, NB, A_DV], F32, st)
            a_wi = sb("a_wi", [P, TS], F32, st)
            a_qs = sb("a_qs", [P, TS], F32, st)
            a_nq = sb("a_nq", [P, TS], F32, st)
        FP = 2 + TP + NB * (2 + SL)
        with ExitStack() as st:
            act_hi = sb("act_hi", [P, FH, T], F32R, st)
            act_lo = sb("act_lo", [P, FH, T], F32R, st)
            f_old = sb("f_old", [P, 2 * FT, NB * 2], F32, st)
            f_new = sb("f_new", [P, 2 * FT, (1 + NB) * 2], F32, st)
            f_pad = sb("f_pad", [P, 4, FP], F32, st)
            f_u = sb("f_u", [P, 4, FP], F32, st)
            f_act = sb("f_act", [P, 2, T], F32, st)
        BP = 3 + TP + NB * (3 + SL)
        with ExitStack() as st:
            b_out_hi = sb("b_out_hi", [P, KT, T], F32R, st)
            b_out_lo = sb("b_out_lo", [P, KT, T], F32R, st)
            b_io = sb("b_io", [P, 2, 10, T], F32, st)
            b_sT = sb("b_sT", [P, NB, P], F32, st)
            b_s = sb("b_s", [P, NB, P], F32, st)
            b_sp = sb("b_sp", [P, P], F32, st)
            b_old = sb("b_old", [P, 6, NB * 3], F32, st)
            b_new = sb("b_new", [P, 6, (1 + NB) * 3], F32, st)
            b_pad = sb("b_pad", [P, 2, BP], F32, st)
            b_u = sb("b_u", [P, BP], F32, st)
            b_yi = sb("b_yi", [P, TS], F32, st)
            b_rows = sb("b_rows", [64, 5, T], F32, st)
            b_rsum = sb("b_rsum", [64, TS + 1], F32, st)
            b_nac = sb("b_nac", [P, B_GROUPS, 3, 8], F32, st)
            b_dtc = sb("b_dtc", [P, B_GROUPS, 3, 8], F32, st)
            b_end = sb("b_end", [P, B_GROUPS, 3, 8], F32, st)
            b_sel = sb("b_sel", [64, 2, P], F32, st)
            b_cb = sb("b_cb", [P, SC], F32, st)
            b_dec = sb("b_dec", [P, 2, SC], F32, st)
            b_bt = sb("b_bt", [P, 3, P], F32, st)
            b_bm = sb("b_bm", [TS, NB, P], F32, st)
            b_xdt = sb("b_xdt", [P, 3, 4 * P], F32, st)
            b_xw = sb("b_xw", [P, 3, P], F32, st)
            b_ea = sb("b_ea", [P, TS], F32, st)

        a_h, a_den, a_em, b_y, b_r = work, rstd, sumsq, rstd, sumsq
        b_th = work[:, :, :].rearrange("p a t -> p (a t)")[:, 0:BP]

        ps = ctx.enter_context(nc.psum_tensor("ps", [P, 8, 512], F32))
        M0, M1, M2, M3 = 4, 5, 6, 7

        raw_landed = [sem("raw_landed0"), sem("raw_landed1")]
        w_high, w_low, chunk_done, taken_act, taken_dve = map(sem, ("w_high", "w_low", "chunk_done", "taken_act", "taken_dve"))
        consts_in, x_in, y_ready, y_stored = map(sem, ("consts_in", "x_in", "y_ready", "y_stored"))
        act_own, dve_own, pool_own, pool_passed, pe_passed = map(sem, ("act_own", "dve_own", "pool_own", "pool_passed", "pe_passed"))
        squared, sq_added, mean_ready, var_ready, root_ready = map(sem, (
            "squared", "sq_added", "mean_ready", "var_ready", "root_ready"))
        hn_ready, hn_hi_ready, hn_lo_ready = map(sem, ("hn_ready", "hn_hi_ready", "hn_lo_ready"))
        a_n_in, ga_raw, ga_exp, ga_onep, ga_ln, ga_logs, ga_rows, ga_turned, ga_done = map(sem, (
            "a_n_in", "ga_raw", "ga_exp", "ga_onep", "ga_ln", "ga_logs", "ga_rows", "ga_turned", "ga_done"))
        a_sel_ready, a_scores, a_kv0, a_dlog, a_dexp, a_kv0_tok, a_probs, a_v1, a_v1_tok, a_vmask = map(sem, (
            "a_sel_ready", "a_scores", "a_kv0", "a_dlog", "a_dexp", "a_kv0_tok", "a_probs", "a_v1", "a_v1_tok", "a_vmask"))
        a_num, a_htmp, a_hhi, a_hlo, a_cupd, a_cadd, a_cp_ready = map(sem, (
            "a_num", "a_htmp", "a_hhi", "a_hlo", "a_cupd", "a_cadd", "a_cp_ready"))
        a_c_in, a_c_out = [sem("a_c_in0"), sem("a_c_in1")], [sem("a_c_out0"), sem("a_c_out1")]
        a_cp_out, a_nm_out, a_steps = map(sem, ("a_cp_out", "a_nm_out", "a_steps"))
        f_old_in, f_prefix, f_tap0, f_tap1, f_conved, f_gated, f_silu, f_prod, f_ahi, f_alo, f_kept, f_new_out = map(sem, (
            "f_old_in", "f_prefix", "f_tap0", "f_tap1", "f_conved", "f_gated", "f_silu", "f_prod", "f_ahi", "f_alo", "f_kept", "f_new_out"))
        gb_raw, gb_abs, gb_exp, gb_onep, gb_ln, gb_logs, gb_rows, gb_turned, gb_done = map(sem, (
            "gb_raw", "gb_abs", "gb_exp", "gb_onep", "gb_ln", "gb_logs", "gb_rows", "gb_turned", "gb_done"))
        b_old_in, b_prefix, b_tap0, b_taps, b_conved, b_tanh, b_silu, b_kept, b_new_out, b_zready = map(sem, (
            "b_old_in", "b_prefix", "b_tap0", "b_taps", "b_conved", "b_tanh", "b_silu", "b_kept", "b_new_out", "b_zready"))
        b_cbx, b_cbx_out, b_xt_out, b_xs, b_xs_out, b_bmask, b_selr, b_rowsr, b_dlog, b_dexp, b_wts, b_xwr = map(sem, (
            "b_cbx", "b_cbx_out", "b_xt_out", "b_xs", "b_xs_out", "b_bmask", "b_selr", "b_rowsr", "b_dlog", "b_dexp",
            "b_wts", "b_xwr"))
        b_yst, b_decayed, b_sadd, b_spr, b_yg, b_gsq, b_gms, b_gvar, b_groot, b_gn, b_ghi, b_glo = map(sem, (
            "b_yst", "b_decayed", "b_sadd", "b_spr", "b_yg", "b_gsq", "b_gms", "b_gvar", "b_groot", "b_gn", "b_ghi", "b_glo"))
        b_s_in, b_sT_in, b_s_out, b_sp_out, b_steps = map(sem, ("b_s_in", "b_sT_in", "b_s_out", "b_sp_out", "b_steps"))

        def packed(ap, lo=TP):
            return ap[:, TP:T].rearrange("p (b l) -> p b l", l=SL)

        def f_samples(ap, n=FP):
            return ap[:, TP + 2:FP].rearrange("p (b l) -> p b l", l=SL + 2)

        def b_samples(ap):
            return ap[:, TP + 3:BP].rearrange("p (b l) -> p b l", l=SL + 3)

        CONSTS = [(ident, "ident"), (mean_mat, "mean_mat"), (ones, "ones"), (future, "future"), (seg_keep, "seg_keep"),
                  (seg_drop, "seg_drop"), (in_batch, "in_batch"), (norm_w, "norm_w"), (f_conv, "f_conv"),
                  (b_conv, "b_conv"), (b_normw, "b_normw"), (b_skip, "b_skip"), (b_small, "b_small"),
                  (a_small, "a_small")]
        N_CONSTS = 16 * len(CONSTS)

        block = ctx.enter_context(nc.Block())

        @block.sync
        def _(sp):
            def load(c, src, cols):
                wait(sp, w_low, c.plus(-1))
                sp.dma_start(w_raw[:, c.base % 2, 0:cols], src).then_inc(raw_landed[c.base % 2], 16)

            sp.dma_start(x[:], d["x"]).then_inc(x_in, 16)
            for tile, name in CONSTS:
                sp.dma_start(tile[:], d[name]).then_inc(consts_in, 16)
            sp.dma_start(a_n[:], d["a_n"]).then_inc(a_n_in, 16)
            load(Count(0), d["wa_gate"][0], CH)
            load(Count(1), d["wa_in"][0], CH)
            load(Count(2), d["wa_in"][1], CH)
            with sp.Fori(0, 23) as i:
                for j in range(2):
                    load(Count(C_AIN + 2 + j, (i, 2)), d["wa_in"][i * 2 + (2 + j)], CH)
            with sp.Fori(0, 8) as i:
                for j in range(2):
                    load(Count(C_AOUT + j, (i, 2)), d["wa_out"][i * 2 + j], CH)

            def ffn(c0, up, down):
                with sp.Fori(0, 2) as h:
                    with sp.Fori(0, FH) as i:
                        for j in range(2):
                            load(Count(c0 + j, (h, C_FHALF), (i, 2)), up[h * (2 * FH) + i * 2 + j], CH)
                    with sp.Fori(0, KT) as i:
                        for j in range(2):
                            load(Count(c0 + 2 * FH + j, (h, C_FHALF), (i, 2)), down[h * (2 * KT) + i * 2 + j], DCH)

            ffn(C_F0, d["wf_up0"], d["wf_down0"])
            load(Count(C_BGATE), d["wb_gate"][0], CH)
            with sp.Fori(0, 2) as h:
                with sp.Fori(0, 20) as i:
                    for j in range(2):
                        load(Count(C_BIN + j, (h, C_BHALF), (i, 2)), d["wb_in"][h * 40 + i * 2 + j], CH)
                with sp.Fori(0, KT // 2) as i:
                    for j in range(2):
                        load(Count(C_BIN + 40 + j, (h, C_BHALF), (i, 2)), d["wb_out"][h * KT + i * 2 + j], CH)
            ffn(C_F1, d["wf_up1"], d["wf_down1"])

        @block.tensor
        def _(pe):
            def gemm(c, bank, hi, lo, tiles, first=True, last=True, each=None):
                wait(pe, w_low, c.plus(1))
                s, out = c.base % 2, ps[:, bank, 0:T]
                for k, t in enumerate(tiles):
                    if each is not None:
                        each(k)
                    col = slice(k * P, (k + 1) * P)
                    end = last and k == len(tiles) - 1
                    nc.tensor.matmul(out, w_hi[:, s, col], hi[:, t, :], start=first and k == 0, stop=False)
                    nc.tensor.matmul(out, w_hi[:, s, col], lo[:, t, :], start=False, stop=False)
                    m = nc.tensor.matmul(out, w_lo[:, s, col], hi[:, t, :], start=False, stop=end)
                m.then_inc(chunk_done, 1)

            def mm(out, lhs, rhs, start=True, stop=True):
                return nc.tensor.matmul(out, lhs, rhs, start=start, stop=stop, skip_group_check=True)

            def project(c, taken, bank):
                wait(pe, taken_act, taken)
                gemm(c, bank, hn_hi, hn_lo, range(KT))

            def norm(k):
                wait(pe, sq_added, KT * SQ_RUNS[k])
                mm(ps[:, M0, 0:T], mean_mat[:], sumsq[:]).then_inc(mean_ready, 1)

            def first_project(c, bank, k):
                gemm(c, bank, hn_hi, hn_lo, range(KT), each=lambda t: wait(pe, hn_lo_ready, k * KT + t + 1))

            def score_blocks(bank, keys, queries):
                mm(ps[:, bank, 0:TP], keys[:, 0:P], queries[:, 0:TP])
                mm(ps[:, bank, TP:TP + P], keys[:, P:TP], queries[:, P:TP])
                return mm(ps[0:TS, bank, TP + P:SC], keys[:, TP:T], queries[:, TP:T])

            def turn(out, src):
                return nc.tensor.transpose(out, src, ident[:])

            def turn_blocks(bank, src):
                turn(ps[:, bank, 0:P], src[:, 0:P])
                turn(ps[:, bank, P:2 * P], src[:, P:TP])
                return turn(ps[0:TS, bank, 2 * P:3 * P], src[:, TP:T])

            pe.wait_ge(consts_in, N_CONSTS)
            norm(0)
            first_project(Count(0), 0, 0)
            def a_mix(u, p, j):
                q, k, v0, v1 = (a_io[:, p, n, :] for n in range(4))
                if j == 0:
                    wait(pe, a_sel_ready, u.plus(1))
                    wait(pe, taken_act, u.times(6).plus(1 + 4))
                    wait(pe, a_cadd, u.times(4))
                    wait(pe, a_cp_ready, u)
                    score_blocks(M0, k, q)
                    mm(ps[:, M1, 0:T], a_sel[:], a_rows[:, 5, :])
                    mm(ps[:, M1, T:T + TS], a_sel[:], a_rows[:, 8, TP:T]).then_inc(a_scores, 1)
                    turn_blocks(M2, k)
                    turn_blocks(M3, v0).then_inc(a_kv0, 1)
                if j == 1:
                    wait(pe, a_kv0_tok, u.plus(1))
                    turn_blocks(M2, v1)
                    mm(ps[:, M3, 0:T], a_sel[:], a_rows[:, 7, :]).then_inc(a_v1, 1)
                if j == 2:
                    wait(pe, a_probs, u.plus(1))
                    wait(pe, a_v1_tok, u.plus(1))
                    wait(pe, a_c_in[p], u.half().plus(1).times(16))
                    for e in range(2):
                        ec = slice(e * P, (e + 1) * P)
                        mm(ps[:, M0 + e, 0:TP], a_vt[:, 0, ec], a_prob[:, 0:TP], True, False)
                        mm(ps[:, M0 + e, P:TP], a_vt[:, 1, ec], a_prob[:, TP:TP + P], False, False)
                        mm(ps[:, M0 + e, TP:T], a_vt[0:TS, 2, ec], a_prob[0:TS, TP + P:SC], False, False)
                        for b in range(NB):
                            t = slice(TP + SL * b, TP + SL * (b + 1))
                            mm(ps[:, M0 + e, t], a_c[:, p, b, ec], a_qs[:, SL * b:SL * (b + 1)], False, True)
                    mm(ps[:, M2, 0:TP], ones[:], a_prob[:, 0:TP], True, False)
                    mm(ps[:, M2, P:TP], ones[:], a_prob[:, TP:TP + P], False, False)
                    mm(ps[:, M2, TP:T], ones[0:TS, :], a_prob[0:TS, TP + P:SC], False, False)
                    mm(ps[:, M2, TP:T], ones[:], a_nq[:], False, True).then_inc(a_num, 1)
                if j == 3:
                    wait(pe, a_htmp, u.plus(1).times(2))
                    wait(pe, a_vmask, u.plus(1))
                    mm(ps[:, M3, 0:A_DV], a_kw[:, 0, :], a_vt[:, 0, :], True, False)
                    mm(ps[:, M3, 0:A_DV], a_kw[:, 1, :], a_vt[:, 1, :], False, True)
                    mm(ps[:, M3, A_DV:A_DV + 1], a_kw[:, 0, :], ones[:, 0:1], True, False)
                    mm(ps[:, M3, A_DV:A_DV + 1], a_kw[:, 1, :], ones[:, 0:1], False, True)
                    mm(ps[:, M3, A_DV + 1:A_DV + 1 + NB], a_kw[0:TS, 2, :], in_batch[:])
                    for n in range(3):
                        mm(ps[:, M0 + n, :], a_kw[0:TS, 2, :], a_vm[:, 2 * n:2 * n + 2, :]).then_inc(a_cupd, 1)
                if j == 4:
                    wait(pe, a_cadd, u.times(4).plus(1))
                    mm(ps[:, M0, :], a_kw[0:TS, 2, :], a_vm[:, 6:8, :]).then_inc(a_cupd, 1)

            def a_head(u, p, mixed):
                c = u.times(6)
                for j in range(6):
                    cj = c.plus(C_AIN + j)
                    project(cj, c.plus(1 + j - 3), cj.base % 4)
                    if mixed is not None:
                        a_mix(mixed, 1 - p, j)

            a_head(Count(0), 0, None)
            pe.wait_ge(ga_rows, 1)
            for n, row in enumerate((4, 6)):
                for b in range(3):
                    w = P if b < 2 else TS
                    m = nc.tensor.transpose(ps[0:w, M1, 24 * n + 8 * b:24 * n + 8 * b + 8],
                                            a_rows[:, row, b * P:b * P + w], ident[0:8, 0:8])
            m.then_inc(ga_turned, 1)
            pe.wait_ge(ga_done, 1)
            a_head(Count(1), 1, Count(0))
            with pe.Fori(0, 3) as i:
                for n in range(2):
                    a_head(Count(2 + n, (i, 2)), n, Count(1 + n, (i, 2)))
            for j in range(6):
                a_mix(Count(7), 1, j)

            def project_out(c, n0, hi, lo, ready, ready_at):
                wait(pe, ready, ready_at)
                with pe.Fori(0, KT // 4) as i:
                    for j in range(4):
                        wait(pe, squared, Count(KT + j - 3, (i, 4)))
                        gemm(Count(c + j, (i, 4)), (n0 + j) % 4, hi, lo, range(KT))

            project_out(C_AOUT, N_AOUT, a_out_hi, a_out_lo, a_hlo, Count(2 * A_HEADS))

            def ffn(layer, c0, n0, ea0, ed0, k):
                norm(k)
                with pe.Fori(0, 2) as h:
                    with pe.Fori(0, FH // 2) as i:
                        for j in range(4):
                            wait(pe, taken_act, Count(ea0 + j - 3, (h, 2 * FH), (i, 4)))
                            if j == 0:
                                gemm(Count(c0 + j, (h, C_FHALF), (i, 4)), (n0 + j) % 4, hn_hi, hn_lo, range(KT),
                                     each=lambda t: wait(pe, hn_lo_ready, k * KT + t + 1))
                            else:
                                gemm(Count(c0 + j, (h, C_FHALF), (i, 4)), (n0 + j) % 4, hn_hi, hn_lo, range(KT))
                    wait(pe, f_alo, Count(layer * FT + FH // 2, (h, FH)))
                    pe.sem_inc(pe_passed, 1)
                    with pe.Fori(0, KT // 4) as i:
                        for j in range(4):
                            wait(pe, taken_dve, Count(ed0 + j - 3, (h, KT), (i, 4)))
                            for q in range(2):
                                if j == 0 and q == 1:
                                    wait(pe, f_alo, Count(layer * FT + FH, (h, FH)))
                                gemm(Count(c0 + 2 * FH + 2 * j + q, (h, C_FHALF), (i, 8)), (n0 + 2 * FH + j) % 4,
                                     act_hi, act_lo, range(q * FH // 2, (q + 1) * FH // 2), q == 0, q == 1)

            ffn(0, C_F0, N_F0, EA_F0, ED_F0, 1)
            norm(2)
            first_project(Count(C_BGATE), (N_BIN - 1) % 4, 2)
            pe.wait_ge(gb_rows, 1)
            for n, row in enumerate((0, 1, 2)):
                for b in range(3):
                    w = P if b < 2 else TS
                    m = nc.tensor.transpose(ps[0:w, M1 if n < 2 else M2, 192 * (n % 2) + 64 * b:192 * (n % 2) + 64 * b + 64],
                                            b_rows[:, row, b * P:b * P + w], ident[0:64, 0:64])
            m.then_inc(gb_turned, 1)
            pe.wait_ge(gb_done, 1)

            def b_mix(u, p, j):
                bT, cT = b_io[:, p, 0, :], b_io[:, p, 1, :]
                if j == 0:
                    wait(pe, b_silu, u.plus(1).times(6))
                    wait(pe, b_gvar, u)
                    wait(pe, b_sadd, u.times(8))
                    wait(pe, b_spr, u.times(4))
                    score_blocks(M0, bT, cT)
                    turn_blocks(M1, bT)
                    for k in range(4):
                        turn(ps[:, M2, k * P:(k + 1) * P], b_io[:, p, 2 + k, 0:P])
                        m = turn(ps[:, M3, k * P:(k + 1) * P], b_io[:, p, 2 + k, P:TP])
                    m.then_inc(b_cbx, 1)
                if j in (1, 3, 5, 7):
                    k = (j - 1) // 2
                    if j == 1:
                        wait(pe, b_xt_out, u.plus(1))
                        for n in range(4):
                            m = turn(ps[0:TS, M2, n * P:(n + 1) * P], b_io[:, p, 2 + n, TP:T])
                        m.then_inc(b_xs, 1)
                        wait(pe, b_cbx_out, u.plus(1))
                    else:
                        wait(pe, b_sadd, u.times(8).plus(2 * k))
                    wait(pe, b_selr, u.times(4).plus(k + 1))
                    mm(ps[:, M0, 0:T], b_sel[:, 0, :], b_rows[:, 0, :])
                    mm(ps[:, M1, 0:T], b_sel[:, 1, :], b_rows[:, 0, :])
                    mm(ps[0:64, M1, T:T + TS], b_sel[:, 0, 0:64], b_rsum[:, 0:TS])
                    mm(ps[64:P, M1, T:T + TS], b_sel[:, 1, 0:64], b_rsum[:, 0:TS]).then_inc(b_rowsr, 1)
                if j in (2, 4, 6, 8):
                    k = (j - 2) // 2
                    ch = slice(k * P, (k + 1) * P)
                    wait(pe, b_wts, u.times(4).plus(k + 1))
                    wait(pe, b_xs_out, u.plus(1))
                    wait(pe, b_yg, u.times(4).plus(k))
                    wait(pe, b_sT_in, u.times(4).plus(k + 1).times(16))
                    for b in range(NB):
                        mm(ps[:, M2, T + SL * b:T + SL * (b + 1)], b_sT[:, b, :], cT[:, TP + SL * b:TP + SL * (b + 1)])
                    for e in range(2):
                        rows, hc = slice(64 * e, 64 * (e + 1)), slice(k * P + 64 * e, k * P + 64 * (e + 1))
                        mm(ps[rows, M2, 0:TP], b_xdt[:, 0, hc], b_dec[:, e, 0:TP], True, False)
                        mm(ps[rows, M2, P:TP], b_xdt[:, 1, hc], b_dec[:, e, TP:TP + P], False, False)
                        m = mm(ps[rows, M2, TP:T], b_xdt[0:TS, 2, hc], b_dec[0:TS, e, TP + P:SC], False, True)
                    m.then_inc(b_yst, 1)
                    wait(pe, b_xwr, u.times(4).plus(k + 1))
                    wait(pe, b_bmask, u.plus(1))
                    wait(pe, b_spr, u.times(4).plus(k))
                    for half in range(2):
                        mm(ps[:, M0 + half, :], b_xw[0:TS, 2, :], b_bm[:, 4 * half:4 * half + 4, :])
                    mm(ps[:, M3, 0:P], b_xw[:, 0, :], b_bt[:, 0, :], True, False)
                    mm(ps[:, M3, 0:P], b_xw[:, 1, :], b_bt[:, 1, :], False, True).then_inc(b_yst, 1)
                if j == 9:
                    wait(pe, b_gsq, u.plus(1).times(4))
                    wait(pe, b_yg, u.plus(1).times(4))
                    for k in range(4):
                        m = mm(ps[:, M2, 0:T], mean_mat[:], b_io[:, p, 2 + k, :], k == 0, k == 3)
                    m.then_inc(b_gms, 1)

            with pe.Fori(0, 2) as h:
                for g in range(5):
                    for j in range(10):
                        if g < 4:
                            c = 10 * g + j
                            wait(pe, taken_act, Count(EA_BIN + c - 3, (h, 40)))
                            gemm(Count(C_BIN + c, (h, C_BHALF)), (N_BIN + c) % 4, hn_hi, hn_lo, range(KT))
                        if g > 0:
                            b_mix(Count(g - 1, (h, 4)), (g - 1) % 2, j)
                wait(pe, b_glo, Count(12, (h, 16)))
                pe.sem_inc(pe_passed, 1)
                with pe.Fori(0, KT // 4) as i:
                    for j in range(4):
                        wait(pe, taken_dve, Count(ED_BIN + j - 3, (h, KT), (i, 4)))
                        gemm(Count(C_BIN + 40 + j, (h, C_BHALF), (i, 4)), (N_BIN + 40 + j) % 4, b_out_hi, b_out_lo, range(KT),
                             each=(lambda t: t >= 12 and wait(pe, b_glo, Count(t + 1, (h, 16)))) if j == 0 else None)
            ffn(1, C_F1, N_F1, EA_F1, ED_F1, 3)
            norm(4)

        @block.scalar
        def _(act):
            own = Own(act, act_own)
            A = nc.scalar.activation

            def split(c, cols=CH):
                wait(act, raw_landed[c.base % 2], c.half().plus(1).times(16))
                wait(act, chunk_done, c.plus(-1))
                A(w_hi[:, c.base % 2, 0:cols], w_raw[:, c.base % 2, 0:cols], ACT.Copy).then_inc(w_high, 1)

            def norm(k):
                wait(act, var_ready, k + 1)
                A(rstd[:], rstd[:], ACT.Sqrt).then_inc(root_ready, 1)
                if k < 4:
                    for t in range(KT):
                        wait(act, hn_ready, KT * k + t + 1)
                        A(hn_hi[:, t, :], work[:, t % 2, :], ACT.Copy).then_inc(hn_hi_ready, 1)

            def residual(c0, tiles_done, sq0, per, last=False):
                def pair(i, tail):
                    for j in range(2):
                        for q in range(per):
                            ahead = tail and j * per + q >= 2 * per - 2
                            if not (ahead and last):
                                split(c0.plus(j * per + q + 2).add(i, 2 * per), CH if ahead or per == 1 else DCH)
                        wait(act, taken_dve, tiles_done.plus(j + 1).add(i, 2))
                        wait(act, sq_added, sq0.plus(j - 1).add(i, 2))
                        A(work[:, j, :], x[:, Count(j).add(i, 2).value, :], ACT.Square).then_inc(squared, 1)
                with act.Fori(0, KT // 2 - (per - 1)) as i:
                    pair(i, False)
                if per == 2:
                    pair(KT // 2 - 1, True)

            act.wait_ge(x_in, 16)
            for t in range(KT):
                wait(act, sq_added, t - 1)
                A(work[:, t % 2, :], x[:, t, :], ACT.Square).then_inc(squared, 1)
            act.wait_ge(consts_in, N_CONSTS)

            split(Count(0))
            split(Count(1))
            norm(0)
            act.wait_ge(chunk_done, 1)
            split(Count(2))
            A(a_rows[:, 0, :], ps[0:8, 0, 0:T], ACT.Identity, bias=a_small[:, 0:1])
            A(a_rows[:, 1, :], ps[32:40, 0, 0:T], ACT.Copy).then_inc(taken_act, 1)
            act.wait_ge(taken_act, 1)
            own.link(A(a_rows[:, 1, :], a_rows[:, 1, :], ACT.Identity, bias=a_small[:, 1:2]))
            own.link(A(a_rows[:, 2, :], a_rows[:, 1, :], ACT.Abs))
            A(a_rows[:, 3, :], a_rows[:, 2, :], ACT.Exp, scale=-1.0).then_inc(ga_exp, 1)
            act.wait_ge(ga_onep, 1)
            A(a_rows[:, 4, :], a_rows[:, 2, :], ACT.Ln).then_inc(ga_ln, 1)
            act.wait_ge(ga_logs, 1)
            A(a_rows[:, 6, :], a_rows[:, 6, :], ACT.Exp)
            A(a_rows[:, 8, TP:T], a_rows[:, 8, TP:T], ACT.Exp).then_inc(ga_rows, 1)

            def gate_columns():
                act.wait_ge(ga_turned, 1)
                cols = ps[:, M1, 0:48].rearrange("p (n b h) -> p n h b", n=2, b=3)
                A(a_acol[:, :, 0:2], cols[:, 0, :, 0:2], ACT.Copy)
                A(a_wcol[:, :, 0:2], cols[:, 1, :, 0:2], ACT.Copy)
                A(a_acol[0:TS, :, 2], cols[0:TS, 0, :, 2], ACT.Copy)
                A(a_wcol[0:TS, :, 2], cols[0:TS, 1, :, 2], ACT.Copy).then_inc(ga_done, 1)
                act.wait_ge(ga_done, 1)

            def a_post(u, p, j):
                c = u.times(6).plus(C_AIN + j)
                if j == 0 and u.base > 0:
                    wait(act, a_hlo, u.plus(-1).times(2))
                    wait(act, a_v1, u.plus(-1))
                wait(act, chunk_done, c.plus(1))
                src = ps[:, c.base % 4, 0:T]
                if j < 4:
                    A(a_io[:, p, j, :], src, ACT.Copy, scale=A_DK ** -0.5 if j == 1 else 1.0).then_inc(taken_act, 1)
                else:
                    A(a_io[:, p, j, :], src, ACT.Tanh, scale=0.5).then_inc(taken_act, 1)

            def a_mix(u, p, j):
                h = u.value
                if j == 1:
                    wait(act, a_kv0, u.plus(1))
                    wait(act, a_cupd, u.times(4))
                    wait(act, a_vmask, u)
                    for b in range(2):
                        A(a_kw[:, b, :], ps[:, M2, b * P:(b + 1) * P], ACT.Copy, scale=a_wcol[:, h, b:b + 1])
                    A(a_kw[0:TS, 2, :], ps[0:TS, M2, 2 * P:3 * P], ACT.Copy, scale=a_wcol[0:TS, h, 2:3])
                    A(a_vt[:, 0:2, 0:P], ps[:, M3, 0:2 * P].rearrange("p (b e) -> p b e", b=2), ACT.Copy)
                    A(a_vt[0:TS, 2, 0:P], ps[0:TS, M3, 2 * P:3 * P], ACT.Copy).then_inc(a_kv0_tok, 1)
                    wait(act, a_dlog, u.plus(1))
                    A(a_dec[:], a_dec[:], ACT.Exp, scale=-1.0).then_inc(a_dexp, 1)
                if j == 2:
                    wait(act, a_v1, u.plus(1))
                    wait(act, a_htmp, u.times(2))
                    A(a_vt[:, 0:2, P:2 * P], ps[:, M2, 0:2 * P].rearrange("p (b e) -> p b e", b=2), ACT.Copy)
                    A(a_vt[0:TS, 2, P:2 * P], ps[0:TS, M2, 2 * P:3 * P], ACT.Copy)
                    A(a_em[:], ps[:, M3, 0:T], ACT.Exp, scale=-1.0).then_inc(a_v1_tok, 1)
                if j == 3:
                    for e in range(2):
                        wait(act, a_htmp, u.times(2).plus(e + 1))
                        A(a_out_hi[:, u.times(2).plus(e).value, :], a_h[:, e, :], ACT.Copy).then_inc(a_hhi, 1)
                if j == 4:
                    wait(act, a_cupd, u.times(4).plus(1))
                    wait(act, a_cp_out, u.times(16))
                    A(a_nnew[:, h, 0:1], ps[:, M3, A_DV:A_DV + 1], ACT.Copy)
                    A(a_cp[:], ps[:, M3, 0:A_DV], ACT.Copy).then_inc(a_cp_ready, 1)

            def a_head(u, p, mixed):
                for j in range(6):
                    if mixed is not None:
                        a_mix(mixed, 1 - p, j)
                    split(u.times(6).plus(C_AIN + j + 2))
                    a_post(u, p, j)

            a_head(Count(0), 0, None)
            gate_columns()
            a_head(Count(1), 1, Count(0))
            with act.Fori(0, 3) as i:
                for n in range(2):
                    a_head(Count(2 + n, (i, 2)), n, Count(1 + n, (i, 2)))
            for j in range(6):
                a_mix(Count(7), 1, j)
            residual(Count(C_AOUT), Count(0), Count(KT), 1)

            def ffn(layer, c0, ea0, ed0, k):
                first = 2 * FT * layer

                def half(h, last):
                    def pair(i, par):
                        m = Count(first // 2 + par).add(h, FH).add(i, 2)
                        for j in range(2):
                            s = 2 * par + j
                            n = Count(s).add(h, 2 * FH).add(i, 4)
                            c = Count(c0 + s).add(h, C_FHALF).add(i, 4)
                            split(c.plus(2))
                            if j == 1:
                                wait(act, f_conved, m.times(2).plus(1 + 4 * (layer + 1)))
                                wait(act, f_alo, m.plus(-1))
                                gate, th = f_u[:, 2 * par, :], f_act[:, par, :]
                                A(th[:, 0:TP], gate[:, 0:TP], ACT.Tanh)
                                A(packed(th), f_samples(gate)[:, :, 0:SL], ACT.Tanh).then_inc(f_gated, 1)
                            wait(act, f_prefix, n.plus(first + 1))
                            src = ps[:, (c0 + s) % 4, 0:T]
                            A(f_pad[:, s, 2:2 + TP], src[:, 0:TP], ACT.Copy)
                            A(f_samples(f_pad[:, s, :])[:, :, 2:], packed(src), ACT.Copy).then_inc(taken_act, 1)
                            wait(act, taken_act, n.plus(ea0 + 1))
                            w = lambda tap: f_conv[:, layer, n.value, tap:tap + 1]
                            A(f_u[:, s, 0:FP - 2], f_pad[:, s, 0:FP - 2], ACT.Identity, bias=w(3),
                              scale=w(0)).then_inc(f_tap0, 1)
                        wait(act, f_prod, m.plus(1))
                        A(act_hi[:, Count(par).add(i, 2).value, :], f_act[:, par, :], ACT.Copy).then_inc(f_ahi, 1)

                    with act.Fori(0, FH // 2) as i:
                        for par in range(2):
                            pair(i, par)
                    residual(Count(c0 + 2 * FH).add(h, C_FHALF), Count(ed0).add(h, KT),
                             Count(KT * SQ_RUNS[k]).add(h, KT), 2, last)

                norm(k)
                if layer == 0:
                    with act.Fori(0, 2) as h:
                        half(h, False)
                else:
                    half(0, False)
                    half(1, True)

            ffn(0, C_F0, EA_F0, ED_F0, 1)

            norm(2)
            split(Count(C_BGATE + 2))
            wait(act, gb_raw, 1)
            A(b_rows[:, 1, :], ps[0:64, (N_BIN - 1) % 4, 0:T], ACT.Identity, bias=b_small[:, 0:1]).then_inc(taken_act, 1)
            A(b_rsum[:, TS:TS + 1], b_small[:, 1:2], ACT.Exp)
            wait(act, taken_act, EA_BGATE + 1)
            own.link(A(b_rows[:, 3, :], b_rows[:, 1, :], ACT.Abs))
            A(b_rows[:, 2, :], b_rows[:, 3, :], ACT.Exp, scale=-1.0).then_inc(gb_exp, 1)
            act.wait_ge(gb_onep, 1)
            A(b_rows[:, 4, :], b_rows[:, 3, :], ACT.Ln).then_inc(gb_ln, 1)
            act.wait_ge(gb_logs, 1)
            A(b_rows[:, 2, :], b_rows[:, 2, :], ACT.Exp, scale=-1.0)
            A(b_rsum[:, 0:TS], b_rows[:, 0, TP:T], ACT.Exp, scale=-1.0).then_inc(gb_rows, 1)

            def gate_columns_b():
                act.wait_ge(gb_turned, 1)
                for n, col in enumerate((b_nac, b_dtc, b_end)):
                    src = ps[:, M1 if n < 2 else M2, 192 * (n % 2):192 * (n % 2) + 192].rearrange(
                        "p (b g h) -> p g b h", b=3, g=B_GROUPS)
                    for b in range(3):
                        w = P if b < 2 else TS
                        m = A(col[0:w, :, b, :], src[0:w, :, b, :], ACT.Copy)
                m.then_inc(gb_done, 1)
                act.wait_ge(gb_done, 1)

            def b_take(u, g, h, p, j):
                c = Count(C_BIN + 10 * g + j).add(h, C_BHALF)
                wait(act, chunk_done, c.plus(1))
                src = ps[:, (N_BIN + 10 * g + j) % 4, 0:T]
                n = u.times(6).plus(j)
                if j < 6:
                    wait(act, b_prefix, n.plus(1))
                    A(b_pad[:, j % 2, 3:3 + TP], src[:, 0:TP], ACT.Copy)
                    A(b_samples(b_pad[:, j % 2, :])[:, :, 3:], packed(src), ACT.Copy).then_inc(taken_act, 1)
                    wait(act, taken_act, Count(EA_BIN + 10 * g + j + 1).add(h, 40))
                    wait(act, b_silu, n)
                    w = lambda tap: b_conv[:, n.value, tap:tap + 1]
                    A(b_u[:, 0:BP - 3], b_pad[:, j % 2, 0:BP - 3], ACT.Identity, bias=w(4), scale=w(0)).then_inc(b_tap0, 1)
                else:
                    k = j - 6
                    if g > 1:
                        wait(act, b_glo, u.plus(-1).times(4))
                    A(b_io[:, p, j, :], src, ACT.Copy)
                    if k == 0:
                        wait(act, b_silu, u.times(6).plus(6))
                    else:
                        wait(act, b_zready, u.times(4).plus(k))
                    A(b_th[:, 0:T], src, ACT.Tanh, scale=0.5).then_inc(taken_act, 1)

            def b_tanh_of(u, j):
                if j < 6:
                    wait(act, b_conved, u.times(6).plus(j + 3))
                    if j == 0:
                        wait(act, b_zready, u.times(4))
                    A(b_th[:, 0:BP - 3], b_u[:, 0:BP - 3], ACT.Tanh).then_inc(b_tanh, 1)

            def b_mix(u, g, p, j):
                if j == 1:
                    wait(act, b_cbx, u.plus(1))
                    wait(act, b_wts, u.times(4))
                    wait(act, b_yst, u.times(8))
                    wait(act, b_bmask, u)
                    A(b_cb[:, 0:TP + P], ps[:, M0, 0:TP + P], ACT.Copy)
                    A(b_cb[0:TS, TP + P:SC], ps[0:TS, M0, TP + P:SC], ACT.Copy)
                    A(b_bt[:, 0:2, :], ps[:, M1, 0:2 * P].rearrange("p (b e) -> p b e", b=2), ACT.Copy)
                    A(b_bt[0:TS, 2, :], ps[0:TS, M1, 2 * P:3 * P], ACT.Copy).then_inc(b_cbx_out, 1)
                if j in (2, 4, 6, 8):
                    k = (j - 2) // 2
                    wait(act, b_dlog, u.times(4).plus(k + 1))
                    A(b_dec[:], b_dec[:], ACT.Exp, scale=-1.0).then_inc(b_dexp, 1)
                if j in (3, 5, 7, 9):
                    k = (j - 3) // 2
                    n = u.times(4).plus(k)
                    wait(act, b_yst, n.times(2).plus(2))
                    wait(act, b_sp_out, n.times(16))
                    A(b_sp[:], ps[:, M3, 0:P], ACT.Copy).then_inc(b_spr, 1)
                    wait(act, b_yg, n.plus(1))
                    A(b_io[:, p, 2 + k, :], b_io[:, p, 6 + k, :], ACT.Square).then_inc(b_gsq, 1)

            def b_group_norm(u, g, p):
                wait(act, b_gvar, u.plus(1))
                A(b_r[:], b_r[:], ACT.Sqrt).then_inc(b_groot, 1)
                for k in range(4):
                    wait(act, b_gn, u.times(4).plus(k + 1))
                    A(b_out_hi[:, 4 * g + k, :], work[:, k % 2, :], ACT.Copy).then_inc(b_ghi, 1)

            gate_columns_b()
            with act.Fori(0, 2) as h:
                for g in range(5):
                    for j in range(10):
                        step = lambda: g > 0 and j < 9 and b_mix(Count(g - 1).add(h, 4), g - 1, (g - 1) % 2, j + 1)
                        even = j % 2 == 1
                        if g < 4:
                            split(Count(C_BIN + 10 * g + j + 2).add(h, C_BHALF))
                            b_take(Count(g).add(h, 4), g, h, g % 2, j)
                        if even:
                            step()
                        if g < 4:
                            b_tanh_of(Count(g).add(h, 4), j)
                        if not even:
                            step()
                    if g > 0:
                        b_group_norm(Count(g - 1).add(h, 4), g - 1, (g - 1) % 2)
                residual(Count(C_BIN + 40).add(h, C_BHALF), Count(ED_BIN).add(h, KT),
                         Count(KT * SQ_RUNS[2]).add(h, KT), 1)
            ffn(1, C_F1, EA_F1, ED_F1, 3)
            norm(4)

        @block.vector
        def _(dve):
            own = Own(dve, dve_own)
            V = nc.vector
            STT, TT, TS_ = V.scalar_tensor_tensor, V.tensor_tensor, V.tensor_scalar

            def split(c, cols=CH):
                wait(dve, w_high, c.plus(1))
                s = c.base % 2
                TT(w_lo[:, s, 0:cols], w_raw[:, s, 0:cols], w_hi[:, s, 0:cols].bitcast(F32), ALU.subtract).then_inc(w_low, 1)

            def norm(k):
                wait(dve, mean_ready, k + 1)
                TS_(rstd[:], ps[:, M0, 0:T], EPS, None, ALU.add).then_inc(var_ready, 1)
                wait(dve, root_ready, k + 1)
                own.link(V.reciprocal(rstd[:], rstd[:]))
                for t in range(KT):
                    if k < 4:
                        if t > 1:
                            wait(dve, hn_lo_ready, KT * k + t - 1)
                        STT(work[:, t % 2, :], x[:, t, :], norm_w[:, k, t:t + 1], rstd[:], ALU.mult,
                            ALU.mult).then_inc(hn_ready, 1)
                    else:
                        STT(x[:, t, :], x[:, t, :], norm_w[:, k, t:t + 1], rstd[:], ALU.mult,
                            ALU.mult).then_inc(y_ready, 1)

            def residual(c0, n0, per, last=False):
                def four(i, tail):
                    for j in range(4):
                        for q in range(per):
                            ahead = tail and j * per + q >= 4 * per - 2
                            if q == per - 1:
                                wait(dve, chunk_done, c0.plus((j + 1) * per).add(i, 4 * per))
                                t = Count(j).add(i, 4).value
                                TT(x[:, t, :], x[:, t, :], ps[:, (n0 + j) % 4, 0:T], ALU.add).then_inc(taken_dve, 1)
                            if not (ahead and last):
                                split(c0.plus(j * per + q + 2).add(i, 4 * per), CH if ahead or per == 1 else DCH)
                with dve.Fori(0, KT // 4 - (per - 1)) as i:
                    four(i, False)
                if per == 2:
                    four(KT // 4 - 1, True)

            dve.wait_ge(consts_in, N_CONSTS)
            TS_(b_conv[:], b_conv[:], 0.5, None, ALU.mult)
            gate_taps = f_conv[:].rearrange("p l (t two) k -> p l t two k", two=2)[:, :, :, 0, :]
            TS_(gate_taps, gate_taps, 0.5, None, ALU.mult)
            TS_(b_normw[:], b_normw[:], 0.5, None, ALU.mult)
            V.memset(a_dec[:], 0.0)

            split(Count(0))
            split(Count(1))
            norm(0)
            split(Count(2))
            row = lambda n: a_rows[:, n, :]
            dve.wait_ge(ga_exp, 1)
            TS_(row(2), row(3), 1.0, None, ALU.add).then_inc(ga_onep, 1)
            dve.wait_ge(ga_onep, 1)
            own.link(TS_(row(5), row(2), -1.0, None, ALU.add))
            own.link(TT(row(5), row(3), row(5), ALU.subtract))
            own.link(V.reciprocal(row(6), row(2)))
            own.link(TT(row(5), row(5), row(6), ALU.mult))
            dve.wait_ge(ga_ln, 1)
            own.link(TT(row(4), row(4), row(5), ALU.add))
            own.link(STT(row(1), row(1), 0.0, row(4), ALU.min, ALU.subtract))
            own.link(V.tensor_tensor_scan(row(3), seg_keep[0:8, :], row(1), 0.0, ALU.mult, ALU.add))
            own.link(TT(row(4), row(0), row(3), ALU.subtract))
            own.link(V.tensor_copy(row(2), row(4)))
            m0 = a_small[:, 2:2 + NB]
            own.mark(TS_(a_rows[:, 2, 0:1], a_rows[:, 4, 0:1], 0.0, None, ALU.max))
            own.link(TT(packed(row(2))[:, :, 0], packed(row(4))[:, :, 0], m0, ALU.max))
            own.link(V.tensor_tensor_scan(row(5), seg_drop[:], row(2), 0.0, ALU.add, ALU.max))
            own.link(TT(row(7), row(3), row(5), ALU.add))
            TS_(a_rows[:, 6, 0:TP], a_rows[:, 4, 0:TP], a_rows[:, 5, TP - 1:TP], None, ALU.subtract)
            m_end = packed(row(5))[:, :, SL - 1:SL].to_broadcast([8, NB, SL])
            TT(packed(row(6)), packed(row(4)), m_end, ALU.subtract)
            TT(packed(row(8)), m0.unsqueeze(2).to_broadcast([8, NB, SL]), packed(row(5)), ALU.subtract)
            V.tensor_copy(a_mnew[:, 0:1], a_rows[:, 7, TP - 1:TP])
            V.tensor_copy(a_mnew[:, 1:], packed(row(7))[:, :, SL - 1]).then_inc(ga_logs, 1)

            A_STEPS = 8

            def a_link(u, k, ins):
                ins.then_inc(a_steps, 1)
                wait(dve, a_steps, u.times(A_STEPS).plus(k))

            def a_mix(u, p, j):
                h = u.value
                q = a_io[:, p, 0, TP:T]
                if j == 1:
                    wait(dve, a_scores, u.plus(1))
                    STT(a_dec[:, 0:TP], ps[:, M1, 0:TP], a_acol[:, h, 0:1], future[:, 0:TP], ALU.subtract, ALU.max)
                    STT(a_dec[:, TP:TP + P], ps[:, M1, P:TP], a_acol[:, h, 1:2], future[:, TP:TP + P], ALU.subtract, ALU.max)
                    STT(a_dec[0:TS, TP + P:SC], ps[0:TS, M1, TP:T], a_acol[0:TS, h, 2:3], future[0:TS, TP + P:SC],
                        ALU.subtract, ALU.max).then_inc(a_dlog, 1)
                    wait(dve, a_num, u)
                    a_link(u, 1, V.tensor_copy(a_wi[:], ps[:, M1, T:T + TS]))
                    a_link(u, 2, TT(a_qs[:], q, a_wi[:], ALU.mult))
                    by_batch = lambda t: t.rearrange("p (b l) -> p b l", l=SL)
                    TT(by_batch(a_nq[:]), by_batch(a_qs[:]), a_n[:, h, :].unsqueeze(2).to_broadcast([P, NB, SL]), ALU.mult)
                    wait(dve, a_dexp, u.plus(1))
                    TT(a_prob[:, 0:TP + P], ps[:, M0, 0:TP + P], a_dec[:, 0:TP + P], ALU.mult)
                    TT(a_prob[0:TS, TP + P:SC], ps[0:TS, M0, TP + P:SC], a_dec[0:TS, TP + P:SC], ALU.mult).then_inc(a_probs, 1)
                if j == 2:
                    wait(dve, taken_act, u.times(6).plus(1 + 6))
                    a_link(u, 3, TS_(a_io[:, p, 4:6, :], a_io[:, p, 4:6, :], 0.5, 0.5, ALU.mult, ALU.add))
                if j == 3:
                    wait(dve, a_num, u.plus(1))
                    wait(dve, a_v1_tok, u.plus(1))
                    a_link(u, 4, STT(a_den[:], ps[:, M2, 0:T], -1.0, a_em[:], ALU.mult, ALU.max))
                    a_link(u, 5, TT(a_den[:], a_den[:], ps[:, M2, 0:T], ALU.max))
                    a_link(u, 6, V.reciprocal(a_den[:], a_den[:]))
                    a_link(u, 7, TT(a_io[:, p, 4:6, :], a_io[:, p, 4:6, :], a_den[:].unsqueeze(1).to_broadcast([P, 2, T]), ALU.mult))
                    for e in range(2):
                        TT(a_h[:, e, :], ps[:, M0 + e, 0:T], a_io[:, p, 4 + e, :], ALU.mult).then_inc(a_htmp, 1)
                    for e in range(2):
                        n = u.times(2).plus(e)
                        wait(dve, a_hhi, n.plus(1))
                        TT(a_out_lo[:, n.value, :], a_h[:, e, :], a_out_hi[:, n.value, :].bitcast(F32),
                           ALU.subtract).then_inc(a_hlo, 1)
                last_step = a_wi[:].rearrange("p (b l) -> p b l", l=SL)[:, :, SL - 1]

                def c_add(n):
                    wait(dve, a_cupd, u.times(4).plus(n + 1))
                    for e in range(2):
                        b = 2 * n + e
                        m = STT(a_c[:, p, b, :], a_c[:, p, b, :], a_wi[:, SL * b + SL - 1:SL * (b + 1)],
                                ps[:, M0 + n % 3, e * A_DV:(e + 1) * A_DV], ALU.mult, ALU.add)
                    m.then_inc(a_cadd, 1)
                if j == 4:
                    wait(dve, a_cupd, u.times(4).plus(1))
                    wait(dve, a_cp_ready, u.plus(1))
                    a_link(u, 8, TT(a_nnew[:, h, 1:1 + NB], a_n[:, h, :], last_step, ALU.mult))
                    TT(a_nnew[:, h, 1:1 + NB], a_nnew[:, h, 1:1 + NB], ps[:, M3, A_DV + 1:A_DV + 1 + NB], ALU.add)
                    for n in range(3):
                        c_add(n)
                if j == 5:
                    c_add(3)

            def a_head(u, p, mixed):
                for j in range(6):
                    if mixed is not None:
                        a_mix(mixed, 1 - p, j)
                    split(u.times(6).plus(C_AIN + j + 2))

            a_head(Count(0), 0, None)
            dve.wait_ge(ga_done, 1)
            dve.wait_ge(a_n_in, 16)
            a_head(Count(1), 1, Count(0))
            with dve.Fori(0, 3) as i:
                for n in range(2):
                    a_head(Count(2 + n, (i, 2)), n, Count(1 + n, (i, 2)))
            for j in range(6):
                a_mix(Count(7), 1, j)
            residual(Count(C_AOUT), N_AOUT, 1)

            def ffn(layer, c0, n0, k):
                first = 2 * FT * layer
                if layer == 0:
                    for s in a_c_out:
                        dve.wait_ge(s, 16 * A_HEADS // 2)
                    dve.wait_ge(a_cp_out, 16 * A_HEADS)
                    dve.wait_ge(a_nm_out, 32)
                else:
                    dve.wait_ge(b_s_out, 16 * 32)
                    dve.wait_ge(b_sp_out, 16 * 32)
                    dve.wait_ge(b_new_out, 16 * B_GROUPS)
                wait(dve, mean_ready, k + 1)
                for s in range(4):
                    V.memset(f_pad[:, s, 0:2], 0.0).then_inc(f_conved, 1)
                norm(k)

                def half(h, last):
                    def pair(i, par):
                        m = Count(first // 2 + par).add(h, FH).add(i, 2)
                        for j in range(2):
                            s = 2 * par + j
                            n = Count(s).add(h, 2 * FH).add(i, 4)
                            split(Count(c0 + s + 2).add(h, C_FHALF).add(i, 4))
                            g, v, prod = f_u[:, 2 * par, :], f_u[:, 2 * par + 1, :], f_act[:, par, :]
                            if j == 1:
                                wait(dve, f_gated, m.plus(1))
                                STT(prod[:, 0:TP], prod[:, 0:TP], 1.0, g[:, 0:TP], ALU.add, ALU.mult)
                                STT(packed(prod), packed(prod), 1.0, f_samples(g)[:, :, 0:SL], ALU.add,
                                    ALU.mult).then_inc(f_silu, 1)
                            wait(dve, f_tap0, n.plus(first + 1))
                            w = lambda tap: f_conv[:, layer, n.value, tap:tap + 1]
                            STT(f_u[:, s, 0:FP - 2], f_pad[:, s, 1:FP - 1], w(1), f_u[:, s, 0:FP - 2], ALU.mult,
                                ALU.add).then_inc(f_tap1, 1)
                            wait(dve, f_tap1, n.plus(first + 1))
                            STT(f_u[:, s, 0:FP - 2], f_pad[:, s, 2:FP], w(2), f_u[:, s, 0:FP - 2], ALU.mult,
                                ALU.add).then_inc(f_conved, 1)
                        wait(dve, f_silu, m.plus(1))
                        wait(dve, f_conved, m.times(2).plus(2 + 4 * (layer + 1)))
                        TT(prod[:, 0:TP], prod[:, 0:TP], v[:, 0:TP], ALU.mult)
                        TT(packed(prod), packed(prod), f_samples(v)[:, :, 0:SL], ALU.mult).then_inc(f_prod, 1)
                        wait(dve, f_ahi, m.plus(1))
                        t = Count(par).add(i, 2).value
                        TT(act_lo[:, t, :], f_act[:, par, :], act_hi[:, t, :].bitcast(F32), ALU.subtract).then_inc(f_alo, 1)

                    with dve.Fori(0, FH // 2) as i:
                        for par in range(2):
                            pair(i, par)
                    residual(Count(c0 + 2 * FH).add(h, C_FHALF), n0 + 2 * FH, 2, last)

                if layer == 0:
                    with dve.Fori(0, 2) as h:
                        half(h, False)
                else:
                    half(0, False)
                    half(1, True)

            ffn(0, C_F0, N_F0, 1)

            dve.wait_ge(f_new_out, 16)
            wait(dve, mean_ready, 3)
            for s in range(2):
                V.memset(b_pad[:, s, 0:3], 0.0).then_inc(b_conved, 1)
            V.memset(b_cb[:], 0.0)
            V.memset(b_dec[:], 0.0).then_inc(gb_raw, 1)
            norm(2)
            split(Count(C_BGATE + 2))
            brow = lambda n: b_rows[:, n, :]
            dve.wait_ge(gb_exp, 1)
            TS_(brow(3), brow(2), 1.0, None, ALU.add).then_inc(gb_onep, 1)
            dve.wait_ge(gb_onep, 1)
            own.link(TS_(brow(0), brow(3), -1.0, None, ALU.add))
            own.link(TT(brow(0), brow(2), brow(0), ALU.subtract))
            own.link(V.reciprocal(brow(2), brow(3)))
            own.link(TT(brow(0), brow(0), brow(2), ALU.mult))
            dve.wait_ge(gb_ln, 1)
            own.link(TT(brow(4), brow(4), brow(0), ALU.add))
            own.link(STT(brow(1), brow(1), 0.0, brow(4), ALU.max, ALU.add))
            own.link(TS_(brow(4), brow(1), b_rsum[:, TS:TS + 1], None, ALU.mult))
            own.link(V.tensor_tensor_scan(brow(0), seg_keep[:], brow(4), 0.0, ALU.mult, ALU.add))
            own.link(TS_(b_rows[:, 2, 0:TP], b_rows[:, 0, 0:TP], -1.0, b_rows[:, 0, TP - 1:TP], ALU.mult, ALU.add))
            end = packed(brow(0))[:, :, SL - 1:SL].to_broadcast([64, NB, SL])
            TT(packed(brow(2)), end, packed(brow(0)), ALU.subtract).then_inc(gb_logs, 1)

            def b_post(u, g, h, p, j):
                n = u.times(6).plus(j)
                if j < 6:
                    pad, out = b_pad[:, j % 2, :], b_u[:, 0:BP - 3]
                    w = lambda tap: b_conv[:, n.value, tap:tap + 1]
                    wait(dve, b_tap0, n.plus(1))
                    STT(out, pad[:, 1:BP - 2], w(1), out, ALU.mult, ALU.add).then_inc(b_taps, 1)
                    wait(dve, b_taps, n.times(2).plus(1))
                    STT(out, pad[:, 2:BP - 1], w(2), out, ALU.mult, ALU.add).then_inc(b_taps, 1)
                    wait(dve, b_taps, n.times(2).plus(2))
                    STT(out, pad[:, 3:BP], w(3), out, ALU.mult, ALU.add).then_inc(b_conved, 1)
                    wait(dve, b_tanh, n.plus(1))
                    STT(b_io[:, p, j, 0:TP], b_th[:, 0:TP], 1.0, b_u[:, 0:TP], ALU.add, ALU.mult)
                    STT(packed(b_io[:, p, j, :]), b_samples(b_th)[:, :, 0:SL], 1.0, b_samples(b_u)[:, :, 0:SL], ALU.add,
                        ALU.mult).then_inc(b_silu, 1)
                else:
                    wait(dve, taken_act, Count(EA_BIN + 10 * g + j + 1).add(h, 40))
                    STT(b_io[:, p, j, :], b_th[:, 0:T], 1.0, b_io[:, p, j, :], ALU.add, ALU.mult).then_inc(b_zready, 1)

            B_STEPS = 4 * 3 + 1

            def b_link(u, k, ins):
                ins.then_inc(b_steps, 1)
                wait(dve, b_steps, u.times(B_STEPS).plus(k))

            def heads(ap, blocks=None):
                return ap.rearrange("p (h e) -> p h e", e=64)

            def b_mix(u, g, p, j):
                uv = u.value
                if j == 1:
                    wait(dve, b_cbx, u.plus(1))
                    wait(dve, b_xwr, u.times(4))
                    wait(dve, b_yst, u.times(8))
                    TT(heads(b_xdt[:, 0, :]), heads(ps[:, M2, :]), b_dtc[:, uv, 0, :].unsqueeze(2).to_broadcast([P, 8, 64]), ALU.mult)
                    TT(heads(b_xdt[:, 1, :]), heads(ps[:, M3, :]), b_dtc[:, uv, 1, :].unsqueeze(2).to_broadcast([P, 8, 64]),
                       ALU.mult).then_inc(b_xt_out, 1)
                if j == 2:
                    wait(dve, b_xs, u.plus(1))
                    TT(heads(b_xdt[0:TS, 2, :]), heads(ps[0:TS, M2, :]),
                       b_dtc[0:TS, uv, 2, :].unsqueeze(2).to_broadcast([TS, 8, 64]), ALU.mult).then_inc(b_xs_out, 1)
                if j in (2, 4, 6, 8):
                    k = (j - 2) // 2
                    n = u.times(4).plus(k)
                    wait(dve, b_rowsr, n.plus(1))
                    wait(dve, b_yst, n.times(2))
                    wait(dve, b_decayed, n)
                    V.tensor_copy(b_ea[:], ps[:, M1, T:T + TS])
                    for e in range(2):
                        col = lambda b, w: b_nac[0:w, uv, b, 2 * k + e:2 * k + e + 1]
                        STT(b_dec[:, e, 0:TP], ps[:, M0 + e, 0:TP], col(0, P), future[:, 0:TP], ALU.subtract, ALU.max)
                        STT(b_dec[:, e, TP:TP + P], ps[:, M0 + e, P:TP], col(1, P), future[:, TP:TP + P], ALU.subtract, ALU.max)
                        m = STT(b_dec[0:TS, e, TP + P:SC], ps[0:TS, M0 + e, TP:T], col(2, TS), future[0:TS, TP + P:SC],
                                ALU.subtract, ALU.max)
                    m.then_inc(b_dlog, 1)

            def b_weights(u, j):
                if j in (2, 4, 6, 8):
                    n = u.times(4).plus((j - 2) // 2)
                    wait(dve, b_cbx_out, u.plus(1))
                    wait(dve, b_dexp, n.plus(1))
                    TT(b_dec[:], b_dec[:], b_cb[:].unsqueeze(1).to_broadcast([P, 2, SC]), ALU.mult).then_inc(b_wts, 1)

            def b_outputs(u, p, j):
                if j in (3, 5, 7, 9):
                    k = (j - 3) // 2
                    n = u.times(4).plus(k)
                    wait(dve, b_yst, n.times(2).plus(1))
                    b_link(u, 3 * k + 1, TT(b_yi[:], ps[:, M2, T:T + TS], b_ea[:], ALU.mult))
                    b_link(u, 3 * k + 2, STT(b_y[:], b_io[:, p, 2 + k, :], b_skip[:, n.value, 0:1], ps[:, M2, 0:T], ALU.mult, ALU.add))
                    b_link(u, 3 * k + 3, TT(b_y[:, TP:T], b_y[:, TP:T], b_yi[:], ALU.add))
                    wait(dve, b_zready, n.plus(1))
                    TT(b_io[:, p, 6 + k, :], b_y[:], b_io[:, p, 6 + k, :], ALU.mult).then_inc(b_yg, 1)
                    wait(dve, b_yst, n.times(2).plus(2))
                    wait(dve, b_decayed, n.plus(1))
                    for half in range(2):
                        s = b_s[:, 4 * half:4 * half + 4, :]
                        TT(s, s, ps[:, M0 + half, :].rearrange("p (b n) -> p b n", b=4), ALU.add).then_inc(b_sadd, 1)

            def b_group_norm(u, g, p):
                wait(dve, b_gms, u.plus(1))
                TS_(b_r[:], ps[:, M2, 0:T], EPS, None, ALU.add).then_inc(b_gvar, 1)
                wait(dve, b_groot, u.plus(1))
                b_link(u, 13, V.reciprocal(b_r[:], b_r[:]))
                for k in range(4):
                    n = u.times(4).plus(k)
                    if k > 1:
                        wait(dve, b_glo, n.plus(-1))
                    STT(work[:, k % 2, :], b_io[:, p, 6 + k, :], b_normw[:, n.value, 0:1], b_r[:], ALU.mult,
                        ALU.mult).then_inc(b_gn, 1)
                    wait(dve, b_ghi, n.plus(1))
                    TT(b_out_lo[:, 4 * g + k, :], work[:, k % 2, :], b_out_hi[:, 4 * g + k, :].bitcast(F32),
                       ALU.subtract).then_inc(b_glo, 1)

            dve.wait_ge(gb_done, 1)
            with dve.Fori(0, 2) as h:
                for g in range(5):
                    for j in range(10):
                        mixed, mixes, even = Count(g - 1).add(h, 4), g > 0 and j < 9, j % 2 == 1
                        if mixes and even:
                            b_mix(mixed, g - 1, (g - 1) % 2, j + 1)
                        if g < 4:
                            split(Count(C_BIN + 10 * g + j + 2).add(h, C_BHALF))
                        if mixes and even:
                            b_weights(mixed, j + 1)
                        if g < 4:
                            b_post(Count(g).add(h, 4), g, h, g % 2, j)
                        if mixes and not even:
                            b_mix(mixed, g - 1, (g - 1) % 2, j + 1)
                            b_outputs(mixed, (g - 1) % 2, j + 1)
                    if g > 0:
                        b_group_norm(Count(g - 1).add(h, 4), g - 1, (g - 1) % 2)
                residual(Count(C_BIN + 40).add(h, C_BHALF), N_BIN + 40, 1)
            ffn(1, C_F1, N_F1, 3)
            norm(4)

        @block.gpsimd
        def _(pool):
            G = nc.gpsimd
            own = Own(pool, pool_own)

            def until(sem, count):
                wait(pool, sem, count)
                if isinstance(count, Count) and count.terms:
                    pool.sem_inc(pool_passed, 1)

            def add_square(r, buf):
                until(squared, r.plus(1))
                until(sq_added, r)
                G.tensor_tensor(sumsq[:], sumsq[:], work[:, buf, :], ALU.add).then_inc(sq_added, 1)

            def residual(norms, sq0, used=None):
                until(mean_ready, norms)
                if used is not None:
                    until(*used)
                own.link(G.memset(sumsq[:], 0.0))
                if own.terms:
                    pool.sem_inc(pool_passed, 1)
                with pool.Fori(0, KT // 2) as i:
                    for j in range(2):
                        add_square(sq0.plus(j).add(i, 2), j)

            def split_norm(k):
                for t in range(KT):
                    until(hn_hi_ready, KT * k + t + 1)
                    G.tensor_tensor(hn_lo[:, t, :], work[:, t % 2, :], hn_hi[:, t, :].bitcast(F32),
                                    ALU.subtract).then_inc(hn_lo_ready, 1)

            own.link(G.memset(sumsq[:], 0.0))
            for t in range(KT):
                add_square(Count(t), t % 2)
            pool.dma_start(a_c[:, 0, :, :], d["a_c"][0]).then_inc(a_c_in[0], 16)
            pool.wait_ge(consts_in, N_CONSTS)
            split_norm(0)

            def a_mix(u, p, j):
                if j == 0:
                    until(a_v1, u)
                    G.tensor_copy(a_sel[:], ident[0:8, bass.ds(u.value, 1)].to_broadcast([8, P])).then_inc(a_sel_ready, 1)
                if j == 1 and not (u.base == A_HEADS - 1 and not u.terms):
                    nxt = u.plus(1)
                    until(a_c_out[1 - p], nxt.half().times(16))
                    pool.dma_start(a_c[:, 1 - p, :, :], d["a_c"][nxt.value]).then_inc(a_c_in[1 - p], 16)
                if j == 2:
                    until(a_v1_tok, u.plus(1))
                    until(a_cupd, u.times(4))
                    G.tensor_tensor(a_vm[:], a_vt[0:TS, 2, :].unsqueeze(1).to_broadcast([TS, NB, A_DV]),
                                    in_batch[:].unsqueeze(2).to_broadcast([TS, NB, A_DV]), ALU.mult).then_inc(a_vmask, 1)
                if j == 5:
                    until(a_cadd, u.plus(1).times(4))
                    pool.dma_start(o["C_s"][u.value], a_c[:, p, :, :]).then_inc(a_c_out[p], 16)
                    until(a_cp_ready, u.plus(1))
                    pool.dma_start(o["C_p"][u.value], a_cp[:]).then_inc(a_cp_out, 16)

            def head(u, p):
                for j in range(6):
                    a_mix(u, p, j)

            head(Count(0), 0)
            with pool.Fori(0, 3) as i:
                for n in range(2):
                    head(Count(1 + n, (i, 2)), 1 - n)
            head(Count(7), 1)
            pool.dma_start(o["n"], a_nnew[:]).then_inc(a_nm_out, 16)
            pool.dma_start(o["m"], a_mnew[:]).then_inc(a_nm_out, 16)
            residual(1, Count(KT), (a_htmp, Count(2 * A_HEADS)))

            def ffn(layer, k):
                first = 2 * FT * layer
                if layer == 0:
                    for s in a_c_out:
                        pool.wait_ge(s, 16 * A_HEADS // 2)
                    pool.wait_ge(a_cp_out, 16 * A_HEADS)
                    pool.wait_ge(a_nm_out, 32)
                else:
                    pool.wait_ge(b_s_out, 16 * 32)
                    pool.wait_ge(b_sp_out, 16 * 32)
                    pool.wait_ge(b_new_out, 16 * B_GROUPS)
                until(mean_ready, k + 1)
                pool.dma_start(f_old[:], d["f_old"][layer]).then_inc(f_old_in, 16)
                split_norm(k)
                pool.wait_ge(f_old_in, 16 * (layer + 1))

                def half(h):
                    with pool.Fori(0, FH // 2) as i:
                        for s in range(4):
                            n = Count(s).add(h, 2 * FH).add(i, 4)
                            until(f_conved, n.plus(first + 1 + 4 * layer))
                            pad = f_samples(f_pad[:, s, :])
                            G.tensor_copy(pad[:, :, 0:2], f_old[:, n.value, :].rearrange("p (b k) -> p b k", k=2)).then_inc(f_prefix, 1)
                            until(f_tap0, n.plus(first + 1))
                            G.tensor_copy(f_new[:, n.value, 0:2], f_pad[:, s, TP:TP + 2])
                            G.tensor_copy(f_new[:, n.value, 2:].rearrange("p (b k) -> p b k", k=2),
                                          pad[:, :, SL:SL + 2]).then_inc(f_kept, 1)
                    residual(k + 1, Count(KT * SQ_RUNS[k]).add(h, KT))

                if layer == 0:
                    with own.loop(2, 1) as h:
                        half(h)
                else:
                    half(0)
                    half(1)
                pool.wait_ge(f_kept, first + 2 * FT)
                pool.dma_start(o["fconv"][layer], f_new[:]).then_inc(f_new_out, 16)

            ffn(0, 1)

            pool.wait_ge(f_new_out, 16)
            until(mean_ready, 3)

            def load_state(n):
                pool.dma_start(b_sT[:], d["b_sT"][n.value]).then_inc(b_sT_in, 16)
                pool.dma_start(b_s[:], d["b_s"][n.value]).then_inc(b_s_in, 16)

            def b_fill(u, j):
                n = u.times(6).plus(j)
                if j == 0:
                    until(b_old_in, u.plus(1).times(16))
                until(b_conved, n.plus(1))
                G.tensor_copy(b_samples(b_pad[:, j % 2, :])[:, :, 0:3],
                              b_old[:, j, :].rearrange("p (b k) -> p b k", k=3)).then_inc(b_prefix, 1)

            def b_post(u, g, p, j):
                if j >= 6:
                    return
                n = u.times(6).plus(j)
                pad = b_samples(b_pad[:, j % 2, :])
                if j == 0:
                    until(b_new_out, u.times(16))
                until(b_tap0, n.plus(1))
                G.tensor_copy(b_new[:, j, 0:3], b_pad[:, j % 2, TP:TP + 3])
                G.tensor_copy(b_new[:, j, 3:].rearrange("p (b k) -> p b k", k=3), pad[:, :, SL:SL + 3]).then_inc(b_kept, 1)
                if j == 5:
                    until(b_prefix, n.plus(1))
                    if g < 3:
                        pool.dma_start(b_old[:], d["b_old"][u.plus(1).value]).then_inc(b_old_in, 16)
                    until(b_kept, n.plus(1))
                    pool.dma_start(o["bconv"][u.value], b_new[:]).then_inc(b_new_out, 16)

            def b_mix(u, g, p, j):
                uv = u.value
                def select(k):
                    n = u.times(4).plus(k)
                    until(b_rowsr, n)
                    G.tensor_copy(b_sel[:], ident[0:64, bass.ds(u.times(8).plus(2 * k).value, 2)].unsqueeze(2)
                                  .to_broadcast([64, 2, P])).then_inc(b_selr, 1)
                if j == 0:
                    select(0)
                if j == 1:
                    until(b_cbx_out, u.plus(1))
                    G.tensor_tensor(b_bm[:], b_bt[0:TS, 2, :].unsqueeze(1).to_broadcast([TS, NB, P]),
                                    in_batch[:].unsqueeze(2).to_broadcast([TS, NB, P]), ALU.mult).then_inc(b_bmask, 1)
                if j in (2, 4, 6, 8):
                    k = (j - 2) // 2
                    n = u.times(4).plus(k)
                    ch = slice(k * P, (k + 1) * P)
                    until(b_xs_out, u.plus(1))
                    until(b_yst, n.times(2))
                    for b in range(3):
                        w = P if b < 2 else TS
                        m = G.tensor_tensor(b_xw[0:w, b, :].rearrange("p (h e) -> p h e", e=64),
                                            b_xdt[0:w, b, ch].rearrange("p (h e) -> p h e", e=64),
                                            b_end[0:w, uv, b, 2 * k:2 * k + 2].unsqueeze(2).to_broadcast([w, 2, 64]), ALU.mult)
                    m.then_inc(b_xwr, 1)
                    if k < 3:
                        select(k + 1)
                    until(b_s_in, n.plus(1).times(16))
                    until(b_dlog, n.plus(1))
                    dec = b_ea[:].rearrange("p (b l) -> p b l", l=SL)[:, :, SL - 1:SL].to_broadcast([P, NB, P])
                    G.tensor_tensor(b_s[:], b_s[:], dec, ALU.mult).then_inc(b_decayed, 1)
                if j in (3, 5, 7, 9):
                    k = (j - 3) // 2
                    n = u.times(4).plus(k)
                    until(b_sadd, n.plus(1).times(2))
                    pool.dma_start(o["ssm_s"][n.value], b_s[:]).then_inc(b_s_out, 16)
                    until(b_spr, n.plus(1))
                    pool.dma_start(o["ssm_p"][n.value], b_sp[:]).then_inc(b_sp_out, 16)
                    if not (g == 3 and k == 3):
                        until(b_s_out, n.plus(1).times(16))
                        load_state(n.plus(1))

            split_norm(2)
            pool.wait_ge(gb_done, 1)
            with own.loop(2, 1) as h:
                pool.dma_start(b_old[:], d["b_old"][Count(0).add(h, 4).value]).then_inc(b_old_in, 16)
                load_state(Count(0).add(h, 16))
                b_fill(Count(0).add(h, 4), 0)
                for g in range(5):
                    if g > 0:
                        b_mix(Count(g - 1).add(h, 4), g - 1, (g - 1) % 2, 0)
                    for j in range(10):
                        if g < 4:
                            b_post(Count(g).add(h, 4), g, g % 2, j)
                            if j < 5:
                                b_fill(Count(g).add(h, 4), j + 1)
                        if g < 3 and j == 9:
                            b_fill(Count(g + 1).add(h, 4), 0)
                        if g > 0 and j < 9:
                            b_mix(Count(g - 1).add(h, 4), g - 1, (g - 1) % 2, j + 1)
                until(b_s_out, Count(256).add(h, 256))
                until(b_sp_out, Count(256).add(h, 256))
                until(b_new_out, Count(64).add(h, 64))
                residual(3, Count(KT * SQ_RUNS[2]).add(h, KT), (b_glo, Count(16).add(h, 16)))
            ffn(1, 3)
            for t in range(4):
                until(y_ready, 4 * (t + 1))
                pool.dma_start(o["y"][:, 4 * t:4 * t + 4, :], x[:, 4 * t:4 * t + 4, :]).then_inc(y_stored, 16)
            pool.wait_ge(y_stored, 64)
            pool.wait_ge(f_new_out, 32)


def kernel(**inputs):
    import concourse.bacc as bacc
    from concourse.bass_utils import run_bass_kernel_spmd

    a = {k: np.asarray(v) for k, v in inputs.items()}

    def chunks(w, kt):
        k, n = w.shape
        w = w.reshape(k // (kt * P), kt, P, n // P, P).transpose(3, 0, 2, 1, 4)
        return w.reshape(-1, P, kt * P)

    def tiles(v, *tail):
        v = v.reshape(v.shape[:-1] + (-1, P))
        v = np.moveaxis(v, (-1, -2), (0, 1))
        return v.reshape(v.shape[:2] + tail) if tail else v

    w = a["a_w_in"][0]
    hk = A_HEADS * A_DK
    q, k, v, og, gates = np.split(w, [hk, 2 * hk, 2 * hk + D_MODEL, 2 * hk + 2 * D_MODEL], axis=1)
    by_head = [z.reshape(D_MODEL, A_HEADS, -1) for z in (q, k, v, og)]
    wa_in = np.concatenate(by_head, axis=2).reshape(D_MODEL, -1)
    wa_gate = np.zeros((D_MODEL, P), np.float32)
    wa_gate[:, 0:8], wa_gate[:, 32:40] = gates[:, :8], gates[:, 8:]
    w = a["b_w_in"][0]
    z, xs, bm, cm, dt = np.split(w, [B_DINNER, 2 * B_DINNER, 2 * B_DINNER + 1024, 2 * B_DINNER + 2048], axis=1)

    def by_group(*parts):
        return np.concatenate([v.reshape(v.shape[:-1] + (B_GROUPS, -1)) for v in parts], axis=-1).reshape(parts[0].shape[:-1] + (-1,))

    def conv_by_group(v):
        xp, bp, cp = np.split(v, [B_DINNER, B_DINNER + 1024], axis=-1)
        return by_group(bp, cp, xp)

    wb_in = by_group(bm, cm, xs, z)
    wb_gate = np.zeros((D_MODEL, P), np.float32)
    wb_gate[:, 0:64] = dt

    def gate_value(v):
        s = v.shape[:-1]
        return np.swapaxes(v.reshape(s + (2, FT, P)), -3, -2).reshape(s + (-1,))

    f_tapb = np.concatenate([a["f_conv_w"], a["f_conv_b"][:, None]], axis=1)
    b_tapb = np.concatenate([a["b_conv_w"][0], a["b_conv_b"]], axis=0)
    x = np.concatenate([a["x_prompt"][0], a["x_sample"].reshape(TS, D_MODEL)], axis=0)
    s_idx, t_idx = np.arange(P)[:, None], np.arange(P)[None, :]
    future = np.zeros((P, SC), np.float32)
    future[:, 0:P] = future[:, TP:TP + P] = np.where(s_idx <= t_idx, 0.0, BIG)
    ss, tt = np.arange(TS)[:, None], np.arange(TS)[None, :]
    future[0:TS, TP + P:SC] = np.where((ss <= tt) & (ss // SL == tt // SL), 0.0, BIG)
    starts = [0] + [TP + SL * b for b in range(NB)]
    seg_keep = np.ones((64, T), np.float32)
    seg_keep[:, starts] = 0.0
    seg_drop = np.zeros((8, T), np.float32)
    seg_drop[:, starts] = -BIG
    ssm = a["state_ssm"][0].reshape(NB, 32, P, P)
    ins = {
        "x": tiles(x).astype(np.float32, copy=False),
        "ident": np.eye(P, dtype=np.float32),
        "mean_mat": np.full((P, P), 1.0 / D_MODEL, np.float32),
        "ones": np.ones((P, P), np.float32),
        "future": future, "seg_keep": seg_keep, "seg_drop": seg_drop,
        "in_batch": (ss // SL == np.arange(NB)[None, :]).astype(np.float32),
        "norm_w": np.moveaxis(tiles(np.concatenate([a["norm_mix"][0:1], a["norm_ffn"][0:1], a["norm_mix"][1:2],
                                                    a["norm_ffn"][1:2], a["norm_final"][None]])), 1, 2),
        "f_conv": np.moveaxis(tiles(gate_value(f_tapb)), 1, 2),
        "b_conv": tiles(conv_by_group(b_tapb)),
        "b_normw": tiles(a["b_norm_w"][0])[:, :, None],
        "b_skip": np.repeat(a["b_D"][0], 64).reshape(32, P).T[:, :, None],
        "b_small": np.stack([a["b_dt_bias"][0], a["b_A_log"][0]], axis=1),
        "a_small": np.concatenate([a["a_b_if"][0].reshape(2, 8).T, a["state_mlstm_m"][0].T], axis=1),
        "a_n": a["state_mlstm_n"][0].transpose(2, 1, 0),
        "a_c": a["state_mlstm_C"][0].transpose(1, 2, 0, 3),
        "f_old": np.stack([tiles(gate_value(s), NB * 2) for s in a["state_ffn_conv"]]),
        "b_old": np.moveaxis(tiles(conv_by_group(a["state_ssm_conv"][0]), NB * 3).reshape(P, B_GROUPS, 6, NB * 3), 1, 0),
        "b_sT": ssm.transpose(1, 3, 0, 2),
        "b_s": ssm.transpose(1, 2, 0, 3),
        "wa_gate": chunks(wa_gate, KT), "wa_in": chunks(wa_in, KT), "wa_out": chunks(a["a_w_out"][0], KT),
        "wb_gate": chunks(wb_gate, KT), "wb_in": chunks(wb_in, KT),
        "wb_out": np.concatenate([chunks(a["b_w_out"][0][h * 2048:(h + 1) * 2048], KT) for h in range(2)]),
    }
    for l in range(2):
        ins[f"wf_up{l}"] = chunks(gate_value(a["f_w_up"][l]), KT)
        ins[f"wf_down{l}"] = np.concatenate([chunks(a["f_w_down"][l][h * FH * P:(h + 1) * FH * P], FH // 2) for h in range(2)])
    ins = {n: np.ascontiguousarray(v) for n, v in ins.items()}
    outs = {"y": (P, KT, T), "C_s": (A_HEADS, P, NB, A_DV), "C_p": (A_HEADS, P, A_DV), "n": (P, A_HEADS, 1 + NB),
            "m": (A_HEADS, 1 + NB), "ssm_s": (32, P, NB, P), "ssm_p": (32, P, P),
            "bconv": (B_GROUPS, P, 6, (1 + NB) * 3), "fconv": (2, P, 2 * FT, (1 + NB) * 2)}
    nc = bacc.Bacc("TRN2", target_bir_lowering=False, num_devices=1, dynamic_dma_scratch_size=8192)
    d = {n: nc.dram_tensor(n + "_in", v.shape, F32, kind="ExternalInput").ap() for n, v in ins.items()}
    o = {n: nc.dram_tensor(n + "_out", s, F32, kind="ExternalOutput").ap() for n, s in outs.items()}
    trunk(nc, d, o)
    r = run_bass_kernel_spmd(nc, [{n + "_in": v for n, v in ins.items()}], core_ids=[0]).results[0]
    r = {n: np.asarray(r[n + "_out"]) for n in outs}

    y = r["y"].transpose(2, 1, 0).reshape(T, D_MODEL)
    C_s = r["C_s"].transpose(2, 0, 1, 3)[None]
    n_all = r["n"].transpose(2, 1, 0)
    m_all = r["m"].T
    ssm_s = r["ssm_s"].transpose(2, 0, 1, 3).reshape(NB, B_HEADS, 64, P)[None]
    ssm_p = r["ssm_p"].reshape(1, 1, B_HEADS, 64, P)
    bc = r["bconv"].reshape(B_GROUPS, P, 6, 1 + NB, 3).transpose(3, 4, 0, 2, 1)
    bc = np.concatenate([bc[:, :, :, 2:6].reshape(1 + NB, 3, -1), bc[:, :, :, 0].reshape(1 + NB, 3, -1),
                         bc[:, :, :, 1].reshape(1 + NB, 3, -1)], axis=-1)
    fc = r["fconv"].reshape(2, P, FT, 2, 1 + NB, 2).transpose(0, 4, 5, 3, 2, 1).reshape(2, 1 + NB, 2, 2 * D_FF)
    out = (y[None, :TP], y[TP:].reshape(NB, SL, D_MODEL), r["C_p"][None, None], C_s,
           n_all[None, 0:1], n_all[None, 1:], m_all[None, 0:1], m_all[None, 1:], ssm_p, ssm_s,
           bc[None, 0:1], bc[None, 1:], fc[:, 0:1], fc[:, 1:])
    return tuple(np.ascontiguousarray(v) for v in out)
```

```python
from contextlib import ExitStack, contextmanager

import numpy as np

import concourse.bass as bass
from concourse import mybir

F32 = mybir.dt.float32
F32R = mybir.dt.float32r
ACT = mybir.ActivationFunctionType
ALU = mybir.AluOpType

P = 128
D_MODEL = 2048
KT = D_MODEL // P
TP, NB, SL = 256, 8, 4
TS = NB * SL
T = TP + TS
A_HEADS, A_DK, A_DV = 8, 128, 256
B_HEADS, B_GROUPS = 64, 8
B_DINNER = 4096
D_FF = 5632
FT = D_FF // P
FH = FT // 2
EPS = 1e-6
BIG = 1e30
CH = 16 * P
DCH = FH // 2 * P
SC = TP + P + TS

C_AIN = 1
C_AOUT = C_AIN + 6 * A_HEADS
C_F0 = C_AOUT + KT
C_FHALF = 2 * FH + 2 * KT
C_BGATE = C_F0 + 2 * C_FHALF
C_BIN = C_BGATE + 1
C_BOUT = KT // 2
C_BTURN = 20 + C_BOUT
C_F1 = C_BIN + 80 + 4 * C_BOUT
C_END = C_F1 + 2 * C_FHALF
N_AOUT = C_AOUT
N_F0 = C_F0
N_FHALF = 2 * FH + KT
N_BIN = N_F0 + 2 * N_FHALF + 1
N_F1 = N_BIN + 80 + 4 * KT
EA_F0 = 1 + 48
EA_BGATE = EA_F0 + 4 * FH
EA_BIN = EA_BGATE + 1
EA_F1 = EA_BIN + 80
ED_F0 = KT
ED_BIN = ED_F0 + 2 * KT
ED_F1 = ED_BIN + 4 * KT




def b_place(u, p):
    if not u.terms and u.base in (0, B_GROUPS - 1):
        return 0 if u.base == 0 else 12
    return 4 if p == 1 else 8


class Count:

    def __init__(self, base, *terms):
        self.base, self.terms = base, terms

    def plus(self, n):
        return Count(self.base + n, *self.terms)

    def times(self, n):
        return Count(self.base * n, *[(r, s * n) for r, s in self.terms])

    def add(self, reg, step):
        if isinstance(reg, int):
            return Count(self.base + reg * step, *self.terms)
        return Count(self.base, *self.terms, (reg, step))

    def half(self):
        return Count(self.base // 2, *[(r, s // 2) for r, s in self.terms])

    @property
    def value(self):
        v = self.base
        for r, s in self.terms:
            v = r * s + v
        return v


def wait(eng, sem, count):
    if isinstance(count, int):
        count = Count(count)
    if count.base <= 0:
        return
    eng.wait_ge(sem, count.value)


class Own:

    def __init__(self, eng, sem):
        self.eng, self.sem, self.n, self.terms = eng, sem, 0, []

    def mark(self, ins):
        ins.then_inc(self.sem, 1)
        self.n += 1

    def sync(self):
        wait(self.eng, self.sem, Count(self.n, *self.terms))

    def link(self, ins):
        self.mark(ins)
        self.sync()

    @contextmanager
    def loop(self, times, per):
        start = self.n
        with self.eng.Fori(0, times) as i:
            self.terms.append((i, per))
            yield i
            self.terms.pop()
        assert self.n - start == per, f"a turn of this loop counts {self.n - start}, not {per}"
        self.n = start + times * per


def trunk(nc, d, o):
    with ExitStack() as ctx:
        def sb(name, shape, dt=F32, stack=ctx):
            return stack.enter_context(nc.sbuf_tensor(name, shape, dt))

        def sem(name):
            return ctx.enter_context(nc.semaphore(name))

        x = sb("x", [P, KT, T])
        hn_hi = sb("hn_hi", [P, KT, T], F32R)
        hn_lo = sb("hn_lo", [P, KT, T], F32R)
        w_raw = sb("w_raw", [P, 2, CH])
        w_hi = sb("w_hi", [P, 2, CH], F32R)
        w_lo = sb("w_lo", [P, 2, CH], F32R)
        ident = sb("ident", [P, P])
        mean_mat = sb("mean_mat", [P, P])
        ones = sb("ones", [P, P])
        future = sb("future", [P, SC])
        seg_keep = sb("seg_keep", [64, T])
        seg_drop = sb("seg_drop", [8, T])
        in_batch = sb("in_batch", [TS, NB])
        norm_w = sb("norm_w", [P, 5, KT])
        f_conv = sb("f_conv", [P, 2, 2 * FT, 4])
        b_conv = sb("b_conv", [P, 48, 5])
        b_normw = sb("b_normw", [P, 32, 1])
        b_skip = sb("b_skip", [P, 32, 1])
        b_small = sb("b_small", [64, 2])
        a_small = sb("a_small", [8, 2 + NB])
        rstd = sb("rstd", [P, T])
        sumsq = sb("sumsq", [P, T])
        work = sb("work", [P, 2, T])

        with ExitStack() as st:
            a_out_hi = sb("a_out_hi", [P, KT, T], F32R, st)
            a_out_lo = sb("a_out_lo", [P, KT, T], F32R, st)
            a_io = sb("a_io", [P, 2, 6, T], F32, st)
            a_c = sb("a_c", [P, 2, NB, A_DV], F32, st)
            a_cp = sb("a_cp", [P, A_DV], F32, st)
            a_n = sb("a_n", [P, A_HEADS, NB], F32, st)
            a_nnew = sb("a_nnew", [P, A_HEADS, 1 + NB], F32, st)
            a_mnew = sb("a_mnew", [8, 1 + NB], F32, st)
            a_rows = sb("a_rows", [8, 9, T], F32, st)
            a_acol = sb("a_acol", [P, 8, 3], F32, st)
            a_wcol = sb("a_wcol", [P, 8, 3], F32, st)
            a_sel = sb("a_sel", [8, P], F32, st)
            a_dec = sb("a_dec", [P, SC], F32, st)
            a_prob = sb("a_prob", [P, SC], F32, st)
            a_kw = sb("a_kw", [P, 3, P], F32, st)
            a_vt = sb("a_vt", [P, 3, A_DV], F32, st)
            a_vm = sb("a_vm", [TS, NB, A_DV], F32, st)
            a_wi = sb("a_wi", [P, TS], F32, st)
            a_qs = sb("a_qs", [P, TS], F32, st)
            a_nq = sb("a_nq", [P, TS], F32, st)
        FP = 2 + TP + NB * (2 + SL)
        with ExitStack() as st:
            act_hi = sb("act_hi", [P, FH, T], F32R, st)
            act_lo = sb("act_lo", [P, FH, T], F32R, st)
            f_old = sb("f_old", [P, 2 * FT, NB * 2], F32, st)
            f_new = sb("f_new", [P, 2 * FT, (1 + NB) * 2], F32, st)
            f_pad = sb("f_pad", [P, 4, FP], F32, st)
            f_u = sb("f_u", [P, 4, FP], F32, st)
            f_act = sb("f_act", [P, 2, T], F32, st)
        BP = 3 + TP + NB * (3 + SL)
        with ExitStack() as st:
            b_out_hi = sb("b_out_hi", [P, KT, T], F32R, st)
            b_out_lo = sb("b_out_lo", [P, KT, T], F32R, st)
            b_io = sb("b_io", [P, 2, 10, T], F32, st)
            b_sT = sb("b_sT", [P, NB, P], F32, st)
            b_s = sb("b_s", [P, NB, P], F32, st)
            b_sp = sb("b_sp", [P, P], F32, st)
            b_old = sb("b_old", [P, 6, NB * 3], F32, st)
            b_new = sb("b_new", [P, 6, (1 + NB) * 3], F32, st)
            b_pad = sb("b_pad", [P, 2, BP], F32, st)
            b_u = sb("b_u", [P, BP], F32, st)
            b_yi = sb("b_yi", [P, TS], F32, st)
            b_rows = sb("b_rows", [64, 5, T], F32, st)
            b_rsum = sb("b_rsum", [64, TS + 1], F32, st)
            b_nac = sb("b_nac", [P, B_GROUPS, 3, 8], F32, st)
            b_dtc = sb("b_dtc", [P, B_GROUPS, 3, 8], F32, st)
            b_end = sb("b_end", [P, B_GROUPS, 3, 8], F32, st)
            b_sel = sb("b_sel", [64, 2, P], F32, st)
            b_cb = sb("b_cb", [P, SC], F32, st)
            b_dec = sb("b_dec", [P, 2, SC], F32, st)
            b_bt = sb("b_bt", [P, 3, P], F32, st)
            b_bm = sb("b_bm", [TS, NB, P], F32, st)
            b_xdt = sb("b_xdt", [P, 3, 4 * P], F32, st)
            b_xw = sb("b_xw", [P, 3, P], F32, st)
            b_ea = sb("b_ea", [P, TS], F32, st)

        a_h, a_em, b_r = work, sumsq, sumsq
        b_th = work[:, :, :].rearrange("p a t -> p (a t)")[:, 0:BP]

        ps = ctx.enter_context(nc.psum_tensor("ps", [P, 8, 512], F32))
        M0, M1, M2, M3 = 4, 5, 6, 7

        raw_landed = [sem("raw_landed0"), sem("raw_landed1")]
        w_high, w_low, chunk_done, proj_taken, res_added = map(sem, ("w_high", "w_low", "chunk_done", "proj_taken", "res_added"))
        consts_in, norm_w_in, y_ready, y_stored = map(sem, ("consts_in", "norm_w_in", "y_ready", "y_stored"))
        x_in = [sem(f"x_in{n}") for n in range(4)]
        act_own, dve_own, pool_own, pool_passed, pe_passed = map(sem, ("act_own", "dve_own", "pool_own", "pool_passed", "pe_passed"))
        squared, sq_added, mean_ready, var_ready, root_ready = map(sem, (
            "squared", "sq_added", "mean_ready", "var_ready", "root_ready"))
        hn_hi_ready, hn_lo_ready, rstd_ready = map(sem, ("hn_hi_ready", "hn_lo_ready", "rstd_ready"))
        a_n_in, ga_exp, ga_onep, ga_ln, ga_logs, ga_rows, ga_turned, ga_done = map(sem, (
            "a_n_in", "ga_exp", "ga_onep", "ga_ln", "ga_logs", "ga_rows", "ga_turned", "ga_done"))
        a_sel_ready, a_scores, a_kv0, a_dlog, a_dexp, a_kv0_tok, a_probs, a_v1, a_v1_tok, a_vmask = map(sem, (
            "a_sel_ready", "a_scores", "a_kv0", "a_dlog", "a_dexp", "a_kv0_tok", "a_probs", "a_v1", "a_v1_tok", "a_vmask"))
        a_num, a_htmp, a_hhi, a_hlo, a_cupd, a_cadd, a_cp_ready = map(sem, (
            "a_num", "a_htmp", "a_hhi", "a_hlo", "a_cupd", "a_cadd", "a_cp_ready"))
        a_c_in, a_c_out = [sem("a_c_in0"), sem("a_c_in1")], [sem("a_c_out0"), sem("a_c_out1")]
        a_cp_out, a_nm_out, a_steps, a_otanh = map(sem, ("a_cp_out", "a_nm_out", "a_steps", "a_otanh"))
        f_old_in, f_prefix, f_tap0, f_tap1, f_conved, f_gated, f_silu, f_prod, f_ahi, f_alo, f_kept, f_new_out = map(sem, (
            "f_old_in", "f_prefix", "f_tap0", "f_tap1", "f_conved", "f_gated", "f_silu", "f_prod", "f_ahi", "f_alo", "f_kept", "f_new_out"))
        gb_exp, gb_onep, gb_ln, gb_logs, gb_rows, gb_turned, gb_done = map(sem, (
            "gb_exp", "gb_onep", "gb_ln", "gb_logs", "gb_rows", "gb_turned", "gb_done"))
        b_old_in, b_prefix, b_tap0, b_taps, b_conved, b_tanh, b_silu, b_kept, b_new_out, b_ztanh, b_zready = map(sem, (
            "b_old_in", "b_prefix", "b_tap0", "b_taps", "b_conved", "b_tanh", "b_silu", "b_kept", "b_new_out", "b_ztanh", "b_zready"))
        b_cbx, b_cbx_out, b_xt_out, b_xs, b_xs_out, b_bmask, b_selr, b_rowsr, b_dlog, b_dexp, b_wts, b_xwr = map(sem, (
            "b_cbx", "b_cbx_out", "b_xt_out", "b_xs", "b_xs_out", "b_bmask", "b_selr", "b_rowsr", "b_dlog", "b_dexp",
            "b_wts", "b_xwr"))
        b_yst, b_decayed, b_sadd, b_spr, b_yg, b_gsq, b_gms, b_gvar, b_groot, b_gn, b_ghi, b_glo = map(sem, (
            "b_yst", "b_decayed", "b_sadd", "b_spr", "b_yg", "b_gsq", "b_gms", "b_gvar", "b_groot", "b_gn", "b_ghi", "b_glo"))
        b_s_in, b_sT_in, b_s_out, b_sp_out, b_steps = map(sem, ("b_s_in", "b_sT_in", "b_s_out", "b_sp_out", "b_steps"))

        def packed(ap, lo=TP):
            return ap[:, TP:T].rearrange("p (b l) -> p b l", l=SL)

        def f_samples(ap, n=FP):
            return ap[:, TP + 2:FP].rearrange("p (b l) -> p b l", l=SL + 2)

        def b_samples(ap):
            return ap[:, TP + 3:BP].rearrange("p (b l) -> p b l", l=SL + 3)

        CONSTS = [(ident, "ident"), (mean_mat, "mean_mat"), (ones, "ones"), (future, "future"), (seg_keep, "seg_keep"),
                  (seg_drop, "seg_drop"), (in_batch, "in_batch"), (f_conv, "f_conv"),
                  (b_conv, "b_conv"), (b_normw, "b_normw"), (b_skip, "b_skip"), (b_small, "b_small"),
                  (a_small, "a_small")]
        N_CONSTS = 16 * len(CONSTS)

        block = ctx.enter_context(nc.Block())

        @block.sync
        def _(sp):
            def load(c, src, cols):
                wait(sp, w_low, c.plus(-1))
                sp.dma_start(w_raw[:, c.base % 2, 0:cols], src).then_inc(raw_landed[c.base % 2], 16)

            sp.dma_start(norm_w[:], d["norm_w"]).then_inc(norm_w_in, 16)
            load(Count(0), d["wa_gate"][0], CH)
            for n in range(4):
                sp.dma_start(x[:, 4 * n:4 * n + 4, :], d["x"][:, 4 * n:4 * n + 4, :]).then_inc(x_in[n], 16)
            load(Count(1), d["wa_in"][0], CH)
            for tile, name in CONSTS:
                sp.dma_start(tile[:], d[name]).then_inc(consts_in, 16)
            sp.dma_start(a_n[:], d["a_n"]).then_inc(a_n_in, 16)
            load(Count(2), d["wa_in"][1], CH)
            with sp.Fori(0, 23) as i:
                for j in range(2):
                    load(Count(C_AIN + 2 + j, (i, 2)), d["wa_in"][i * 2 + (2 + j)], CH)
            with sp.Fori(0, 8) as i:
                for j in range(2):
                    load(Count(C_AOUT + j, (i, 2)), d["wa_out"][i * 2 + j], CH)

            def ffn(c0, up, down):
                with sp.Fori(0, 2) as h:
                    with sp.Fori(0, FH) as i:
                        for j in range(2):
                            load(Count(c0 + j, (h, C_FHALF), (i, 2)), up[h * (2 * FH) + i * 2 + j], CH)
                    with sp.Fori(0, KT) as i:
                        for j in range(2):
                            load(Count(c0 + 2 * FH + j, (h, C_FHALF), (i, 2)), down[h * (2 * KT) + i * 2 + j], DCH)

            ffn(C_F0, d["wf_up0"], d["wf_down0"])
            load(Count(C_BGATE), d["wb_gate"][0], CH)

            def b_in(u, c):
                with sp.Fori(0, 5) as i:
                    for j in range(2):
                        load(c.plus(j).add(i, 2), d["wb_in"][u.times(10).plus(j).add(i, 2).value], CH)

            def b_out(part, c):
                with sp.Fori(0, C_BOUT // 2) as i:
                    for j in range(2):
                        load(c.plus(j).add(i, 2), d["wb_out"][part.times(C_BOUT).plus(j).add(i, 2).value], CH)

            b_in(Count(0), Count(C_BIN))
            b_in(Count(1), Count(C_BIN + 10))
            with sp.Fori(0, 2) as i:
                for n in range(2):
                    b_in(Count(2 + n, (i, 2)), Count(C_BIN + 20 + 10 * n, (i, C_BTURN)))
                b_out(Count(0, (i, 1)), Count(C_BIN + 40, (i, C_BTURN)))
            b_in(Count(6), Count(C_BIN + 76))
            b_in(Count(7), Count(C_BIN + 86))
            b_out(Count(2), Count(C_BIN + 96))
            b_out(Count(3), Count(C_BIN + 104))
            ffn(C_F1, d["wf_up1"], d["wf_down1"])

        @block.tensor
        def _(pe):
            def gemm(c, bank, hi, lo, tiles, first=True, last=True, each=None, at=0, done=True):
                wait(pe, w_low, c.plus(1))
                s, out = c.base % 2, ps[:, bank, 0:T]
                for k, t in enumerate(tiles):
                    if each is not None:
                        each(k)
                    col = slice((at + k) * P, (at + k + 1) * P)
                    end = last and k == len(tiles) - 1
                    nc.tensor.matmul(out, w_hi[:, s, col], hi[:, t, :], start=first and k == 0, stop=False)
                    nc.tensor.matmul(out, w_hi[:, s, col], lo[:, t, :], start=False, stop=False)
                    m = nc.tensor.matmul(out, w_lo[:, s, col], hi[:, t, :], start=False, stop=end)
                if done:
                    m.then_inc(chunk_done, 1)

            def mm(out, lhs, rhs, start=True, stop=True):
                return nc.tensor.matmul(out, lhs, rhs, start=start, stop=stop, skip_group_check=True)

            def project(c, taken, bank):
                wait(pe, proj_taken, taken)
                gemm(c, bank, hn_hi, hn_lo, range(KT))

            def norm(k):
                wait(pe, sq_added, KT * (k + 1))
                mm(ps[:, M0, 0:T], mean_mat[:], sumsq[:]).then_inc(mean_ready, 1)

            def first_project(c, bank, k):
                gemm(c, bank, hn_hi, hn_lo, range(KT), each=lambda t: wait(pe, hn_lo_ready, k * KT + t + 1))

            def score_blocks(bank, keys, queries):
                mm(ps[:, bank, 0:TP], keys[:, 0:P], queries[:, 0:TP])
                mm(ps[:, bank, TP:TP + P], keys[:, P:TP], queries[:, P:TP])
                return mm(ps[0:TS, bank, TP + P:SC], keys[:, TP:T], queries[:, TP:T])

            def turn(out, src):
                return nc.tensor.transpose(out, src, ident[:])

            def turn_blocks(bank, src):
                turn(ps[:, bank, 0:P], src[:, 0:P])
                turn(ps[:, bank, P:2 * P], src[:, P:TP])
                return turn(ps[0:TS, bank, 2 * P:3 * P], src[:, TP:T])

            first_project(Count(0), 0, 0)
            def a_mix(u, p, j):
                q, k, v0, v1 = (a_io[:, p, n, :] for n in range(4))
                if j == 0:
                    wait(pe, a_sel_ready, u.plus(1))
                    wait(pe, proj_taken, u.times(6).plus(1 + 4))
                    wait(pe, a_cadd, u.times(4))
                    wait(pe, a_cp_ready, u)
                    score_blocks(M0, k, q)
                    mm(ps[:, M1, 0:T], a_sel[:], a_rows[:, 5, :])
                    mm(ps[:, M1, T:T + TS], a_sel[:], a_rows[:, 8, TP:T]).then_inc(a_scores, 1)
                    turn_blocks(M2, k)
                    turn_blocks(M3, v0).then_inc(a_kv0, 1)
                if j == 1:
                    wait(pe, a_kv0_tok, u.plus(1))
                    turn_blocks(M2, v1)
                    mm(ps[:, M3, 0:T], a_sel[:], a_rows[:, 7, :]).then_inc(a_v1, 1)
                if j == 2:
                    wait(pe, a_probs, u.plus(1))
                    wait(pe, a_v1_tok, u.plus(1))
                    wait(pe, a_c_in[p], u.half().plus(1).times(16))
                    for e in range(2):
                        ec = slice(e * P, (e + 1) * P)
                        mm(ps[:, M0 + e, 0:TP], a_vt[:, 0, ec], a_prob[:, 0:TP], True, False)
                        mm(ps[:, M0 + e, P:TP], a_vt[:, 1, ec], a_prob[:, TP:TP + P], False, False)
                        mm(ps[:, M0 + e, TP:T], a_vt[0:TS, 2, ec], a_prob[0:TS, TP + P:SC], False, False)
                        for b in range(NB):
                            t = slice(TP + SL * b, TP + SL * (b + 1))
                            mm(ps[:, M0 + e, t], a_c[:, p, b, ec], a_qs[:, SL * b:SL * (b + 1)], False, True)
                    mm(ps[:, M2, 0:TP], ones[:], a_prob[:, 0:TP], True, False)
                    mm(ps[:, M2, P:TP], ones[:], a_prob[:, TP:TP + P], False, False)
                    mm(ps[:, M2, TP:T], ones[0:TS, :], a_prob[0:TS, TP + P:SC], False, False)
                    mm(ps[:, M2, TP:T], ones[:], a_nq[:], False, True).then_inc(a_num, 1)
                if j == 3:
                    wait(pe, a_htmp, u.plus(1).times(2))
                    wait(pe, a_vmask, u.plus(1))
                    mm(ps[:, M3, 0:A_DV], a_kw[:, 0, :], a_vt[:, 0, :], True, False)
                    mm(ps[:, M3, 0:A_DV], a_kw[:, 1, :], a_vt[:, 1, :], False, True)
                    mm(ps[:, M3, A_DV:A_DV + 1], a_kw[:, 0, :], ones[:, 0:1], True, False)
                    mm(ps[:, M3, A_DV:A_DV + 1], a_kw[:, 1, :], ones[:, 0:1], False, True)
                    mm(ps[:, M3, A_DV + 1:A_DV + 1 + NB], a_kw[0:TS, 2, :], in_batch[:])
                    for n in range(3):
                        mm(ps[:, M0 + n, :], a_kw[0:TS, 2, :], a_vm[:, 2 * n:2 * n + 2, :]).then_inc(a_cupd, 1)
                if j == 4:
                    wait(pe, a_cadd, u.times(4).plus(1))
                    mm(ps[:, M0, :], a_kw[0:TS, 2, :], a_vm[:, 6:8, :]).then_inc(a_cupd, 1)

            def a_head(u, p, mixed):
                c = u.times(6)
                for j in range(6):
                    cj = c.plus(C_AIN + j)
                    project(cj, c.plus(1 + j - 3), cj.base % 4)
                    if mixed is None and j == 0:
                        pe.wait_ge(consts_in, N_CONSTS)
                        norm(0)
                    if mixed is not None:
                        a_mix(mixed, 1 - p, j)

            a_head(Count(0), 0, None)
            pe.wait_ge(ga_rows, 1)
            for n, row in enumerate((4, 6)):
                for b in range(3):
                    w = P if b < 2 else TS
                    m = nc.tensor.transpose(ps[0:w, M1, 24 * n + 8 * b:24 * n + 8 * b + 8],
                                            a_rows[:, row, b * P:b * P + w], ident[0:8, 0:8])
            m.then_inc(ga_turned, 1)
            pe.wait_ge(ga_done, 1)
            a_head(Count(1), 1, Count(0))
            with pe.Fori(0, 3) as i:
                for n in range(2):
                    a_head(Count(2 + n, (i, 2)), n, Count(1 + n, (i, 2)))
            for j in range(6):
                a_mix(Count(7), 1, j)

            def project_out(c, n0, hi, lo, ready, ready_at):
                wait(pe, ready, ready_at)
                with pe.Fori(0, KT // 4) as i:
                    for j in range(4):
                        wait(pe, squared, Count(KT + j - 3, (i, 4)))
                        gemm(Count(c + j, (i, 4)), (n0 + j) % 4, hi, lo, range(KT))

            project_out(C_AOUT, N_AOUT, a_out_hi, a_out_lo, a_hlo, Count(2 * A_HEADS))

            def ffn(layer, c0, n0, ea0, ed0, k):
                norm(k)
                with pe.Fori(0, 2) as h:
                    with pe.Fori(0, FH // 2) as i:
                        for j in range(4):
                            wait(pe, proj_taken, Count(ea0 + j - 3, (h, 2 * FH), (i, 4)))
                            if j == 0:
                                gemm(Count(c0 + j, (h, C_FHALF), (i, 4)), (n0 + j) % 4, hn_hi, hn_lo, range(KT),
                                     each=lambda t: wait(pe, hn_lo_ready, k * KT + t + 1))
                            else:
                                gemm(Count(c0 + j, (h, C_FHALF), (i, 4)), (n0 + j) % 4, hn_hi, hn_lo, range(KT))
                    wait(pe, f_alo, Count(layer * FT + FH // 2, (h, FH)))
                    pe.sem_inc(pe_passed, 1)
                    with pe.Fori(0, KT // 4) as i:
                        for j in range(4):
                            wait(pe, res_added, Count(ed0 + j - 3, (h, KT), (i, 4)))
                            for q in range(2):
                                if j == 0 and q == 1:
                                    wait(pe, f_alo, Count(layer * FT + FH, (h, FH)))
                                gemm(Count(c0 + 2 * FH + 2 * j + q, (h, C_FHALF), (i, 8)), (n0 + 2 * FH + j) % 4,
                                     act_hi, act_lo, range(q * FH // 2, (q + 1) * FH // 2), q == 0, q == 1)

            ffn(0, C_F0, N_F0, EA_F0, ED_F0, 1)
            first_project(Count(C_BGATE), (N_BIN - 1) % 4, 2)
            norm(2)

            def gate_columns_b():
                pe.wait_ge(gb_rows, 1)
                for n, row in enumerate((0, 1, 2)):
                    for b in range(3):
                        w = P if b < 2 else TS
                        m = nc.tensor.transpose(ps[0:w, M1 if n < 2 else M2, 192 * (n % 2) + 64 * b:192 * (n % 2) + 64 * b + 64],
                                                b_rows[:, row, b * P:b * P + w], ident[0:64, 0:64])
                m.then_inc(gb_turned, 1)

            def b_mix(u, p, j):
                bT, cT = b_io[:, p, 0, :], b_io[:, p, 1, :]
                if j == 0:
                    wait(pe, b_silu, u.plus(1).times(6))
                    wait(pe, b_gvar, u)
                    wait(pe, b_sadd, u.times(8))
                    wait(pe, b_spr, u.times(4))
                    score_blocks(M0, bT, cT)
                    turn_blocks(M1, bT)
                    for k in range(4):
                        turn(ps[:, M2, k * P:(k + 1) * P], b_io[:, p, 2 + k, 0:P])
                        m = turn(ps[:, M3, k * P:(k + 1) * P], b_io[:, p, 2 + k, P:TP])
                    m.then_inc(b_cbx, 1)
                if j in (1, 3, 5, 7):
                    k = (j - 1) // 2
                    if j == 1:
                        wait(pe, b_xt_out, u.plus(1))
                        for n in range(4):
                            m = turn(ps[0:TS, M2, n * P:(n + 1) * P], b_io[:, p, 2 + n, TP:T])
                        m.then_inc(b_xs, 1)
                        wait(pe, b_cbx_out, u.plus(1))
                    else:
                        wait(pe, b_sadd, u.times(8).plus(2 * k))
                    wait(pe, b_selr, u.times(4).plus(k + 1))
                    mm(ps[:, M0, 0:T], b_sel[:, 0, :], b_rows[:, 0, :])
                    mm(ps[:, M1, 0:T], b_sel[:, 1, :], b_rows[:, 0, :])
                    mm(ps[0:64, M1, T:T + TS], b_sel[:, 0, 0:64], b_rsum[:, 0:TS])
                    mm(ps[64:P, M1, T:T + TS], b_sel[:, 1, 0:64], b_rsum[:, 0:TS]).then_inc(b_rowsr, 1)
                if j in (2, 4, 6, 8):
                    k = (j - 2) // 2
                    ch = slice(k * P, (k + 1) * P)
                    wait(pe, b_wts, u.times(4).plus(k + 1))
                    wait(pe, b_xs_out, u.plus(1))
                    wait(pe, b_yg, u.times(4).plus(k))
                    wait(pe, b_sT_in, u.times(4).plus(k + 1).times(16))
                    for b in range(NB):
                        mm(ps[:, M2, T + SL * b:T + SL * (b + 1)], b_sT[:, b, :], cT[:, TP + SL * b:TP + SL * (b + 1)])
                    for e in range(2):
                        rows, hc = slice(64 * e, 64 * (e + 1)), slice(k * P + 64 * e, k * P + 64 * (e + 1))
                        mm(ps[rows, M2, 0:TP], b_xdt[:, 0, hc], b_dec[:, e, 0:TP], True, False)
                        mm(ps[rows, M2, P:TP], b_xdt[:, 1, hc], b_dec[:, e, TP:TP + P], False, False)
                        m = mm(ps[rows, M2, TP:T], b_xdt[0:TS, 2, hc], b_dec[0:TS, e, TP + P:SC], False, True)
                    m.then_inc(b_yst, 1)
                    wait(pe, b_xwr, u.times(4).plus(k + 1))
                    wait(pe, b_bmask, u.plus(1))
                    wait(pe, b_spr, u.times(4).plus(k))
                    for half in range(2):
                        mm(ps[:, M0 + half, :], b_xw[0:TS, 2, :], b_bm[:, 4 * half:4 * half + 4, :])
                    mm(ps[:, M3, 0:P], b_xw[:, 0, :], b_bt[:, 0, :], True, False)
                    mm(ps[:, M3, 0:P], b_xw[:, 1, :], b_bt[:, 1, :], False, True).then_inc(b_yst, 1)
                if j == 9:
                    wait(pe, b_gsq, u.plus(1).times(4))
                    wait(pe, b_yg, u.plus(1).times(4))
                    for k in range(4):
                        m = mm(ps[:, M2, 0:T], mean_mat[:], b_io[:, p, 2 + k, :], k == 0, k == 3)
                    m.then_inc(b_gms, 1)

            def b_group(u, p, c, mixed):
                for j in range(10):
                    wait(pe, proj_taken, u.times(10).plus(EA_BIN + j - 3))
                    gemm(c.plus(j), (N_BIN + 10 * p + j) % 4, hn_hi, hn_lo, range(KT))
                    if mixed is not None:
                        b_mix(mixed, 1 - p, j)
                    elif j == 2:
                        gate_columns_b()
                if mixed is None:
                    pe.wait_ge(gb_done, 1)

            def b_out_chunk(c, m, added, tiles, ready=None):
                for e in range(2):
                    wait(pe, res_added, added.plus(e - 3))
                    gemm(c, (N_BIN + 2 * m + e) % 4, b_out_hi, b_out_lo, tiles, at=8 * e, done=e == 1,
                         each=(lambda k: wait(pe, b_glo, ready[k])) if ready and e == 0 else None)

            def b_out_all(c, added, tiles, ready):
                with pe.Fori(0, C_BOUT // 2) as i:
                    for m in range(2):
                        b_out_chunk(c.plus(m).add(i, 2), m, added.plus(2 * m).add(i, 4), tiles, ready if m == 0 else None)

            b_group(Count(0), 0, Count(C_BIN), None)
            b_group(Count(1), 1, Count(C_BIN + 10), Count(0))
            with pe.Fori(0, 2) as i:
                for n in range(2):
                    b_group(Count(2 + n, (i, 2)), n, Count(C_BIN + 20 + 10 * n, (i, C_BTURN)), Count(1 + n, (i, 2)))
                b_out_all(Count(C_BIN + 40, (i, C_BTURN)), Count(ED_BIN, (i, KT)), range(4, 12),
                          [Count(4 + k + 1, (i, 8)) for k in range(8)])
            b_group(Count(6), 0, Count(C_BIN + 76), Count(5))
            b_group(Count(7), 1, Count(C_BIN + 86), Count(6))
            for j in range(10):
                if j < C_BOUT:
                    b_out_chunk(Count(C_BIN + 96 + j), j, Count(ED_BIN + 2 * KT + 2 * j), range(4, 12),
                                [Count(20 + k + 1) for k in range(8)] if j == 0 else None)
                b_mix(Count(7), 1, j)
            b_out_all(Count(C_BIN + 104), Count(ED_BIN + 3 * KT), [0, 1, 2, 3, 12, 13, 14, 15],
                      [Count(28 + max(k - 3, 0)) for k in range(8)])
            ffn(1, C_F1, N_F1, EA_F1, ED_F1, 3)
            norm(4)

        @block.scalar
        def _(act):
            own = Own(act, act_own)
            A = nc.scalar.activation

            def split(c, cols=CH):
                wait(act, raw_landed[c.base % 2], c.half().plus(1).times(16))
                wait(act, chunk_done, c.plus(-1))
                A(w_hi[:, c.base % 2, 0:cols], w_raw[:, c.base % 2, 0:cols], ACT.Copy).then_inc(w_high, 1)

            def norm(k):
                wait(act, var_ready, k + 1)
                A(rstd[:], rstd[:], ACT.Sqrt).then_inc(root_ready, 1)

            def input_high(k, t):
                A(hn_hi[:, t, :], x[:, t, :], ACT.Copy, scale=norm_w[:, k, t:t + 1] if isinstance(t, int)
                  else norm_w[:, k, bass.ds(t, 1)]).then_inc(hn_hi_ready, 1)

            def new_tile(buf, t, added, sq, k):
                wait(act, res_added, added)
                wait(act, sq_added, sq.plus(-1))
                A(work[:, buf, :], x[:, t.value, :], ACT.Square).then_inc(squared, 1)
                if k is not None:
                    input_high(k, t.value)

            def residual(c0, tiles_done, sq0, per, last=False, k=None):
                def pair(i, tail):
                    for j in range(2):
                        for q in range(per):
                            ahead = tail and j * per + q >= 2 * per - 2
                            if not (ahead and last):
                                split(c0.plus(j * per + q + 2).add(i, 2 * per), CH if ahead or per == 1 else DCH)
                        if sq0 is not None:
                            new_tile(j, Count(j).add(i, 2), tiles_done.plus(j + 1).add(i, 2), sq0.plus(j).add(i, 2), k)
                with act.Fori(0, KT // 2 - (per - 1)) as i:
                    pair(i, False)
                if per == 2:
                    pair(KT // 2 - 1, True)

            split(Count(0))
            act.wait_ge(norm_w_in, 16)
            for t in range(KT):
                act.wait_ge(x_in[t // 4], 16)
                input_high(0, t)
            split(Count(1))
            for t in range(KT):
                wait(act, sq_added, t - 1)
                A(work[:, t % 2, :], x[:, t, :], ACT.Square).then_inc(squared, 1)
                if t == KT // 2:
                    split(Count(2))
            act.wait_ge(consts_in, N_CONSTS)
            norm(0)
            act.wait_ge(proj_taken, 1)
            A(a_rows[:, 0, :], a_rows[:, 0, :], ACT.Identity, bias=a_small[:, 0:1])
            own.link(A(a_rows[:, 1, :], a_rows[:, 1, :], ACT.Identity, bias=a_small[:, 1:2]))
            own.link(A(a_rows[:, 2, :], a_rows[:, 1, :], ACT.Abs))
            A(a_rows[:, 3, :], a_rows[:, 2, :], ACT.Exp, scale=-1.0).then_inc(ga_exp, 1)
            act.wait_ge(ga_onep, 1)
            A(a_rows[:, 4, :], a_rows[:, 2, :], ACT.Ln).then_inc(ga_ln, 1)
            act.wait_ge(ga_logs, 1)
            A(a_rows[:, 6, :], a_rows[:, 6, :], ACT.Exp)
            A(a_rows[:, 8, TP:T], a_rows[:, 8, TP:T], ACT.Exp).then_inc(ga_rows, 1)

            def gate_columns():
                act.wait_ge(ga_turned, 1)
                cols = ps[:, M1, 0:48].rearrange("p (n b h) -> p n h b", n=2, b=3)
                A(a_acol[:, :, 0:2], cols[:, 0, :, 0:2], ACT.Copy)
                A(a_wcol[:, :, 0:2], cols[:, 1, :, 0:2], ACT.Copy)
                A(a_acol[0:TS, :, 2], cols[0:TS, 0, :, 2], ACT.Copy)
                A(a_wcol[0:TS, :, 2], cols[0:TS, 1, :, 2], ACT.Copy).then_inc(ga_done, 1)
                act.wait_ge(ga_done, 1)

            def a_post(u, p, j):
                if j >= 4:
                    wait(act, proj_taken, u.times(6).plus(1 + j + 1))
                    A(a_io[:, p, j, :], a_io[:, p, j, :], ACT.Tanh, scale=0.5).then_inc(a_otanh, 1)

            def a_mix(u, p, j):
                h = u.value
                if j == 1:
                    wait(act, a_kv0, u.plus(1))
                    wait(act, a_cupd, u.times(4))
                    wait(act, a_vmask, u)
                    for b in range(2):
                        A(a_kw[:, b, :], ps[:, M2, b * P:(b + 1) * P], ACT.Copy, scale=a_wcol[:, h, b:b + 1])
                    A(a_kw[0:TS, 2, :], ps[0:TS, M2, 2 * P:3 * P], ACT.Copy, scale=a_wcol[0:TS, h, 2:3])
                    A(a_vt[:, 0:2, 0:P], ps[:, M3, 0:2 * P].rearrange("p (b e) -> p b e", b=2), ACT.Copy)
                    A(a_vt[0:TS, 2, 0:P], ps[0:TS, M3, 2 * P:3 * P], ACT.Copy).then_inc(a_kv0_tok, 1)
                    wait(act, a_dlog, u.plus(1))
                    A(a_dec[:], a_dec[:], ACT.Exp, scale=-1.0).then_inc(a_dexp, 1)
                if j == 2:
                    wait(act, a_v1, u.plus(1))
                    wait(act, a_htmp, u.times(2))
                    A(a_vt[:, 0:2, P:2 * P], ps[:, M2, 0:2 * P].rearrange("p (b e) -> p b e", b=2), ACT.Copy)
                    A(a_vt[0:TS, 2, P:2 * P], ps[0:TS, M2, 2 * P:3 * P], ACT.Copy)
                    A(a_em[:], ps[:, M3, 0:T], ACT.Exp, scale=-1.0).then_inc(a_v1_tok, 1)
                if j == 3:
                    for e in range(2):
                        wait(act, a_htmp, u.times(2).plus(e + 1))
                        A(a_out_hi[:, u.times(2).plus(e).value, :], a_h[:, e, :], ACT.Copy).then_inc(a_hhi, 1)
                if j == 4:
                    wait(act, a_cupd, u.times(4).plus(1))
                    wait(act, a_cp_out, u.times(16))
                    A(a_nnew[:, h, 0:1], ps[:, M3, A_DV:A_DV + 1], ACT.Copy)
                    A(a_cp[:], ps[:, M3, 0:A_DV], ACT.Copy).then_inc(a_cp_ready, 1)

            def a_head(u, p, mixed):
                for j in range(6):
                    if mixed is not None:
                        a_mix(mixed, 1 - p, j)
                    split(u.times(6).plus(C_AIN + j + 2))
                    a_post(u, p, j)

            a_head(Count(0), 0, None)
            gate_columns()
            a_head(Count(1), 1, Count(0))
            with act.Fori(0, 3) as i:
                for n in range(2):
                    a_head(Count(2 + n, (i, 2)), n, Count(1 + n, (i, 2)))
            for j in range(6):
                a_mix(Count(7), 1, j)
            residual(Count(C_AOUT), Count(0), Count(KT), 1, k=1)

            def ffn(layer, c0, ea0, ed0, k):
                first = 2 * FT * layer

                def half(h):
                    last = layer == 1 and h == 1
                    def pair(i, par):
                        m = Count(first // 2 + par).add(h, FH).add(i, 2)
                        for j in range(2):
                            s = 2 * par + j
                            n = Count(s).add(h, 2 * FH).add(i, 4)
                            c = Count(c0 + s).add(h, C_FHALF).add(i, 4)
                            split(c.plus(2))
                            if j == 1:
                                wait(act, f_conved, m.times(2).plus(1 + 4 * (layer + 1)))
                                wait(act, f_alo, m.plus(-1))
                                gate, th = f_u[:, 2 * par, :], f_act[:, par, :]
                                A(th[:, 0:TP], gate[:, 0:TP], ACT.Tanh)
                                A(packed(th), f_samples(gate)[:, :, 0:SL], ACT.Tanh).then_inc(f_gated, 1)
                            wait(act, proj_taken, n.plus(ea0 + 1))
                            w = lambda tap: f_conv[:, layer, n.value, tap:tap + 1]
                            A(f_u[:, s, 0:FP - 2], f_pad[:, s, 0:FP - 2], ACT.Identity, bias=w(3),
                              scale=w(0)).then_inc(f_tap0, 1)
                        wait(act, f_prod, m.plus(1))
                        A(act_hi[:, Count(par).add(i, 2).value, :], f_act[:, par, :], ACT.Copy).then_inc(f_ahi, 1)

                    with act.Fori(0, FH // 2) as i:
                        for par in range(2):
                            pair(i, par)
                    residual(Count(c0 + 2 * FH).add(h, C_FHALF), Count(ed0).add(h, KT),
                             Count(KT * (k + 1)) if h == 1 else None, 2, last, 2 if layer == 0 and h == 1 else None)

                norm(k)
                half(0)
                half(1)

            ffn(0, C_F0, EA_F0, ED_F0, 1)

            split(Count(C_BGATE + 2))
            norm(2)
            wait(act, proj_taken, EA_BGATE + 1)
            own.link(A(b_rows[:, 1, :], b_rows[:, 1, :], ACT.Identity, bias=b_small[:, 0:1]))
            A(b_rsum[:, TS:TS + 1], b_small[:, 1:2], ACT.Exp)
            own.link(A(b_rows[:, 3, :], b_rows[:, 1, :], ACT.Abs))
            A(b_rows[:, 2, :], b_rows[:, 3, :], ACT.Exp, scale=-1.0).then_inc(gb_exp, 1)
            act.wait_ge(gb_onep, 1)
            A(b_rows[:, 4, :], b_rows[:, 3, :], ACT.Ln).then_inc(gb_ln, 1)
            act.wait_ge(gb_logs, 1)
            A(b_rows[:, 2, :], b_rows[:, 2, :], ACT.Exp, scale=-1.0)
            A(b_rsum[:, 0:TS], b_rows[:, 0, TP:T], ACT.Exp, scale=-1.0).then_inc(gb_rows, 1)

            def gate_columns_b():
                act.wait_ge(gb_turned, 1)
                for n, col in enumerate((b_nac, b_dtc, b_end)):
                    src = ps[:, M1 if n < 2 else M2, 192 * (n % 2):192 * (n % 2) + 192].rearrange(
                        "p (b g h) -> p g b h", b=3, g=B_GROUPS)
                    for b in range(3):
                        w = P if b < 2 else TS
                        m = A(col[0:w, :, b, :], src[0:w, :, b, :], ACT.Copy)
                m.then_inc(gb_done, 1)
                act.wait_ge(gb_done, 1)

            def b_first_tap(u, p, j):
                wait(act, proj_taken, u.times(10).plus(EA_BIN + j + 1))
                n = u.times(6).plus(j)
                if j < 6:
                    wait(act, b_silu, n)
                    w = lambda tap: b_conv[:, n.value, tap:tap + 1]
                    A(b_u[:, 0:BP - 3], b_pad[:, j % 2, 0:BP - 3], ACT.Identity, bias=w(4), scale=w(0)).then_inc(b_tap0, 1)
                else:
                    if j == 6:
                        wait(act, b_silu, u.times(6).plus(6))
                    else:
                        wait(act, b_zready, u.times(4).plus(j - 6))
                    A(b_th[:, 0:T], b_io[:, p, j, :], ACT.Tanh, scale=0.5).then_inc(b_ztanh, 1)

            def b_tanh_of(u, j):
                if j < 6:
                    wait(act, b_conved, u.times(6).plus(j + 3))
                    if j == 0:
                        wait(act, b_zready, u.times(4))
                    A(b_th[:, 0:BP - 3], b_u[:, 0:BP - 3], ACT.Tanh).then_inc(b_tanh, 1)

            def b_mix(u, p, j):
                if j == 1:
                    wait(act, b_cbx, u.plus(1))
                    wait(act, b_wts, u.times(4))
                    wait(act, b_yst, u.times(8))
                    wait(act, b_bmask, u)
                    A(b_cb[:, 0:TP + P], ps[:, M0, 0:TP + P], ACT.Copy)
                    A(b_cb[0:TS, TP + P:SC], ps[0:TS, M0, TP + P:SC], ACT.Copy)
                    A(b_bt[:, 0:2, :], ps[:, M1, 0:2 * P].rearrange("p (b e) -> p b e", b=2), ACT.Copy)
                    A(b_bt[0:TS, 2, :], ps[0:TS, M1, 2 * P:3 * P], ACT.Copy).then_inc(b_cbx_out, 1)
                if j in (2, 4, 6, 8):
                    k = (j - 2) // 2
                    wait(act, b_dlog, u.times(4).plus(k + 1))
                    A(b_dec[:], b_dec[:], ACT.Exp, scale=-1.0).then_inc(b_dexp, 1)
                if j in (3, 5, 7, 9):
                    k = (j - 3) // 2
                    n = u.times(4).plus(k)
                    wait(act, b_yst, n.times(2).plus(2))
                    wait(act, b_sp_out, n.times(16))
                    A(b_sp[:], ps[:, M3, 0:P], ACT.Copy).then_inc(b_spr, 1)
                    wait(act, b_yg, n.plus(1))
                    A(b_io[:, p, 2 + k, :], b_io[:, p, 6 + k, :], ACT.Square).then_inc(b_gsq, 1)

            def b_group_norm(u, p):
                wait(act, b_gvar, u.plus(1))
                A(b_r[:], b_r[:], ACT.Sqrt).then_inc(b_groot, 1)
                for k in range(4):
                    wait(act, b_gn, u.times(4).plus(k + 1))
                    A(b_out_hi[:, b_place(u, p) + k, :], work[:, k % 2, :], ACT.Copy).then_inc(b_ghi, 1)

            def b_group(u, p, c, mixed):
                for j in range(10):
                    split(c.plus(j + 2))
                    b_first_tap(u, p, j)
                    mixes = mixed is not None and j < 9
                    if mixes and j % 2 == 1:
                        b_mix(mixed, 1 - p, j + 1)
                    b_tanh_of(u, j)
                    if mixes and j % 2 == 0:
                        b_mix(mixed, 1 - p, j + 1)
                    if mixed is None and j == 3:
                        gate_columns_b()
                if mixed is not None:
                    b_group_norm(mixed, 1 - p)

            def b_out_all(c, added=None, sq=None, k=None):
                with act.Fori(0, C_BOUT // 2) as i:
                    for m in range(2):
                        split(c.plus(m + 2).add(i, 2))
                        for e in range(2):
                            if k is not None:
                                t = Count(2 * m + e, (i, 4))
                                new_tile(e, t, t.plus(added + 1), t.plus(sq), k)

            b_group(Count(0), 0, Count(C_BIN), None)
            b_group(Count(1), 1, Count(C_BIN + 10), Count(0))
            with act.Fori(0, 2) as i:
                for n in range(2):
                    b_group(Count(2 + n, (i, 2)), n, Count(C_BIN + 20 + 10 * n, (i, C_BTURN)), Count(1 + n, (i, 2)))
                b_out_all(Count(C_BIN + 40, (i, C_BTURN)))
            b_group(Count(6), 0, Count(C_BIN + 76), Count(5))
            b_group(Count(7), 1, Count(C_BIN + 86), Count(6))
            for j in range(10):
                if j < C_BOUT:
                    split(Count(C_BIN + 96 + j + 2))
                if j < 9:
                    b_mix(Count(7), 1, j + 1)
            b_group_norm(Count(7), 1)
            b_out_all(Count(C_BIN + 104), ED_BIN + 3 * KT, 3 * KT, 3)
            ffn(1, C_F1, EA_F1, ED_F1, 3)
            norm(4)

        @block.vector
        def _(dve):
            own = Own(dve, dve_own)
            V = nc.vector
            STT, TT, TS_ = V.scalar_tensor_tensor, V.tensor_tensor, V.tensor_scalar

            def split(c, cols=CH):
                wait(dve, w_high, c.plus(1))
                s = c.base % 2
                TT(w_lo[:, s, 0:cols], w_raw[:, s, 0:cols], w_hi[:, s, 0:cols].bitcast(F32), ALU.subtract).then_inc(w_low, 1)

            def norm(k):
                wait(dve, mean_ready, k + 1)
                TS_(rstd[:], ps[:, M0, 0:T], EPS, None, ALU.add).then_inc(var_ready, 1)
                wait(dve, root_ready, k + 1)
                V.reciprocal(rstd[:], rstd[:]).then_inc(rstd_ready, 1)
                wait(dve, rstd_ready, k + 1)

            def input_low(k, t):
                wait(dve, hn_hi_ready, t.plus(KT * k + 1))
                t = t.value
                w = norm_w[:, k, t:t + 1] if isinstance(t, int) else norm_w[:, k, bass.ds(t, 1)]
                STT(hn_lo[:, t, :], x[:, t, :], w, hn_hi[:, t, :].bitcast(F32), ALU.mult, ALU.subtract).then_inc(hn_lo_ready, 1)

            def residual(c0, n0, per, last=False, k=None):
                def four(i, tail):
                    for j in range(4):
                        for q in range(per):
                            ahead = tail and j * per + q >= 4 * per - 2
                            if q == per - 1:
                                wait(dve, chunk_done, c0.plus((j + 1) * per).add(i, 4 * per))
                                t = Count(j).add(i, 4).value
                                TT(x[:, t, :], x[:, t, :], ps[:, (n0 + j) % 4, 0:T], ALU.add).then_inc(res_added, 1)
                            if not (ahead and last):
                                split(c0.plus(j * per + q + 2).add(i, 4 * per), CH if ahead or per == 1 else DCH)
                        if k is not None:
                            input_low(k, Count(j).add(i, 4))
                with dve.Fori(0, KT // 4 - (per - 1)) as i:
                    four(i, False)
                if per == 2:
                    four(KT // 4 - 1, True)

            split(Count(0))
            dve.wait_ge(norm_w_in, 16)
            for t in range(KT):
                input_low(0, Count(t))
            split(Count(1))
            dve.wait_ge(consts_in, N_CONSTS)
            TS_(b_conv[:], b_conv[:], 0.5, None, ALU.mult)
            gate_taps = f_conv[:].rearrange("p l (t two) k -> p l t two k", two=2)[:, :, :, 0, :]
            TS_(gate_taps, gate_taps, 0.5, None, ALU.mult)
            TS_(b_normw[:], b_normw[:], 0.5, None, ALU.mult)
            V.memset(a_dec[:], 0.0)

            split(Count(2))
            norm(0)
            TT(a_rows[:, 0, :], ps[0:8, 0, 0:T], rstd[0:8, :], ALU.mult)
            TT(a_rows[:, 1, :], ps[32:40, 0, 0:T], rstd[32:40, :], ALU.mult).then_inc(proj_taken, 1)
            row = lambda n: a_rows[:, n, :]
            dve.wait_ge(ga_exp, 1)
            TS_(row(2), row(3), 1.0, None, ALU.add).then_inc(ga_onep, 1)
            dve.wait_ge(ga_onep, 1)
            own.link(TS_(row(5), row(2), -1.0, None, ALU.add))
            own.link(TT(row(5), row(3), row(5), ALU.subtract))
            own.link(V.reciprocal(row(6), row(2)))
            own.link(TT(row(5), row(5), row(6), ALU.mult))
            dve.wait_ge(ga_ln, 1)
            own.link(TT(row(4), row(4), row(5), ALU.add))
            own.link(STT(row(1), row(1), 0.0, row(4), ALU.min, ALU.subtract))
            own.link(V.tensor_tensor_scan(row(3), seg_keep[0:8, :], row(1), 0.0, ALU.mult, ALU.add))
            own.link(TT(row(4), row(0), row(3), ALU.subtract))
            own.link(V.tensor_copy(row(2), row(4)))
            m0 = a_small[:, 2:2 + NB]
            own.mark(TS_(a_rows[:, 2, 0:1], a_rows[:, 4, 0:1], 0.0, None, ALU.max))
            own.link(TT(packed(row(2))[:, :, 0], packed(row(4))[:, :, 0], m0, ALU.max))
            own.link(V.tensor_tensor_scan(row(5), seg_drop[:], row(2), 0.0, ALU.add, ALU.max))
            own.link(TT(row(7), row(3), row(5), ALU.add))
            TS_(a_rows[:, 6, 0:TP], a_rows[:, 4, 0:TP], a_rows[:, 5, TP - 1:TP], None, ALU.subtract)
            m_end = packed(row(5))[:, :, SL - 1:SL].to_broadcast([8, NB, SL])
            TT(packed(row(6)), packed(row(4)), m_end, ALU.subtract)
            TT(packed(row(8)), m0.unsqueeze(2).to_broadcast([8, NB, SL]), packed(row(5)), ALU.subtract)
            V.tensor_copy(a_mnew[:, 0:1], a_rows[:, 7, TP - 1:TP])
            V.tensor_copy(a_mnew[:, 1:], packed(row(7))[:, :, SL - 1]).then_inc(ga_logs, 1)

            A_STEPS = 8

            def a_link(u, k, ins):
                ins.then_inc(a_steps, 1)
                wait(dve, a_steps, u.times(A_STEPS).plus(k))

            def a_mix(u, p, j):
                h = u.value
                q = a_io[:, p, 0, TP:T]
                if j == 1:
                    wait(dve, a_scores, u.plus(1))
                    STT(a_dec[:, 0:TP], ps[:, M1, 0:TP], a_acol[:, h, 0:1], future[:, 0:TP], ALU.subtract, ALU.max)
                    STT(a_dec[:, TP:TP + P], ps[:, M1, P:TP], a_acol[:, h, 1:2], future[:, TP:TP + P], ALU.subtract, ALU.max)
                    STT(a_dec[0:TS, TP + P:SC], ps[0:TS, M1, TP:T], a_acol[0:TS, h, 2:3], future[0:TS, TP + P:SC],
                        ALU.subtract, ALU.max).then_inc(a_dlog, 1)
                    wait(dve, a_num, u)
                    a_link(u, 1, V.tensor_copy(a_wi[:], ps[:, M1, T:T + TS]))
                    a_link(u, 2, TT(a_qs[:], q, a_wi[:], ALU.mult))
                    by_batch = lambda t: t.rearrange("p (b l) -> p b l", l=SL)
                    TT(by_batch(a_nq[:]), by_batch(a_qs[:]), a_n[:, h, :].unsqueeze(2).to_broadcast([P, NB, SL]), ALU.mult)
                    wait(dve, a_dexp, u.plus(1))
                    TT(a_prob[:, 0:TP + P], ps[:, M0, 0:TP + P], a_dec[:, 0:TP + P], ALU.mult)
                    TT(a_prob[0:TS, TP + P:SC], ps[0:TS, M0, TP + P:SC], a_dec[0:TS, TP + P:SC], ALU.mult).then_inc(a_probs, 1)
                if j == 2:
                    wait(dve, a_otanh, u.times(2).plus(2))
                    a_link(u, 3, TS_(a_io[:, p, 4:6, :], a_io[:, p, 4:6, :], 0.5, 0.5, ALU.mult, ALU.add))
                if j == 3:
                    wait(dve, a_num, u.plus(1))
                    wait(dve, a_v1_tok, u.plus(1))
                    a_link(u, 4, STT(a_em[:], ps[:, M2, 0:T], -1.0, a_em[:], ALU.mult, ALU.max))
                    a_link(u, 5, TT(a_em[:], a_em[:], ps[:, M2, 0:T], ALU.max))
                    a_link(u, 6, V.reciprocal(a_em[:], a_em[:]))
                    a_link(u, 7, TT(a_io[:, p, 4:6, :], a_io[:, p, 4:6, :], a_em[:].unsqueeze(1).to_broadcast([P, 2, T]), ALU.mult))
                    for e in range(2):
                        TT(a_h[:, e, :], ps[:, M0 + e, 0:T], a_io[:, p, 4 + e, :], ALU.mult).then_inc(a_htmp, 1)
                    for e in range(2):
                        n = u.times(2).plus(e)
                        wait(dve, a_hhi, n.plus(1))
                        TT(a_out_lo[:, n.value, :], a_h[:, e, :], a_out_hi[:, n.value, :].bitcast(F32),
                           ALU.subtract).then_inc(a_hlo, 1)
                last_step = a_wi[:].rearrange("p (b l) -> p b l", l=SL)[:, :, SL - 1]

                def c_add(n):
                    wait(dve, a_cupd, u.times(4).plus(n + 1))
                    for e in range(2):
                        b = 2 * n + e
                        m = STT(a_c[:, p, b, :], a_c[:, p, b, :], a_wi[:, SL * b + SL - 1:SL * (b + 1)],
                                ps[:, M0 + n % 3, e * A_DV:(e + 1) * A_DV], ALU.mult, ALU.add)
                    m.then_inc(a_cadd, 1)
                if j == 4:
                    wait(dve, a_cupd, u.times(4).plus(1))
                    wait(dve, a_cp_ready, u.plus(1))
                    a_link(u, 8, TT(a_nnew[:, h, 1:1 + NB], a_n[:, h, :], last_step, ALU.mult))
                    TT(a_nnew[:, h, 1:1 + NB], a_nnew[:, h, 1:1 + NB], ps[:, M3, A_DV + 1:A_DV + 1 + NB], ALU.add)
                    for n in range(3):
                        c_add(n)
                if j == 5:
                    c_add(3)

            def a_take(u, p, j):
                c = u.times(6).plus(C_AIN + j)
                if j == 0 and u.base > 0:
                    wait(dve, a_v1, u.plus(-1))
                wait(dve, chunk_done, c.plus(1))
                STT(a_io[:, p, j, :], ps[:, c.base % 4, 0:T], A_DK ** -0.5 if j == 1 else 1.0, rstd[:], ALU.mult,
                    ALU.mult).then_inc(proj_taken, 1)

            def a_head(u, p, mixed):
                for j in range(6):
                    if mixed is not None:
                        a_mix(mixed, 1 - p, j)
                    a_take(u, p, j)
                    split(u.times(6).plus(C_AIN + j + 2))

            a_head(Count(0), 0, None)
            dve.wait_ge(ga_done, 1)
            dve.wait_ge(a_n_in, 16)
            a_head(Count(1), 1, Count(0))
            with dve.Fori(0, 3) as i:
                for n in range(2):
                    a_head(Count(2 + n, (i, 2)), n, Count(1 + n, (i, 2)))
            for j in range(6):
                a_mix(Count(7), 1, j)
            residual(Count(C_AOUT), N_AOUT, 1, k=1)

            def ffn(layer, c0, n0, ea0, k):
                first = 2 * FT * layer
                if layer == 0:
                    for s in a_c_out:
                        dve.wait_ge(s, 16 * A_HEADS // 2)
                    dve.wait_ge(a_cp_out, 16 * A_HEADS)
                    dve.wait_ge(a_nm_out, 32)
                else:
                    dve.wait_ge(b_s_out, 16 * 32)
                    dve.wait_ge(b_sp_out, 16 * 32)
                    dve.wait_ge(b_new_out, 16 * B_GROUPS)
                wait(dve, mean_ready, k + 1)
                for s in range(4):
                    V.memset(f_pad[:, s, 0:2], 0.0).then_inc(f_conved, 1)
                norm(k)

                def half(h):
                    last = layer == 1 and h == 1
                    def pair(i, par):
                        m = Count(first // 2 + par).add(h, FH).add(i, 2)
                        for j in range(2):
                            s = 2 * par + j
                            n = Count(s).add(h, 2 * FH).add(i, 4)
                            c = Count(c0 + s).add(h, C_FHALF).add(i, 4)
                            wait(dve, chunk_done, c.plus(1))
                            wait(dve, f_prefix, n.plus(first + 1))
                            src = ps[:, (c0 + s) % 4, 0:T]
                            TT(f_pad[:, s, 2:2 + TP], src[:, 0:TP], rstd[:, 0:TP], ALU.mult)
                            TT(f_samples(f_pad[:, s, :])[:, :, 2:], packed(src), packed(rstd), ALU.mult).then_inc(proj_taken, 1)
                            split(c.plus(2))
                            g, v, prod = f_u[:, 2 * par, :], f_u[:, 2 * par + 1, :], f_act[:, par, :]
                            if j == 1:
                                wait(dve, f_gated, m.plus(1))
                                STT(prod[:, 0:TP], prod[:, 0:TP], 1.0, g[:, 0:TP], ALU.add, ALU.mult)
                                STT(packed(prod), packed(prod), 1.0, f_samples(g)[:, :, 0:SL], ALU.add,
                                    ALU.mult).then_inc(f_silu, 1)
                            wait(dve, proj_taken, n.plus(ea0 + 1))
                            wait(dve, f_tap0, n.plus(first + 1))
                            w = lambda tap: f_conv[:, layer, n.value, tap:tap + 1]
                            STT(f_u[:, s, 0:FP - 2], f_pad[:, s, 1:FP - 1], w(1), f_u[:, s, 0:FP - 2], ALU.mult,
                                ALU.add).then_inc(f_tap1, 1)
                            wait(dve, f_tap1, n.plus(first + 1))
                            STT(f_u[:, s, 0:FP - 2], f_pad[:, s, 2:FP], w(2), f_u[:, s, 0:FP - 2], ALU.mult,
                                ALU.add).then_inc(f_conved, 1)
                        wait(dve, f_silu, m.plus(1))
                        wait(dve, f_conved, m.times(2).plus(2 + 4 * (layer + 1)))
                        TT(prod[:, 0:TP], prod[:, 0:TP], v[:, 0:TP], ALU.mult)
                        TT(packed(prod), packed(prod), f_samples(v)[:, :, 0:SL], ALU.mult).then_inc(f_prod, 1)
                        wait(dve, f_ahi, m.plus(1))
                        t = Count(par).add(i, 2).value
                        TT(act_lo[:, t, :], f_act[:, par, :], act_hi[:, t, :].bitcast(F32), ALU.subtract).then_inc(f_alo, 1)

                    with dve.Fori(0, FH // 2) as i:
                        for par in range(2):
                            pair(i, par)
                    residual(Count(c0 + 2 * FH).add(h, C_FHALF), n0 + 2 * FH, 2, last, 2 if layer == 0 and h == 1 else None)

                half(0)
                half(1)

            ffn(0, C_F0, N_F0, EA_F0, 1)

            dve.wait_ge(f_new_out, 16)
            wait(dve, mean_ready, 3)
            for s in range(2):
                V.memset(b_pad[:, s, 0:3], 0.0).then_inc(b_conved, 1)
            V.memset(b_cb[:], 0.0)
            V.memset(b_dec[:], 0.0)
            split(Count(C_BGATE + 2))
            norm(2)
            TT(b_rows[:, 1, :], ps[0:64, (N_BIN - 1) % 4, 0:T], rstd[0:64, :], ALU.mult).then_inc(proj_taken, 1)
            brow = lambda n: b_rows[:, n, :]
            dve.wait_ge(gb_exp, 1)
            TS_(brow(3), brow(2), 1.0, None, ALU.add).then_inc(gb_onep, 1)
            dve.wait_ge(gb_onep, 1)
            own.link(TS_(brow(0), brow(3), -1.0, None, ALU.add))
            own.link(TT(brow(0), brow(2), brow(0), ALU.subtract))
            own.link(V.reciprocal(brow(2), brow(3)))
            own.link(TT(brow(0), brow(0), brow(2), ALU.mult))
            dve.wait_ge(gb_ln, 1)
            own.link(TT(brow(4), brow(4), brow(0), ALU.add))
            own.link(STT(brow(1), brow(1), 0.0, brow(4), ALU.max, ALU.add))
            own.link(TS_(brow(4), brow(1), b_rsum[:, TS:TS + 1], None, ALU.mult))
            own.link(V.tensor_tensor_scan(brow(0), seg_keep[:], brow(4), 0.0, ALU.mult, ALU.add))
            own.link(TS_(b_rows[:, 2, 0:TP], b_rows[:, 0, 0:TP], -1.0, b_rows[:, 0, TP - 1:TP], ALU.mult, ALU.add))
            end = packed(brow(0))[:, :, SL - 1:SL].to_broadcast([64, NB, SL])
            TT(packed(brow(2)), end, packed(brow(0)), ALU.subtract).then_inc(gb_logs, 1)

            def b_take(u, p, c, j):
                wait(dve, chunk_done, c.plus(j + 1))
                src = ps[:, (N_BIN + 10 * p + j) % 4, 0:T]
                if j < 6:
                    wait(dve, b_prefix, u.times(6).plus(j + 1))
                    TT(b_pad[:, j % 2, 3:3 + TP], src[:, 0:TP], rstd[:, 0:TP], ALU.mult)
                    TT(b_samples(b_pad[:, j % 2, :])[:, :, 3:], packed(src), packed(rstd), ALU.mult).then_inc(proj_taken, 1)
                else:
                    TT(b_io[:, p, j, :], src, rstd[:], ALU.mult).then_inc(proj_taken, 1)

            def b_post(u, p, j):
                n = u.times(6).plus(j)
                if j < 6:
                    wait(dve, proj_taken, u.times(10).plus(EA_BIN + j + 1))
                    pad, out = b_pad[:, j % 2, :], b_u[:, 0:BP - 3]
                    w = lambda tap: b_conv[:, n.value, tap:tap + 1]
                    wait(dve, b_tap0, n.plus(1))
                    STT(out, pad[:, 1:BP - 2], w(1), out, ALU.mult, ALU.add).then_inc(b_taps, 1)
                    wait(dve, b_taps, n.times(2).plus(1))
                    STT(out, pad[:, 2:BP - 1], w(2), out, ALU.mult, ALU.add).then_inc(b_taps, 1)
                    wait(dve, b_taps, n.times(2).plus(2))
                    STT(out, pad[:, 3:BP], w(3), out, ALU.mult, ALU.add).then_inc(b_conved, 1)
                    wait(dve, b_tanh, n.plus(1))
                    STT(b_io[:, p, j, 0:TP], b_th[:, 0:TP], 1.0, b_u[:, 0:TP], ALU.add, ALU.mult)
                    STT(packed(b_io[:, p, j, :]), b_samples(b_th)[:, :, 0:SL], 1.0, b_samples(b_u)[:, :, 0:SL], ALU.add,
                        ALU.mult).then_inc(b_silu, 1)
                else:
                    wait(dve, b_ztanh, u.times(4).plus(j - 6 + 1))
                    STT(b_io[:, p, j, :], b_th[:, 0:T], 1.0, b_io[:, p, j, :], ALU.add, ALU.mult).then_inc(b_zready, 1)

            B_STEPS = 4 * 3 + 1

            def b_link(u, k, ins):
                ins.then_inc(b_steps, 1)
                wait(dve, b_steps, u.times(B_STEPS).plus(k))

            def heads(ap, blocks=None):
                return ap.rearrange("p (h e) -> p h e", e=64)

            def b_mix(u, p, j):
                uv = u.value
                if j == 1:
                    wait(dve, b_cbx, u.plus(1))
                    wait(dve, b_xwr, u.times(4))
                    wait(dve, b_yst, u.times(8))
                    TT(heads(b_xdt[:, 0, :]), heads(ps[:, M2, :]), b_dtc[:, uv, 0, :].unsqueeze(2).to_broadcast([P, 8, 64]), ALU.mult)
                    TT(heads(b_xdt[:, 1, :]), heads(ps[:, M3, :]), b_dtc[:, uv, 1, :].unsqueeze(2).to_broadcast([P, 8, 64]),
                       ALU.mult).then_inc(b_xt_out, 1)
                if j == 2:
                    wait(dve, b_xs, u.plus(1))
                    TT(heads(b_xdt[0:TS, 2, :]), heads(ps[0:TS, M2, :]),
                       b_dtc[0:TS, uv, 2, :].unsqueeze(2).to_broadcast([TS, 8, 64]), ALU.mult).then_inc(b_xs_out, 1)
                if j in (2, 4, 6, 8):
                    k = (j - 2) // 2
                    n = u.times(4).plus(k)
                    wait(dve, b_rowsr, n.plus(1))
                    wait(dve, b_yst, n.times(2))
                    wait(dve, b_decayed, n)
                    V.tensor_copy(b_ea[:], ps[:, M1, T:T + TS])
                    for e in range(2):
                        col = lambda b, w: b_nac[0:w, uv, b, 2 * k + e:2 * k + e + 1]
                        STT(b_dec[:, e, 0:TP], ps[:, M0 + e, 0:TP], col(0, P), future[:, 0:TP], ALU.subtract, ALU.max)
                        STT(b_dec[:, e, TP:TP + P], ps[:, M0 + e, P:TP], col(1, P), future[:, TP:TP + P], ALU.subtract, ALU.max)
                        m = STT(b_dec[0:TS, e, TP + P:SC], ps[0:TS, M0 + e, TP:T], col(2, TS), future[0:TS, TP + P:SC],
                                ALU.subtract, ALU.max)
                    m.then_inc(b_dlog, 1)

            def b_weights(u, j):
                if j in (2, 4, 6, 8):
                    n = u.times(4).plus((j - 2) // 2)
                    wait(dve, b_cbx_out, u.plus(1))
                    wait(dve, b_dexp, n.plus(1))
                    TT(b_dec[:], b_dec[:], b_cb[:].unsqueeze(1).to_broadcast([P, 2, SC]), ALU.mult).then_inc(b_wts, 1)

            def b_outputs(u, p, j):
                if j in (3, 5, 7, 9):
                    k = (j - 3) // 2
                    n = u.times(4).plus(k)
                    wait(dve, b_yst, n.times(2).plus(1))
                    b_link(u, 3 * k + 1, TT(b_yi[:], ps[:, M2, T:T + TS], b_ea[:], ALU.mult))
                    y = b_io[:, p, 2 + k, :]
                    b_link(u, 3 * k + 2, STT(y, b_io[:, p, 2 + k, :], b_skip[:, n.value, 0:1], ps[:, M2, 0:T], ALU.mult, ALU.add))
                    b_link(u, 3 * k + 3, TT(y[:, TP:T], y[:, TP:T], b_yi[:], ALU.add))
                    wait(dve, b_zready, n.plus(1))
                    TT(b_io[:, p, 6 + k, :], y, b_io[:, p, 6 + k, :], ALU.mult).then_inc(b_yg, 1)
                    wait(dve, b_yst, n.times(2).plus(2))
                    wait(dve, b_decayed, n.plus(1))
                    for half in range(2):
                        s = b_s[:, 4 * half:4 * half + 4, :]
                        TT(s, s, ps[:, M0 + half, :].rearrange("p (b n) -> p b n", b=4), ALU.add).then_inc(b_sadd, 1)

            def b_group_norm(u, p):
                wait(dve, b_gms, u.plus(1))
                TS_(b_r[:], ps[:, M2, 0:T], EPS, None, ALU.add).then_inc(b_gvar, 1)
                wait(dve, b_groot, u.plus(1))
                b_link(u, 13, V.reciprocal(b_r[:], b_r[:]))
                for k in range(4):
                    n = u.times(4).plus(k)
                    if k > 1:
                        wait(dve, b_glo, n.plus(-1))
                    STT(work[:, k % 2, :], b_io[:, p, 6 + k, :], b_normw[:, n.value, 0:1], b_r[:], ALU.mult,
                        ALU.mult).then_inc(b_gn, 1)
                    wait(dve, b_ghi, n.plus(1))
                    t = b_place(u, p) + k
                    TT(b_out_lo[:, t, :], work[:, k % 2, :], b_out_hi[:, t, :].bitcast(F32),
                       ALU.subtract).then_inc(b_glo, 1)

            def b_group(u, p, c, mixed):
                for j in range(10):
                    mixes, even = mixed is not None and j < 9, j % 2 == 1
                    b_take(u, p, c, j)
                    if mixes and even:
                        b_mix(mixed, 1 - p, j + 1)
                    split(c.plus(j + 2))
                    if mixes and even:
                        b_weights(mixed, j + 1)
                    b_post(u, p, j)
                    if mixes and not even:
                        b_mix(mixed, 1 - p, j + 1)
                        b_outputs(mixed, 1 - p, j + 1)
                if mixed is None:
                    dve.wait_ge(gb_done, 1)
                else:
                    b_group_norm(mixed, 1 - p)

            def b_out_chunk(c, m, t, k=None):
                wait(dve, chunk_done, c.plus(1))
                for e in range(2):
                    xt = x[:, t.plus(e).value, :]
                    TT(xt, xt, ps[:, (N_BIN + 2 * m + e) % 4, 0:T], ALU.add).then_inc(res_added, 1)
                split(c.plus(2))
                for e in range(2):
                    if k is not None:
                        input_low(k, t.plus(e))

            def b_out_all(c, k=None):
                with dve.Fori(0, C_BOUT // 2) as i:
                    for m in range(2):
                        b_out_chunk(c.plus(m).add(i, 2), m, Count(2 * m, (i, 4)), k)

            b_group(Count(0), 0, Count(C_BIN), None)
            b_group(Count(1), 1, Count(C_BIN + 10), Count(0))
            with dve.Fori(0, 2) as i:
                for n in range(2):
                    b_group(Count(2 + n, (i, 2)), n, Count(C_BIN + 20 + 10 * n, (i, C_BTURN)), Count(1 + n, (i, 2)))
                b_out_all(Count(C_BIN + 40, (i, C_BTURN)))
            b_group(Count(6), 0, Count(C_BIN + 76), Count(5))
            b_group(Count(7), 1, Count(C_BIN + 86), Count(6))
            for j in range(10):
                if j % 2 == 1 and j < 9:
                    b_mix(Count(7), 1, j + 1)
                if j < C_BOUT:
                    b_out_chunk(Count(C_BIN + 96 + j), j, Count(2 * j))
                if j % 2 == 1 and j < 9:
                    b_weights(Count(7), j + 1)
                if j % 2 == 0:
                    b_mix(Count(7), 1, j + 1)
                    b_outputs(Count(7), 1, j + 1)
            b_group_norm(Count(7), 1)
            b_out_all(Count(C_BIN + 104), 3)
            ffn(1, C_F1, N_F1, EA_F1, 3)
            norm(4)
            for t in range(KT):
                STT(x[:, t, :], x[:, t, :], norm_w[:, 4, t:t + 1], rstd[:], ALU.mult, ALU.mult).then_inc(y_ready, 1)

        @block.gpsimd
        def _(pool):
            G = nc.gpsimd
            own = Own(pool, pool_own)

            def until(sem, count):
                wait(pool, sem, count)
                if isinstance(count, Count) and count.terms:
                    pool.sem_inc(pool_passed, 1)

            def add_square(r, buf):
                until(squared, r.plus(1))
                until(sq_added, r)
                G.tensor_tensor(sumsq[:], sumsq[:], work[:, buf, :], ALU.add).then_inc(sq_added, 1)

            def residual(norms, sq0, used=None):
                until(mean_ready, norms)
                if used is not None:
                    until(*used)
                own.link(G.memset(sumsq[:], 0.0))
                if own.terms:
                    pool.sem_inc(pool_passed, 1)
                with pool.Fori(0, KT // 2) as i:
                    for j in range(2):
                        add_square(sq0.plus(j).add(i, 2), j)

            own.link(G.memset(sumsq[:], 0.0))
            for t in range(KT):
                add_square(Count(t), t % 2)
            pool.dma_start(a_c[:, 0, :, :], d["a_c"][0]).then_inc(a_c_in[0], 16)
            pool.wait_ge(consts_in, N_CONSTS)

            def a_mix(u, p, j):
                if j == 0:
                    until(a_v1, u)
                    G.tensor_copy(a_sel[:], ident[0:8, bass.ds(u.value, 1)].to_broadcast([8, P])).then_inc(a_sel_ready, 1)
                if j == 1 and not (u.base == A_HEADS - 1 and not u.terms):
                    nxt = u.plus(1)
                    until(a_c_out[1 - p], nxt.half().times(16))
                    pool.dma_start(a_c[:, 1 - p, :, :], d["a_c"][nxt.value]).then_inc(a_c_in[1 - p], 16)
                if j == 2:
                    until(a_v1_tok, u.plus(1))
                    until(a_cupd, u.times(4))
                    G.tensor_tensor(a_vm[:], a_vt[0:TS, 2, :].unsqueeze(1).to_broadcast([TS, NB, A_DV]),
                                    in_batch[:].unsqueeze(2).to_broadcast([TS, NB, A_DV]), ALU.mult).then_inc(a_vmask, 1)
                if j == 5:
                    until(a_cadd, u.plus(1).times(4))
                    pool.dma_start(o["C_s"][u.value], a_c[:, p, :, :]).then_inc(a_c_out[p], 16)
                    until(a_cp_ready, u.plus(1))
                    pool.dma_start(o["C_p"][u.value], a_cp[:]).then_inc(a_cp_out, 16)

            def head(u, p):
                for j in range(6):
                    a_mix(u, p, j)

            head(Count(0), 0)
            with pool.Fori(0, 3) as i:
                for n in range(2):
                    head(Count(1 + n, (i, 2)), 1 - n)
            head(Count(7), 1)
            pool.dma_start(o["n"], a_nnew[:]).then_inc(a_nm_out, 16)
            pool.dma_start(o["m"], a_mnew[:]).then_inc(a_nm_out, 16)
            residual(1, Count(KT), (a_htmp, Count(2 * A_HEADS)))

            def ffn(layer, k):
                first = 2 * FT * layer
                if layer == 0:
                    for s in a_c_out:
                        pool.wait_ge(s, 16 * A_HEADS // 2)
                    pool.wait_ge(a_cp_out, 16 * A_HEADS)
                    pool.wait_ge(a_nm_out, 32)
                else:
                    pool.wait_ge(b_s_out, 16 * 32)
                    pool.wait_ge(b_sp_out, 16 * 32)
                    pool.wait_ge(b_new_out, 16 * B_GROUPS)
                until(mean_ready, k + 1)
                pool.dma_start(f_old[:], d["f_old"][layer]).then_inc(f_old_in, 16)
                pool.wait_ge(f_old_in, 16 * (layer + 1))

                def half(h):
                    with pool.Fori(0, FH // 2) as i:
                        for s in range(4):
                            n = Count(s).add(h, 2 * FH).add(i, 4)
                            until(f_conved, n.plus(first + 1 + 4 * layer))
                            pad = f_samples(f_pad[:, s, :])
                            G.tensor_copy(pad[:, :, 0:2], f_old[:, n.value, :].rearrange("p (b k) -> p b k", k=2)).then_inc(f_prefix, 1)
                            until(f_tap0, n.plus(first + 1))
                            G.tensor_copy(f_new[:, n.value, 0:2], f_pad[:, s, TP:TP + 2])
                            G.tensor_copy(f_new[:, n.value, 2:].rearrange("p (b k) -> p b k", k=2),
                                          pad[:, :, SL:SL + 2]).then_inc(f_kept, 1)

                with pool.Fori(0, 2) as h:
                    half(h)
                residual(k + 1, Count(KT * (k + 1)))
                pool.wait_ge(f_kept, first + 2 * FT)
                pool.dma_start(o["fconv"][layer], f_new[:]).then_inc(f_new_out, 16)

            ffn(0, 1)

            pool.wait_ge(f_new_out, 16)
            until(mean_ready, 3)

            def load_state(n):
                pool.dma_start(b_sT[:], d["b_sT"][n.value]).then_inc(b_sT_in, 16)
                pool.dma_start(b_s[:], d["b_s"][n.value]).then_inc(b_s_in, 16)

            def b_fill(u, j):
                n = u.times(6).plus(j)
                if j == 0:
                    until(b_old_in, u.plus(1).times(16))
                until(b_conved, n.plus(1))
                G.tensor_copy(b_samples(b_pad[:, j % 2, :])[:, :, 0:3],
                              b_old[:, j, :].rearrange("p (b k) -> p b k", k=3)).then_inc(b_prefix, 1)

            def b_post(u, p, j):
                if j >= 6:
                    return
                n = u.times(6).plus(j)
                pad = b_samples(b_pad[:, j % 2, :])
                if j == 0:
                    until(b_new_out, u.times(16))
                until(b_tap0, n.plus(1))
                G.tensor_copy(b_new[:, j, 0:3], b_pad[:, j % 2, TP:TP + 3])
                G.tensor_copy(b_new[:, j, 3:].rearrange("p (b k) -> p b k", k=3), pad[:, :, SL:SL + 3]).then_inc(b_kept, 1)
                if j == 5:
                    until(b_prefix, n.plus(1))
                    if u.base < B_GROUPS - 1:
                        pool.dma_start(b_old[:], d["b_old"][u.plus(1).value]).then_inc(b_old_in, 16)
                    until(b_kept, n.plus(1))
                    pool.dma_start(o["bconv"][u.value], b_new[:]).then_inc(b_new_out, 16)

            def b_mix(u, p, j):
                uv = u.value
                def select(k):
                    n = u.times(4).plus(k)
                    until(b_rowsr, n)
                    G.tensor_copy(b_sel[:], ident[0:64, bass.ds(u.times(8).plus(2 * k).value, 2)].unsqueeze(2)
                                  .to_broadcast([64, 2, P])).then_inc(b_selr, 1)
                if j == 0:
                    select(0)
                if j == 1:
                    until(b_cbx_out, u.plus(1))
                    G.tensor_tensor(b_bm[:], b_bt[0:TS, 2, :].unsqueeze(1).to_broadcast([TS, NB, P]),
                                    in_batch[:].unsqueeze(2).to_broadcast([TS, NB, P]), ALU.mult).then_inc(b_bmask, 1)
                if j in (2, 4, 6, 8):
                    k = (j - 2) // 2
                    n = u.times(4).plus(k)
                    ch = slice(k * P, (k + 1) * P)
                    until(b_xs_out, u.plus(1))
                    until(b_yst, n.times(2))
                    for b in range(3):
                        w = P if b < 2 else TS
                        m = G.tensor_tensor(b_xw[0:w, b, :].rearrange("p (h e) -> p h e", e=64),
                                            b_xdt[0:w, b, ch].rearrange("p (h e) -> p h e", e=64),
                                            b_end[0:w, uv, b, 2 * k:2 * k + 2].unsqueeze(2).to_broadcast([w, 2, 64]), ALU.mult)
                    m.then_inc(b_xwr, 1)
                    if k < 3:
                        select(k + 1)
                    until(b_s_in, n.plus(1).times(16))
                    until(b_dlog, n.plus(1))
                    dec = b_ea[:].rearrange("p (b l) -> p b l", l=SL)[:, :, SL - 1:SL].to_broadcast([P, NB, P])
                    G.tensor_tensor(b_s[:], b_s[:], dec, ALU.mult).then_inc(b_decayed, 1)
                if j in (3, 5, 7, 9):
                    k = (j - 3) // 2
                    n = u.times(4).plus(k)
                    until(b_sadd, n.plus(1).times(2))
                    pool.dma_start(o["ssm_s"][n.value], b_s[:]).then_inc(b_s_out, 16)
                    until(b_spr, n.plus(1))
                    pool.dma_start(o["ssm_p"][n.value], b_sp[:]).then_inc(b_sp_out, 16)
                    if not (u.base == B_GROUPS - 1 and k == 3):
                        until(b_s_out, n.plus(1).times(16))
                        load_state(n.plus(1))

            def b_group(u, p, mixed):
                if mixed is not None:
                    b_mix(mixed, 1 - p, 0)
                for j in range(10):
                    b_post(u, p, j)
                    if j < 5:
                        b_fill(u, j + 1)
                    if j == 9 and u.base < B_GROUPS - 1:
                        b_fill(u.plus(1), 0)
                    if mixed is not None and j < 9:
                        b_mix(mixed, 1 - p, j + 1)

            pool.dma_start(b_old[:], d["b_old"][0]).then_inc(b_old_in, 16)
            load_state(Count(0))
            b_fill(Count(0), 0)
            b_group(Count(0), 0, None)
            pool.wait_ge(gb_done, 1)
            b_group(Count(1), 1, Count(0))
            with pool.Fori(0, 2) as i:
                for n in range(2):
                    b_group(Count(2 + n, (i, 2)), n, Count(1 + n, (i, 2)))
            b_group(Count(6), 0, Count(5))
            b_group(Count(7), 1, Count(6))
            for j in range(10):
                b_mix(Count(7), 1, j)
            residual(3, Count(3 * KT), (b_glo, Count(4 * B_GROUPS)))
            ffn(1, 3)
            for t in range(4):
                until(y_ready, 4 * (t + 1))
                pool.dma_start(o["y"][:, 4 * t:4 * t + 4, :], x[:, 4 * t:4 * t + 4, :]).then_inc(y_stored, 16)
            pool.wait_ge(y_stored, 64)
            pool.wait_ge(f_new_out, 32)


def kernel(**inputs):
    import concourse.bacc as bacc
    from concourse.bass_utils import run_bass_kernel_spmd

    a = {k: np.asarray(v) for k, v in inputs.items()}

    def chunks(w, kt):
        k, n = w.shape
        w = w.reshape(k // (kt * P), kt, P, n // P, P).transpose(3, 0, 2, 1, 4)
        return w.reshape(-1, P, kt * P)

    def tiles(v, *tail):
        v = v.reshape(v.shape[:-1] + (-1, P))
        v = np.moveaxis(v, (-1, -2), (0, 1))
        return v.reshape(v.shape[:2] + tail) if tail else v

    w = a["a_w_in"][0]
    hk = A_HEADS * A_DK
    q, k, v, og, gates = np.split(w, [hk, 2 * hk, 2 * hk + D_MODEL, 2 * hk + 2 * D_MODEL], axis=1)
    by_head = [z.reshape(D_MODEL, A_HEADS, -1) for z in (q, k, v, og)]
    wa_in = np.concatenate(by_head, axis=2).reshape(D_MODEL, -1)
    wa_gate = np.zeros((D_MODEL, P), np.float32)
    wa_gate[:, 0:8], wa_gate[:, 32:40] = gates[:, :8], gates[:, 8:]
    w = a["b_w_in"][0]
    z, xs, bm, cm, dt = np.split(w, [B_DINNER, 2 * B_DINNER, 2 * B_DINNER + 1024, 2 * B_DINNER + 2048], axis=1)

    def by_group(*parts):
        return np.concatenate([v.reshape(v.shape[:-1] + (B_GROUPS, -1)) for v in parts], axis=-1).reshape(parts[0].shape[:-1] + (-1,))

    def conv_by_group(v):
        xp, bp, cp = np.split(v, [B_DINNER, B_DINNER + 1024], axis=-1)
        return by_group(bp, cp, xp)

    wb_in = by_group(bm, cm, xs, z)
    wb_gate = np.zeros((D_MODEL, P), np.float32)
    wb_gate[:, 0:64] = dt

    def gate_value(v):
        s = v.shape[:-1]
        return np.swapaxes(v.reshape(s + (2, FT, P)), -3, -2).reshape(s + (-1,))

    f_tapb = np.concatenate([a["f_conv_w"], a["f_conv_b"][:, None]], axis=1)
    b_tapb = np.concatenate([a["b_conv_w"][0], a["b_conv_b"]], axis=0)
    x = np.concatenate([a["x_prompt"][0], a["x_sample"].reshape(TS, D_MODEL)], axis=0)
    s_idx, t_idx = np.arange(P)[:, None], np.arange(P)[None, :]
    future = np.zeros((P, SC), np.float32)
    future[:, 0:P] = future[:, TP:TP + P] = np.where(s_idx <= t_idx, 0.0, BIG)
    ss, tt = np.arange(TS)[:, None], np.arange(TS)[None, :]
    future[0:TS, TP + P:SC] = np.where((ss <= tt) & (ss // SL == tt // SL), 0.0, BIG)
    starts = [0] + [TP + SL * b for b in range(NB)]
    seg_keep = np.ones((64, T), np.float32)
    seg_keep[:, starts] = 0.0
    seg_drop = np.zeros((8, T), np.float32)
    seg_drop[:, starts] = -BIG
    ssm = a["state_ssm"][0].reshape(NB, 32, P, P)
    ins = {
        "x": tiles(x).astype(np.float32, copy=False),
        "ident": np.eye(P, dtype=np.float32),
        "mean_mat": np.full((P, P), 1.0 / D_MODEL, np.float32),
        "ones": np.ones((P, P), np.float32),
        "future": future, "seg_keep": seg_keep, "seg_drop": seg_drop,
        "in_batch": (ss // SL == np.arange(NB)[None, :]).astype(np.float32),
        "norm_w": np.moveaxis(tiles(np.concatenate([a["norm_mix"][0:1], a["norm_ffn"][0:1], a["norm_mix"][1:2],
                                                    a["norm_ffn"][1:2], a["norm_final"][None]])), 1, 2),
        "f_conv": np.moveaxis(tiles(gate_value(f_tapb)), 1, 2),
        "b_conv": tiles(conv_by_group(b_tapb)),
        "b_normw": tiles(a["b_norm_w"][0])[:, :, None],
        "b_skip": np.repeat(a["b_D"][0], 64).reshape(32, P).T[:, :, None],
        "b_small": np.stack([a["b_dt_bias"][0], a["b_A_log"][0]], axis=1),
        "a_small": np.concatenate([a["a_b_if"][0].reshape(2, 8).T, a["state_mlstm_m"][0].T], axis=1),
        "a_n": a["state_mlstm_n"][0].transpose(2, 1, 0),
        "a_c": a["state_mlstm_C"][0].transpose(1, 2, 0, 3),
        "f_old": np.stack([tiles(gate_value(s), NB * 2) for s in a["state_ffn_conv"]]),
        "b_old": np.moveaxis(tiles(conv_by_group(a["state_ssm_conv"][0]), NB * 3).reshape(P, B_GROUPS, 6, NB * 3), 1, 0),
        "b_sT": ssm.transpose(1, 3, 0, 2),
        "b_s": ssm.transpose(1, 2, 0, 3),
        "wa_gate": chunks(wa_gate, KT), "wa_in": chunks(wa_in, KT), "wa_out": chunks(a["a_w_out"][0], KT),
        "wb_gate": chunks(wb_gate, KT), "wb_in": chunks(wb_in, KT),
        "wb_out": np.concatenate([
            chunks(np.concatenate([a["b_w_out"][0][g * 512:(g + 1) * 512] for g in pair]), KT // 2)
            .reshape(KT // 2, 2, P, CH // 2).transpose(0, 2, 1, 3).reshape(KT // 2, P, CH) for pair in ((1, 2), (3, 4), (5, 6), (0, 7))]),
    }
    for l in range(2):
        ins[f"wf_up{l}"] = chunks(gate_value(a["f_w_up"][l]), KT)
        ins[f"wf_down{l}"] = np.concatenate([chunks(a["f_w_down"][l][h * FH * P:(h + 1) * FH * P], FH // 2) for h in range(2)])
    ins = {n: np.ascontiguousarray(v) for n, v in ins.items()}
    outs = {"y": (P, KT, T), "C_s": (A_HEADS, P, NB, A_DV), "C_p": (A_HEADS, P, A_DV), "n": (P, A_HEADS, 1 + NB),
            "m": (A_HEADS, 1 + NB), "ssm_s": (32, P, NB, P), "ssm_p": (32, P, P),
            "bconv": (B_GROUPS, P, 6, (1 + NB) * 3), "fconv": (2, P, 2 * FT, (1 + NB) * 2)}
    nc = bacc.Bacc("TRN2", target_bir_lowering=False, num_devices=1, dynamic_dma_scratch_size=8192)
    d = {n: nc.dram_tensor(n + "_in", v.shape, F32, kind="ExternalInput").ap() for n, v in ins.items()}
    o = {n: nc.dram_tensor(n + "_out", s, F32, kind="ExternalOutput").ap() for n, s in outs.items()}
    trunk(nc, d, o)
    r = run_bass_kernel_spmd(nc, [{n + "_in": v for n, v in ins.items()}], core_ids=[0]).results[0]
    r = {n: np.asarray(r[n + "_out"]) for n in outs}

    y = r["y"].transpose(2, 1, 0).reshape(T, D_MODEL)
    C_s = r["C_s"].transpose(2, 0, 1, 3)[None]
    n_all = r["n"].transpose(2, 1, 0)
    m_all = r["m"].T
    ssm_s = r["ssm_s"].transpose(2, 0, 1, 3).reshape(NB, B_HEADS, 64, P)[None]
    ssm_p = r["ssm_p"].reshape(1, 1, B_HEADS, 64, P)
    bc = r["bconv"].reshape(B_GROUPS, P, 6, 1 + NB, 3).transpose(3, 4, 0, 2, 1)
    bc = np.concatenate([bc[:, :, :, 2:6].reshape(1 + NB, 3, -1), bc[:, :, :, 0].reshape(1 + NB, 3, -1),
                         bc[:, :, :, 1].reshape(1 + NB, 3, -1)], axis=-1)
    fc = r["fconv"].reshape(2, P, FT, 2, 1 + NB, 2).transpose(0, 4, 5, 3, 2, 1).reshape(2, 1 + NB, 2, 2 * D_FF)
    out = (y[None, :TP], y[TP:].reshape(NB, SL, D_MODEL), r["C_p"][None, None], C_s,
           n_all[None, 0:1], n_all[None, 1:], m_all[None, 0:1], m_all[None, 1:], ssm_p, ssm_s,
           bc[None, 0:1], bc[None, 1:], fc[:, 0:1], fc[:, 1:])
    return tuple(np.ascontiguousarray(v) for v in out)
```

```python
from contextlib import ExitStack

import numpy as np

import concourse.bass as bass
from concourse import mybir

F32 = mybir.dt.float32
F32R = mybir.dt.float32r
ACT = mybir.ActivationFunctionType
ALU = mybir.AluOpType

P = 128
D_MODEL = 2048
KT = D_MODEL // P
TP, NB, SL = 256, 8, 4
TS = NB * SL
T = TP + TS
A_HEADS, A_DK, A_DV = 8, 128, 256
B_HEADS, B_GROUPS = 64, 8
B_DINNER = 4096
D_FF = 5632
FT = D_FF // P
FH = FT // 2
EPS = 1e-6
BIG = 1e30
CH = 16 * P
DCH = FH // 2 * P
SC = TP + P + TS

C_AIN = 1
C_AOUT = C_AIN + 6 * A_HEADS
C_F0 = C_AOUT + KT
C_FHALF = 2 * FH + 2 * KT
C_BGATE = C_F0 + 2 * C_FHALF
C_BIN = C_BGATE + 1
C_PART = KT // 2
C_BTURN = 20 + C_PART
C_F1 = C_BIN + 80 + 4 * C_PART
C_END = C_F1 + 2 * C_FHALF
N_AOUT = C_AOUT
N_F0 = N_AOUT + 2 * KT
N_FHALF = 2 * FH + KT
N_BIN = N_F0 + 2 * N_FHALF + 1
N_F1 = N_BIN + 80 + 4 * KT
EA_F0 = 1 + 48
EA_BGATE = EA_F0 + 4 * FH
EA_BIN = EA_BGATE + 1
EA_F1 = EA_BIN + 80
ED_F0 = 2 * KT
ED_BIN = ED_F0 + 2 * KT
ED_F1 = ED_BIN + 4 * KT




def b_place(u, p):
    if not u.terms and u.base in (0, B_GROUPS - 1):
        return 0 if u.base == 0 else 12
    return 4 if p == 1 else 8


class Count:

    def __init__(self, base, *terms):
        self.base, self.terms = base, terms

    def plus(self, n):
        return Count(self.base + n, *self.terms)

    def times(self, n):
        return Count(self.base * n, *[(r, s * n) for r, s in self.terms])

    def add(self, reg, step):
        if isinstance(reg, int):
            return Count(self.base + reg * step, *self.terms)
        return Count(self.base, *self.terms, (reg, step))

    def half(self):
        return Count(self.base // 2, *[(r, s // 2) for r, s in self.terms])

    @property
    def value(self):
        v = self.base
        for r, s in self.terms:
            v = r * s + v
        return v


def wait(eng, sem, count):
    if isinstance(count, int):
        count = Count(count)
    if count.base <= 0:
        return
    eng.wait_ge(sem, count.value)


class Own:

    def __init__(self, eng, sem):
        self.eng, self.sem, self.n = eng, sem, 0

    def mark(self, ins):
        ins.then_inc(self.sem, 1)
        self.n += 1

    def sync(self):
        wait(self.eng, self.sem, self.n)

    def link(self, ins):
        self.mark(ins)
        self.sync()


def trunk(nc, d, o):
    with ExitStack() as ctx:
        def sb(name, shape, dt=F32, stack=ctx):
            return stack.enter_context(nc.sbuf_tensor(name, shape, dt))

        def sem(name):
            return ctx.enter_context(nc.semaphore(name))

        x = sb("x", [P, KT, T])
        hn_hi = sb("hn_hi", [P, KT, T], F32R)
        hn_lo = sb("hn_lo", [P, KT, T], F32R)
        w_raw = sb("w_raw", [P, 2, CH])
        w_hi = sb("w_hi", [P, 2, CH], F32R)
        w_lo = sb("w_lo", [P, 2, CH], F32R)
        ident = sb("ident", [P, P])
        mean_mat = sb("mean_mat", [P, P])
        future = sb("future", [P, SC])
        seg_keep = sb("seg_keep", [64, T])
        in_batch = sb("in_batch", [3 * TS, NB])
        head_ident = sb("head_ident", [P, 64])
        norm_w = sb("norm_w", [P, 5, KT])
        f_conv = sb("f_conv", [P, 2, 2 * FT, 4])
        b_conv = sb("b_conv", [P, 48, 5])
        b_normw = sb("b_normw", [P, 32, 1])
        b_skip = sb("b_skip", [P, 32, 1])
        b_small = sb("b_small", [64, 2])
        rstd = sb("rstd", [P, T])
        sumsq = sb("sumsq", [P, T])
        work = sb("work", [P, 2, T])

        with ExitStack() as st:
            ones = sb("ones", [P, P], F32, st)
            seg_drop = sb("seg_drop", [8, T], F32, st)
            a_small = sb("a_small", [8, 2 + NB], F32, st)
            a_out_hi = sb("a_out_hi", [P, KT, T], F32R, st)
            a_out_lo = sb("a_out_lo", [P, KT, T], F32R, st)
            a_io = sb("a_io", [P, 2, 6, T], F32, st)
            a_c = sb("a_c", [P, 2, NB, A_DV], F32, st)
            a_cp = sb("a_cp", [P, A_DV], F32, st)
            a_n = sb("a_n", [P, A_HEADS, NB], F32, st)
            a_nnew = sb("a_nnew", [P, A_HEADS, 1 + NB], F32, st)
            a_mnew = sb("a_mnew", [8, 1 + NB], F32, st)
            a_rows = sb("a_rows", [8, 9, T], F32, st)
            a_acol = sb("a_acol", [P, 8, 3], F32, st)
            a_wcol = sb("a_wcol", [P, 8, 3], F32, st)
            a_sel = sb("a_sel", [8, P], F32, st)
            a_dec = sb("a_dec", [P, SC], F32, st)
            a_prob = sb("a_prob", [P, SC], F32, st)
            a_kw = sb("a_kw", [P, 3, P], F32, st)
            a_vt = sb("a_vt", [P, 3, A_DV], F32, st)
            a_k3 = sb("a_k3", [3 * TS, P], F32R, st)
            a_v3 = sb("a_v3", [3 * TS, A_DV], F32R, st)
            a_vm = sb("a_vm", [3 * TS, NB, A_DV], F32R, st)
            a_wi = sb("a_wi", [P, TS], F32, st)
            a_qs = sb("a_qs", [P, TS], F32, st)
            a_nq = sb("a_nq", [P, TS], F32, st)
        FP = 2 + TP + NB * (2 + SL)
        with ExitStack() as st:
            act_hi = sb("act_hi", [P, FH, T], F32R, st)
            act_lo = sb("act_lo", [P, FH, T], F32R, st)
            f_old = sb("f_old", [P, 2 * FT, NB * 2], F32, st)
            f_new = sb("f_new", [P, 2 * FT, (1 + NB) * 2], F32, st)
            f_pad = sb("f_pad", [P, 4, FP], F32, st)
            f_u = sb("f_u", [P, 4, FP], F32, st)
            f_act = sb("f_act", [P, 2, T], F32, st)
        BP = 3 + TP + NB * (3 + SL)
        with ExitStack() as st:
            b_out_hi = sb("b_out_hi", [P, KT, T], F32R, st)
            b_out_lo = sb("b_out_lo", [P, KT, T], F32R, st)
            b_io = sb("b_io", [P, 2, 10, T], F32, st)
            b_sT = sb("b_sT", [P, NB, P], F32, st)
            b_s = sb("b_s", [P, NB, P], F32, st)
            b_sp = sb("b_sp", [P, P], F32, st)
            b_old = sb("b_old", [P, 6, NB * 3], F32, st)
            b_new = sb("b_new", [P, 6, (1 + NB) * 3], F32, st)
            b_pad = sb("b_pad", [P, 2, BP], F32, st)
            b_u = sb("b_u", [P, BP], F32, st)
            b_yi = sb("b_yi", [P, TS], F32, st)
            b_rows = sb("b_rows", [64, 3, T], F32, st)
            b_nac2 = sb("b_nac2", [P, T], F32R, st)
            b_rsum = sb("b_rsum", [64, TS + 1], F32, st)
            b_nac = sb("b_nac", [P, B_GROUPS, 3, 8], F32, st)
            b_dtc = sb("b_dtc", [P, B_GROUPS, 3, 8], F32, st)
            b_end = sb("b_end", [P, B_GROUPS, 3, 8], F32, st)
            b_sel = sb("b_sel", [P, 2, P], F32R, st)
            b_cb = sb("b_cb", [P, SC], F32, st)
            b_dec = sb("b_dec", [P, 2, SC], F32, st)
            b_bt = sb("b_bt", [P, 3, P], F32, st)
            b_x3 = sb("b_x3", [3 * TS, P], F32R, st)
            b_b3 = sb("b_b3", [3 * TS, P], F32R, st)
            b_bm = sb("b_bm", [3 * TS, NB, P], F32R, st)
            b_xdt = sb("b_xdt", [P, 3, 4 * P], F32, st)
            b_xw = sb("b_xw", [P, 3, P], F32, st)
            b_ea = sb("b_ea", [P, TS], F32, st)

        a_h, a_em, b_r = work, sumsq, sumsq
        b_tmp = b_xdt[0:64, 0:2, 0:T]
        b_th = work[:, :, :].rearrange("p a t -> p (a t)")[:, 0:BP]

        ps = ctx.enter_context(nc.psum_tensor("ps", [P, 8, 512], F32))
        M0, M1, M2, M3 = 4, 5, 6, 7

        raw_landed = [sem("raw_landed0"), sem("raw_landed1")]
        w_high, w_low, chunk_done, proj_taken, res_added = map(sem, (
            "w_high", "w_low", "chunk_done", "proj_taken", "res_added"))
        consts_in, norm_w_in, y_ready, y_stored = map(sem, (
            "consts_in", "norm_w_in", "y_ready", "y_stored"))
        x_in = [sem(f"x_in{n}") for n in range(4)]
        act_own, dve_own, pool_own, pool_passed, pe_passed = map(sem, (
            "act_own", "dve_own", "pool_own", "pool_passed", "pe_passed"))
        squared, sq_added, mean_ready, var_ready, root_ready = map(sem, (
            "squared", "sq_added", "mean_ready", "var_ready", "root_ready"))
        hn_hi_ready, hn_lo_ready, rstd_ready = map(sem, (
            "hn_hi_ready", "hn_lo_ready", "rstd_ready"))
        a_n_in, ga_exp, ga_onep, ga_ln, ga_logs, ga_rows, ga_turned, ga_done = map(sem, (
            "a_n_in", "ga_exp", "ga_onep", "ga_ln", "ga_logs", "ga_rows", "ga_turned", "ga_done"))
        a_sel_ready, a_scores, a_kv0, a_dlog, a_dexp, a_kv0_tok, a_probs, a_v1, a_v1_tok, a_vmask = map(sem, (
            "a_sel_ready", "a_scores", "a_kv0", "a_dlog", "a_dexp", "a_kv0_tok", "a_probs", "a_v1", "a_v1_tok",
            "a_vmask"))
        a_num, a_htmp, a_hhi, a_hlo, a_cupd, a_cadd, a_cp_ready = map(sem, (
            "a_num", "a_htmp", "a_hhi", "a_hlo", "a_cupd", "a_cadd", "a_cp_ready"))
        a_c_in, a_c_out = [sem("a_c_in0"), sem("a_c_in1")], [sem("a_c_out0"), sem("a_c_out1")]
        a_cp_out, a_nm_out, a_steps, a_otanh, a_klow = map(sem, (
            "a_cp_out", "a_nm_out", "a_steps", "a_otanh", "a_klow"))
        f_old_in, f_prefix, f_tap0, f_tap1, f_conved, f_gated, f_silu, f_prod, f_ahi, f_alo, f_kept, f_new_out = map(sem, (
            "f_old_in", "f_prefix", "f_tap0", "f_tap1", "f_conved", "f_gated", "f_silu", "f_prod", "f_ahi", "f_alo",
            "f_kept", "f_new_out"))
        gb_exp, gb_onep, gb_ln, gb_logs, gb_rows, gb_turned, gb_done, gb_high, gb_low = map(sem, (
            "gb_exp", "gb_onep", "gb_ln", "gb_logs", "gb_rows", "gb_turned", "gb_done", "gb_high", "gb_low"))
        b_old_in, b_prefix, b_tap0, b_taps, b_conved, b_tanh, b_silu, b_kept, b_new_out, b_ztanh, b_zready = map(sem, (
            "b_old_in", "b_prefix", "b_tap0", "b_taps", "b_conved", "b_tanh", "b_silu", "b_kept", "b_new_out",
            "b_ztanh", "b_zready"))
        b_cbx, b_cbx_out, b_xt_out, b_xs, b_xs_out, b_bmask, b_selr, b_rowsr, b_dlog, b_dexp, b_wts, b_xwr = map(sem, (
            "b_cbx", "b_cbx_out", "b_xt_out", "b_xs", "b_xs_out", "b_bmask", "b_selr", "b_rowsr", "b_dlog", "b_dexp",
            "b_wts", "b_xwr"))
        b_yst, b_decayed, b_sadd, b_spr, b_yg, b_gsq, b_gms, b_gvar, b_groot, b_gn, b_ghi, b_glo = map(sem, (
            "b_yst", "b_decayed", "b_sadd", "b_spr", "b_yg", "b_gsq", "b_gms", "b_gvar", "b_groot", "b_gn", "b_ghi",
            "b_glo"))
        b_s_in, b_sT_in, b_s_out, b_sp_out, b_steps, b_xhigh, b_xlow, b_blow = map(sem, (
            "b_s_in", "b_sT_in", "b_s_out", "b_sp_out", "b_steps", "b_xhigh", "b_xlow", "b_blow"))

        def packed(ap):
            return ap[:, TP:T].rearrange("p (b l) -> p b l", l=SL)

        def f_samples(ap):
            return ap[:, TP + 2:FP].rearrange("p (b l) -> p b l", l=SL + 2)

        def b_samples(ap):
            return ap[:, TP + 3:BP].rearrange("p (b l) -> p b l", l=SL + 3)

        CONSTS = [(ident, "ident"), (mean_mat, "mean_mat"), (ones, "ones"), (future, "future"), (seg_keep, "seg_keep"),
                  (seg_drop, "seg_drop"), (in_batch, "in_batch"), (head_ident, "head_ident"), (f_conv, "f_conv"),
                  (b_conv, "b_conv"), (b_normw, "b_normw"), (b_skip, "b_skip"), (b_small, "b_small"),
                  (a_small, "a_small")]
        N_CONSTS = 16 * len(CONSTS)

        block = ctx.enter_context(nc.Block())

        @block.sync
        def _(sp):
            def load(c, src, cols):
                wait(sp, w_low, c.plus(-1))
                sp.dma_start(w_raw[:, c.base % 2, 0:cols], src).then_inc(raw_landed[c.base % 2], 16)

            sp.dma_start(norm_w[:], d["norm_w"]).then_inc(norm_w_in, 16)
            load(Count(0), d["wa_gate"][0], CH)
            for n in range(4):
                sp.dma_start(x[:, 4 * n:4 * n + 4, :], d["x"][:, 4 * n:4 * n + 4, :]).then_inc(x_in[n], 16)
            load(Count(1), d["wa_in"][0], CH)
            for tile, name in CONSTS:
                sp.dma_start(tile[:], d[name]).then_inc(consts_in, 16)
            sp.dma_start(a_n[:], d["a_n"]).then_inc(a_n_in, 16)
            load(Count(2), d["wa_in"][1], CH)
            with sp.Fori(0, 23) as i:
                for j in range(2):
                    load(Count(C_AIN + 2 + j, (i, 2)), d["wa_in"][i * 2 + (2 + j)], CH)
            with sp.Fori(0, 8) as i:
                for j in range(2):
                    load(Count(C_AOUT + j, (i, 2)), d["wa_out"][i * 2 + j], CH)

            def ffn(c0, up, down):
                with sp.Fori(0, 2) as h:
                    with sp.Fori(0, FH) as i:
                        for j in range(2):
                            load(Count(c0 + j, (h, C_FHALF), (i, 2)), up[h * (2 * FH) + i * 2 + j], CH)
                    with sp.Fori(0, KT) as i:
                        for j in range(2):
                            load(Count(c0 + 2 * FH + j, (h, C_FHALF), (i, 2)), down[h * (2 * KT) + i * 2 + j], DCH)

            ffn(C_F0, d["wf_up0"], d["wf_down0"])
            load(Count(C_BGATE), d["wb_gate"][0], CH)

            def b_in(u, c):
                with sp.Fori(0, 5) as i:
                    for j in range(2):
                        load(c.plus(j).add(i, 2), d["wb_in"][u.times(10).plus(j).add(i, 2).value], CH)

            def b_out(part, c):
                with sp.Fori(0, C_PART // 2) as i:
                    for j in range(2):
                        load(c.plus(j).add(i, 2), d["wb_out"][part.times(C_PART).plus(j).add(i, 2).value], CH)

            b_in(Count(0), Count(C_BIN))
            b_in(Count(1), Count(C_BIN + 10))
            with sp.Fori(0, 2) as i:
                for n in range(2):
                    b_in(Count(2 + n, (i, 2)), Count(C_BIN + 20 + 10 * n, (i, C_BTURN)))
                b_out(Count(0, (i, 1)), Count(C_BIN + 40, (i, C_BTURN)))
            b_in(Count(6), Count(C_BIN + 76))
            b_in(Count(7), Count(C_BIN + 86))
            b_out(Count(2), Count(C_BIN + 96))
            b_out(Count(3), Count(C_BIN + 104))
            ffn(C_F1, d["wf_up1"], d["wf_down1"])

        @block.tensor
        def _(pe):
            def gemm(c, bank, hi, lo, tiles, first=True, last=True, each=None, at=0, done=True):
                wait(pe, w_low, c.plus(1))
                s, out = c.base % 2, ps[:, bank, 0:T]
                for k, t in enumerate(tiles):
                    if each is not None:
                        each(k)
                    col = slice((at + k) * P, (at + k + 1) * P)
                    end = last and k == len(tiles) - 1
                    nc.tensor.matmul(out, w_hi[:, s, col], hi[:, t, :], start=first and k == 0, stop=False)
                    nc.tensor.matmul(out, w_hi[:, s, col], lo[:, t, :], start=False, stop=False)
                    m = nc.tensor.matmul(out, w_lo[:, s, col], hi[:, t, :], start=False, stop=end)
                if done:
                    m.then_inc(chunk_done, 1)

            def mm(out, lhs, rhs, start=True, stop=True):
                return nc.tensor.matmul(out, lhs, rhs, start=start, stop=stop, skip_group_check=True)

            def project(c, taken, bank):
                wait(pe, proj_taken, taken)
                gemm(c, bank, hn_hi, hn_lo, range(KT))

            def norm(k):
                wait(pe, sq_added, KT * (k + 1))
                mm(ps[:, M0, 0:T], mean_mat[:], sumsq[:]).then_inc(mean_ready, 1)

            def first_project(c, bank, k):
                gemm(c, bank, hn_hi, hn_lo, range(KT), each=lambda t: wait(pe, hn_lo_ready, k * KT + t + 1))

            def score_blocks(bank, keys, queries):
                mm(ps[:, bank, 0:TP], keys[:, 0:P], queries[:, 0:TP])
                mm(ps[:, bank, TP:TP + P], keys[:, P:TP], queries[:, P:TP])
                return mm(ps[0:TS, bank, TP + P:SC], keys[:, TP:T], queries[:, TP:T])

            def turn(out, src):
                return nc.tensor.transpose(out, src, ident[:])

            def turn_blocks(bank, src):
                turn(ps[:, bank, 0:P], src[:, 0:P])
                turn(ps[:, bank, P:2 * P], src[:, P:TP])
                return turn(ps[0:TS, bank, 2 * P:3 * P], src[:, TP:T])

            first_project(Count(0), 0, 0)
            def a_mix(u, p, j):
                q, k, v0, v1 = (a_io[:, p, n, :] for n in range(4))
                if j == 0:
                    wait(pe, a_sel_ready, u.plus(1))
                    wait(pe, proj_taken, u.times(6).plus(1 + 4))
                    wait(pe, a_cadd, u.times(4))
                    wait(pe, a_cp_ready, u)
                    score_blocks(M0, k, q)
                    mm(ps[:, M1, 0:T], a_sel[:], a_rows[:, 5, :])
                    mm(ps[:, M1, T:T + TS], a_sel[:], a_rows[:, 8, TP:T]).then_inc(a_scores, 1)
                    turn_blocks(M2, k)
                    turn_blocks(M3, v0).then_inc(a_kv0, 1)
                if j == 1:
                    wait(pe, a_kv0_tok, u.plus(1))
                    turn_blocks(M2, v1)
                    mm(ps[:, M3, 0:T], a_sel[:], a_rows[:, 7, :]).then_inc(a_v1, 1)
                if j == 2:
                    wait(pe, a_probs, u.plus(1))
                    wait(pe, a_v1_tok, u.plus(1))
                    wait(pe, a_c_in[p], u.half().plus(1).times(16))
                    for e in range(2):
                        ec = slice(e * P, (e + 1) * P)
                        mm(ps[:, M0 + e, 0:TP], a_vt[:, 0, ec], a_prob[:, 0:TP], True, False)
                        mm(ps[:, M0 + e, P:TP], a_vt[:, 1, ec], a_prob[:, TP:TP + P], False, False)
                        mm(ps[:, M0 + e, TP:T], a_vt[0:TS, 2, ec], a_prob[0:TS, TP + P:SC], False, False)
                        for b in range(NB):
                            t = slice(TP + SL * b, TP + SL * (b + 1))
                            mm(ps[:, M0 + e, t], a_c[:, p, b, ec], a_qs[:, SL * b:SL * (b + 1)], False, True)
                    mm(ps[:, M2, 0:TP], ones[:], a_prob[:, 0:TP], True, False)
                    mm(ps[:, M2, P:TP], ones[:], a_prob[:, TP:TP + P], False, False)
                    mm(ps[:, M2, TP:T], ones[0:TS, :], a_prob[0:TS, TP + P:SC], False, False)
                    mm(ps[:, M2, TP:T], ones[:], a_nq[:], False, True).then_inc(a_num, 1)
                if j == 3:
                    wait(pe, a_htmp, u.plus(1).times(2))
                    wait(pe, a_vmask, u.plus(1))
                    mm(ps[:, M3, 0:A_DV], a_kw[:, 0, :], a_vt[:, 0, :], True, False)
                    mm(ps[:, M3, 0:A_DV], a_kw[:, 1, :], a_vt[:, 1, :], False, True)
                    mm(ps[:, M3, A_DV:A_DV + 1], a_kw[:, 0, :], ones[:, 0:1], True, False)
                    mm(ps[:, M3, A_DV:A_DV + 1], a_kw[:, 1, :], ones[:, 0:1], False, True)
                    mm(ps[:, M3, A_DV + 1:A_DV + 1 + NB], a_kw[0:TS, 2, :], in_batch[0:TS, :])
                    for n in range(3):
                        mm(ps[:, M0 + n, :], a_k3[:], a_vm[:, 2 * n:2 * n + 2, :]).then_inc(a_cupd, 1)
                if j == 4:
                    wait(pe, a_cadd, u.times(4).plus(1))
                    mm(ps[:, M0, :], a_k3[:], a_vm[:, 6:8, :]).then_inc(a_cupd, 1)

            def a_head(u, p, mixed):
                c = u.times(6)
                for j in range(6):
                    cj = c.plus(C_AIN + j)
                    project(cj, c.plus(1 + j - 3), cj.base % 4)
                    if mixed is None and j == 1:
                        pe.wait_ge(consts_in, N_CONSTS)
                        norm(0)
                    if mixed is not None:
                        a_mix(mixed, 1 - p, j)

            a_head(Count(0), 0, None)
            pe.wait_ge(ga_rows, 1)
            for n, row in enumerate((4, 6)):
                for b in range(3):
                    w = P if b < 2 else TS
                    m = nc.tensor.transpose(ps[0:w, M1, 24 * n + 8 * b:24 * n + 8 * b + 8],
                                            a_rows[:, row, b * P:b * P + w], ident[0:8, 0:8])
            m.then_inc(ga_turned, 1)
            pe.wait_ge(ga_done, 1)
            a_head(Count(1), 1, Count(0))
            with pe.Fori(0, 3) as i:
                for n in range(2):
                    a_head(Count(2 + n, (i, 2)), n, Count(1 + n, (i, 2)))

            def out_chunk(c, n0, m, added, hi, lo, tiles, ready=None, ready_at=None):
                for e in range(2):
                    wait(pe, res_added, added.plus(e - 3))
                    gemm(c, (n0 + 2 * m + e) % 4, hi, lo, tiles, at=8 * e, done=e == 1,
                         each=(lambda k: wait(pe, ready, ready_at[k])) if ready is not None and e == 0 else None)

            def out_part(c, n0, added, hi, lo, tiles, ready, ready_at):
                with pe.Fori(0, C_PART // 2) as i:
                    for m in range(2):
                        out_chunk(c.plus(m).add(i, 2), n0, m, added.plus(2 * m).add(i, 4), hi, lo, tiles,
                                  ready if m == 0 else None, ready_at)

            for j in range(C_PART):
                out_chunk(Count(C_AOUT + j), N_AOUT, j, Count(2 * j), a_out_hi, a_out_lo, range(8),
                          a_hlo if j == 0 else None, range(1, 9))
                if j < 6:
                    a_mix(Count(7), 1, j)
            out_part(Count(C_AOUT + C_PART), N_AOUT, Count(KT), a_out_hi, a_out_lo, range(8, KT), a_hlo, range(9, KT + 1))

            def ffn(layer, c0, n0, ea0, ed0, k):
                norm(k)
                with pe.Fori(0, 2) as h:
                    with pe.Fori(0, FH // 2) as i:
                        for j in range(4):
                            wait(pe, proj_taken, Count(ea0 + j - 3, (h, 2 * FH), (i, 4)))
                            if j == 0:
                                gemm(Count(c0 + j, (h, C_FHALF), (i, 4)), (n0 + j) % 4, hn_hi, hn_lo, range(KT),
                                     each=lambda t: wait(pe, hn_lo_ready, k * KT + t + 1))
                            else:
                                gemm(Count(c0 + j, (h, C_FHALF), (i, 4)), (n0 + j) % 4, hn_hi, hn_lo, range(KT))
                    wait(pe, f_alo, Count(layer * FT + FH // 2, (h, FH)))
                    pe.sem_inc(pe_passed, 1)
                    with pe.Fori(0, KT // 4) as i:
                        for j in range(4):
                            wait(pe, res_added, Count(ed0 + j - 3, (h, KT), (i, 4)))
                            for q in range(2):
                                if j == 0 and q == 1:
                                    wait(pe, f_alo, Count(layer * FT + FH, (h, FH)))
                                gemm(Count(c0 + 2 * FH + 2 * j + q, (h, C_FHALF), (i, 8)), (n0 + 2 * FH + j) % 4,
                                     act_hi, act_lo, range(q * FH // 2, (q + 1) * FH // 2), q == 0, q == 1)

            ffn(0, C_F0, N_F0, EA_F0, ED_F0, 1)
            first_project(Count(C_BGATE), (N_BIN - 1) % 4, 2)
            norm(2)

            def gate_columns_b():
                pe.wait_ge(gb_rows, 1)
                for n, row in enumerate((0, 1, 2)):
                    for b in range(3):
                        w = P if b < 2 else TS
                        m = nc.tensor.transpose(ps[0:w, M1 if n < 2 else M2, 192 * (n % 2) + 64 * b:192 * (n % 2) + 64 * b + 64],
                                                b_rows[:, row, b * P:b * P + w], ident[0:64, 0:64])
                m.then_inc(gb_turned, 1)

            def b_mix(u, p, j):
                bT, cT = b_io[:, p, 0, :], b_io[:, p, 1, :]
                if j == 0:
                    wait(pe, b_silu, u.plus(1).times(6))
                    wait(pe, b_gvar, u)
                    wait(pe, b_sadd, u.times(8))
                    wait(pe, b_spr, u.times(4))
                    score_blocks(M0, bT, cT)
                    turn_blocks(M1, bT)
                    for k in range(4):
                        turn(ps[:, M2, k * P:(k + 1) * P], b_io[:, p, 2 + k, 0:P])
                        m = turn(ps[:, M3, k * P:(k + 1) * P], b_io[:, p, 2 + k, P:TP])
                    m.then_inc(b_cbx, 1)
                if j in (1, 3, 5, 7):
                    k = (j - 1) // 2
                    if j == 1:
                        wait(pe, b_xt_out, u.plus(1))
                        for n in range(4):
                            m = turn(ps[0:TS, M2, n * P:(n + 1) * P], b_io[:, p, 2 + n, TP:T])
                        m.then_inc(b_xs, 1)
                        wait(pe, b_cbx_out, u.plus(1))
                    else:
                        wait(pe, b_sadd, u.times(8).plus(2 * k))
                    wait(pe, b_selr, u.times(4).plus(k + 1))
                    mm(ps[:, M0, 0:T], b_sel[:, 0, :], b_nac2[:])
                    mm(ps[:, M1, 0:T], b_sel[:, 1, :], b_nac2[:])
                    one_head = b_sel[0:64, :, :].bitcast(F32)
                    mm(ps[0:64, M1, T:T + TS], one_head[:, 0, 0:64], b_rsum[:, 0:TS])
                    mm(ps[64:P, M1, T:T + TS], one_head[:, 1, 0:64], b_rsum[:, 0:TS]).then_inc(b_rowsr, 1)
                if j in (2, 4, 6, 8):
                    k = (j - 2) // 2
                    ch = slice(k * P, (k + 1) * P)
                    wait(pe, b_wts, u.times(4).plus(k + 1))
                    wait(pe, b_xs_out, u.plus(1))
                    wait(pe, b_yg, u.times(4).plus(k))
                    wait(pe, b_sT_in, u.times(4).plus(k + 1).times(16))
                    for b in range(NB):
                        mm(ps[:, M2, T + SL * b:T + SL * (b + 1)], b_sT[:, b, :], cT[:, TP + SL * b:TP + SL * (b + 1)])
                    for e in range(2):
                        rows, hc = slice(64 * e, 64 * (e + 1)), slice(k * P + 64 * e, k * P + 64 * (e + 1))
                        mm(ps[rows, M2, 0:TP], b_xdt[:, 0, hc], b_dec[:, e, 0:TP], True, False)
                        mm(ps[rows, M2, P:TP], b_xdt[:, 1, hc], b_dec[:, e, TP:TP + P], False, False)
                        m = mm(ps[rows, M2, TP:T], b_xdt[0:TS, 2, hc], b_dec[0:TS, e, TP + P:SC], False, True)
                    m.then_inc(b_yst, 1)
                    wait(pe, b_xlow, u.times(4).plus(k + 1))
                    wait(pe, b_bmask, u.plus(1))
                    wait(pe, b_spr, u.times(4).plus(k))
                    for half in range(2):
                        mm(ps[:, M0 + half, :], b_x3[:], b_bm[:, 4 * half:4 * half + 4, :])
                    mm(ps[:, M3, 0:P], b_xw[:, 0, :], b_bt[:, 0, :], True, False)
                    mm(ps[:, M3, 0:P], b_xw[:, 1, :], b_bt[:, 1, :], False, True).then_inc(b_yst, 1)
                if j == 9:
                    wait(pe, b_gsq, u.plus(1).times(4))
                    wait(pe, b_yg, u.plus(1).times(4))
                    for k in range(4):
                        m = mm(ps[:, M2, 0:T], mean_mat[:], b_io[:, p, 2 + k, :], k == 0, k == 3)
                    m.then_inc(b_gms, 1)

            def b_group(u, p, c, mixed):
                for j in range(10):
                    wait(pe, proj_taken, u.times(10).plus(EA_BIN + j - 3))
                    gemm(c.plus(j), (N_BIN + 10 * p + j) % 4, hn_hi, hn_lo, range(KT))
                    if mixed is not None:
                        b_mix(mixed, 1 - p, j)
                    elif j == 9:
                        gate_columns_b()
                if mixed is None:
                    pe.wait_ge(gb_done, 1)
                    pe.wait_ge(gb_low, 1)

            b_out = b_out_hi, b_out_lo
            b_group(Count(0), 0, Count(C_BIN), None)
            b_group(Count(1), 1, Count(C_BIN + 10), Count(0))
            with pe.Fori(0, 2) as i:
                for n in range(2):
                    b_group(Count(2 + n, (i, 2)), n, Count(C_BIN + 20 + 10 * n, (i, C_BTURN)), Count(1 + n, (i, 2)))
                out_part(Count(C_BIN + 40, (i, C_BTURN)), N_BIN, Count(ED_BIN, (i, KT)), *b_out, range(4, 12), b_glo,
                         [Count(4 + k + 1, (i, 8)) for k in range(8)])
            b_group(Count(6), 0, Count(C_BIN + 76), Count(5))
            b_group(Count(7), 1, Count(C_BIN + 86), Count(6))
            for j in range(10):
                if j < C_PART:
                    out_chunk(Count(C_BIN + 96 + j), N_BIN, j, Count(ED_BIN + 2 * KT + 2 * j), *b_out, range(4, 12),
                              b_glo if j == 0 else None, range(21, 29))
                b_mix(Count(7), 1, j)
            out_part(Count(C_BIN + 104), N_BIN, Count(ED_BIN + 3 * KT), *b_out, [0, 1, 2, 3, 12, 13, 14, 15], b_glo,
                     [28 + max(k - 3, 0) for k in range(8)])
            ffn(1, C_F1, N_F1, EA_F1, ED_F1, 3)
            norm(4)

        @block.scalar
        def _(act):
            own = Own(act, act_own)
            A = nc.scalar.activation

            def split(c, cols=CH):
                wait(act, raw_landed[c.base % 2], c.half().plus(1).times(16))
                wait(act, chunk_done, c.plus(-1))
                A(w_hi[:, c.base % 2, 0:cols], w_raw[:, c.base % 2, 0:cols], ACT.Copy).then_inc(w_high, 1)

            def norm(k):
                wait(act, var_ready, k + 1)
                A(rstd[:], rstd[:], ACT.Sqrt).then_inc(root_ready, 1)

            def input_high(k, t):
                A(hn_hi[:, t, :], x[:, t, :], ACT.Copy, scale=norm_w[:, k, t:t + 1] if isinstance(t, int)
                  else norm_w[:, k, bass.ds(t, 1)]).then_inc(hn_hi_ready, 1)

            def new_tile(buf, t, added, sq, k):
                wait(act, res_added, added)
                wait(act, sq_added, sq.plus(-1))
                A(work[:, buf, :], x[:, t.value, :], ACT.Square).then_inc(squared, 1)
                if k is not None:
                    input_high(k, t.value)

            def down(c0, tiles_done, sq0, last=False, k=None):
                def pair(i, tail):
                    for j in range(2):
                        for q in range(2):
                            ahead = tail and j == 1
                            if not (ahead and last):
                                split(c0.plus(j * 2 + q + 2).add(i, 4), CH if ahead else DCH)
                        if sq0 is not None:
                            new_tile(j, Count(j).add(i, 2), tiles_done.plus(j + 1).add(i, 2), sq0.plus(j).add(i, 2), k)
                with act.Fori(0, KT // 2 - 1) as i:
                    pair(i, False)
                pair(KT // 2 - 1, True)

            def out_part(c, added=None, sq=None, k=None):
                with act.Fori(0, C_PART // 2) as i:
                    for m in range(2):
                        split(c.plus(m + 2).add(i, 2))
                        for e in range(2):
                            if k is not None:
                                t = Count(2 * m + e, (i, 4))
                                new_tile(e, t, t.plus(added + 1), t.plus(sq), k)

            split(Count(0))
            act.wait_ge(norm_w_in, 16)
            for t in range(KT):
                act.wait_ge(x_in[t // 4], 16)
                input_high(0, t)
            split(Count(1))
            for t in range(KT):
                wait(act, sq_added, t - 1)
                A(work[:, t % 2, :], x[:, t, :], ACT.Square).then_inc(squared, 1)
                if t == KT // 2:
                    split(Count(2))
            act.wait_ge(consts_in, N_CONSTS)

            def gates(j):
                if j == 0:
                    act.wait_ge(proj_taken, 1)
                    A(a_rows[:, 0, :], a_rows[:, 0, :], ACT.Identity, bias=a_small[:, 0:1])
                    own.link(A(a_rows[:, 1, :], a_rows[:, 1, :], ACT.Identity, bias=a_small[:, 1:2]))
                    own.link(A(a_rows[:, 2, :], a_rows[:, 1, :], ACT.Abs))
                    A(a_rows[:, 3, :], a_rows[:, 2, :], ACT.Exp, scale=-1.0).then_inc(ga_exp, 1)
                if j == 1:
                    act.wait_ge(ga_onep, 1)
                    A(a_rows[:, 4, :], a_rows[:, 2, :], ACT.Ln).then_inc(ga_ln, 1)
                if j == 4:
                    act.wait_ge(ga_logs, 1)
                    A(a_rows[:, 6, :], a_rows[:, 6, :], ACT.Exp)
                    A(a_rows[:, 8, TP:T], a_rows[:, 8, TP:T], ACT.Exp).then_inc(ga_rows, 1)

            def gate_columns():
                act.wait_ge(ga_turned, 1)
                cols = ps[:, M1, 0:48].rearrange("p (n b h) -> p n h b", n=2, b=3)
                A(a_acol[:, :, 0:2], cols[:, 0, :, 0:2], ACT.Copy)
                A(a_wcol[:, :, 0:2], cols[:, 1, :, 0:2], ACT.Copy)
                A(a_acol[0:TS, :, 2], cols[0:TS, 0, :, 2], ACT.Copy)
                A(a_wcol[0:TS, :, 2], cols[0:TS, 1, :, 2], ACT.Copy).then_inc(ga_done, 1)
                act.wait_ge(ga_done, 1)

            def a_post(u, p, j):
                if j >= 4:
                    wait(act, proj_taken, u.times(6).plus(1 + j + 1))
                    A(a_io[:, p, j, :], a_io[:, p, j, :], ACT.Tanh, scale=0.5).then_inc(a_otanh, 1)

            def a_mix(u, p, j):
                h = u.value
                if j == 1:
                    wait(act, a_kv0, u.plus(1))
                    wait(act, a_cupd, u.times(4))
                    wait(act, a_vmask, u)
                    for b in range(2):
                        A(a_kw[:, b, :], ps[:, M2, b * P:(b + 1) * P], ACT.Copy, scale=a_wcol[:, h, b:b + 1])
                    A(a_kw[0:TS, 2, :], ps[0:TS, M2, 2 * P:3 * P], ACT.Copy, scale=a_wcol[0:TS, h, 2:3])
                    for n in range(2):
                        A(a_k3[n * TS:(n + 1) * TS, :], ps[0:TS, M2, 2 * P:3 * P], ACT.Copy, scale=a_wcol[0:TS, h, 2:3])
                    for n in (0, 2):
                        A(a_v3[n * TS:(n + 1) * TS, 0:P], ps[0:TS, M3, 2 * P:3 * P], ACT.Copy)
                    A(a_vt[:, 0:2, 0:P], ps[:, M3, 0:2 * P].rearrange("p (b e) -> p b e", b=2), ACT.Copy)
                    A(a_vt[0:TS, 2, 0:P], ps[0:TS, M3, 2 * P:3 * P], ACT.Copy).then_inc(a_kv0_tok, 1)
                    wait(act, a_dlog, u.plus(1))
                    A(a_dec[:], a_dec[:], ACT.Exp, scale=-1.0).then_inc(a_dexp, 1)
                if j == 2:
                    wait(act, a_v1, u.plus(1))
                    wait(act, a_htmp, u.times(2))
                    A(a_vt[:, 0:2, P:2 * P], ps[:, M2, 0:2 * P].rearrange("p (b e) -> p b e", b=2), ACT.Copy)
                    A(a_vt[0:TS, 2, P:2 * P], ps[0:TS, M2, 2 * P:3 * P], ACT.Copy)
                    for n in (0, 2):
                        A(a_v3[n * TS:(n + 1) * TS, P:2 * P], ps[0:TS, M2, 2 * P:3 * P], ACT.Copy)
                    A(a_em[:], ps[:, M3, 0:T], ACT.Exp, scale=-1.0).then_inc(a_v1_tok, 1)
                if j == 3:
                    for e in range(2):
                        wait(act, a_htmp, u.times(2).plus(e + 1))
                        A(a_out_hi[:, u.times(2).plus(e).value, :], a_h[:, e, :], ACT.Copy).then_inc(a_hhi, 1)
                if j == 4:
                    wait(act, a_cupd, u.times(4).plus(1))
                    wait(act, a_cp_out, u.times(16))
                    A(a_nnew[:, h, 0:1], ps[:, M3, A_DV:A_DV + 1], ACT.Copy)
                    A(a_cp[:], ps[:, M3, 0:A_DV], ACT.Copy).then_inc(a_cp_ready, 1)

            def a_head(u, p, mixed):
                for j in range(6):
                    if mixed is not None:
                        a_mix(mixed, 1 - p, j)
                    split(u.times(6).plus(C_AIN + j + 2))
                    if mixed is None:
                        if j == 0:
                            norm(0)
                        gates(j)
                    a_post(u, p, j)

            a_head(Count(0), 0, None)
            gate_columns()
            a_head(Count(1), 1, Count(0))
            with act.Fori(0, 3) as i:
                for n in range(2):
                    a_head(Count(2 + n, (i, 2)), n, Count(1 + n, (i, 2)))
            for j in range(C_PART):
                if j < 6:
                    a_mix(Count(7), 1, j)
                split(Count(C_AOUT + j + 2))
            out_part(Count(C_AOUT + C_PART), KT, KT, 1)

            def ffn(layer, c0, ea0, ed0, k):
                first = 2 * FT * layer

                def half(h):
                    last = layer == 1 and h == 1
                    def pair(i, par):
                        m = Count(first // 2 + par).add(h, FH).add(i, 2)
                        for j in range(2):
                            s = 2 * par + j
                            n = Count(s).add(h, 2 * FH).add(i, 4)
                            c = Count(c0 + s).add(h, C_FHALF).add(i, 4)
                            split(c.plus(2))
                            if j == 1:
                                wait(act, f_conved, m.times(2).plus(1 + 4 * (layer + 1)))
                                wait(act, f_alo, m.plus(-1))
                                gate, th = f_u[:, 2 * par, :], f_act[:, par, :]
                                A(th[:, 0:TP], gate[:, 0:TP], ACT.Tanh)
                                A(packed(th), f_samples(gate)[:, :, 0:SL], ACT.Tanh).then_inc(f_gated, 1)
                            wait(act, proj_taken, n.plus(ea0 + 1))
                            w = lambda tap: f_conv[:, layer, n.value, tap:tap + 1]
                            A(f_u[:, s, 0:FP - 2], f_pad[:, s, 0:FP - 2], ACT.Identity, bias=w(3),
                              scale=w(0)).then_inc(f_tap0, 1)
                        wait(act, f_prod, m.plus(1))
                        A(act_hi[:, Count(par).add(i, 2).value, :], f_act[:, par, :], ACT.Copy).then_inc(f_ahi, 1)

                    with act.Fori(0, FH // 2) as i:
                        for par in range(2):
                            pair(i, par)
                    down(Count(c0 + 2 * FH).add(h, C_FHALF), Count(ed0).add(h, KT),
                         Count(KT * (k + 1)) if h == 1 else None, last, 2 if layer == 0 and h == 1 else None)

                norm(k)
                half(0)
                half(1)

            ffn(0, C_F0, EA_F0, ED_F0, 1)

            split(Count(C_BGATE + 2))
            norm(2)

            def gates_b(j):
                if j == 5:
                    wait(act, proj_taken, EA_BGATE + 1)
                    own.link(A(b_rows[:, 1, :], b_rows[:, 1, :], ACT.Identity, bias=b_small[:, 0:1]))
                    A(b_rsum[:, TS:TS + 1], b_small[:, 1:2], ACT.Exp)
                    own.link(A(b_tmp[:, 0, :], b_rows[:, 1, :], ACT.Abs))
                    A(b_rows[:, 2, :], b_tmp[:, 0, :], ACT.Exp, scale=-1.0).then_inc(gb_exp, 1)
                if j == 6:
                    act.wait_ge(gb_onep, 1)
                    A(b_tmp[:, 1, :], b_tmp[:, 0, :], ACT.Ln).then_inc(gb_ln, 1)
                if j == 8:
                    act.wait_ge(gb_logs, 1)
                    A(b_nac2[0:64, :], b_rows[:, 0, :], ACT.Copy).then_inc(gb_high, 1)
                    A(b_rows[:, 2, :], b_rows[:, 2, :], ACT.Exp, scale=-1.0)
                    A(b_rsum[:, 0:TS], b_rows[:, 0, TP:T], ACT.Exp, scale=-1.0).then_inc(gb_rows, 1)

            def gate_columns_b():
                act.wait_ge(gb_turned, 1)
                for n, col in enumerate((b_nac, b_dtc, b_end)):
                    src = ps[:, M1 if n < 2 else M2, 192 * (n % 2):192 * (n % 2) + 192].rearrange(
                        "p (b g h) -> p g b h", b=3, g=B_GROUPS)
                    for b in range(3):
                        w = P if b < 2 else TS
                        m = A(col[0:w, :, b, :], src[0:w, :, b, :], ACT.Copy)
                m.then_inc(gb_done, 1)
                act.wait_ge(gb_done, 1)

            def b_first_tap(u, p, j):
                wait(act, proj_taken, u.times(10).plus(EA_BIN + j + 1))
                n = u.times(6).plus(j)
                if j < 6:
                    wait(act, b_silu, n)
                    w = lambda tap: b_conv[:, n.value, tap:tap + 1]
                    A(b_u[:, 0:BP - 3], b_pad[:, j % 2, 0:BP - 3], ACT.Identity, bias=w(4), scale=w(0)).then_inc(b_tap0, 1)
                else:
                    if j == 6:
                        wait(act, b_silu, u.times(6).plus(6))
                    else:
                        wait(act, b_zready, u.times(4).plus(j - 6))
                    A(b_th[:, 0:T], b_io[:, p, j, :], ACT.Tanh, scale=0.5).then_inc(b_ztanh, 1)

            def b_tanh_of(u, j):
                if j < 6:
                    wait(act, b_conved, u.times(6).plus(j + 3))
                    if j == 0:
                        wait(act, b_zready, u.times(4))
                    A(b_th[:, 0:BP - 3], b_u[:, 0:BP - 3], ACT.Tanh).then_inc(b_tanh, 1)

            def b_mix(u, p, j):
                if j == 1:
                    wait(act, b_cbx, u.plus(1))
                    wait(act, b_wts, u.times(4))
                    wait(act, b_yst, u.times(8))
                    wait(act, b_bmask, u)
                    A(b_cb[:, 0:TP + P], ps[:, M0, 0:TP + P], ACT.Copy)
                    A(b_cb[0:TS, TP + P:SC], ps[0:TS, M0, TP + P:SC], ACT.Copy)
                    A(b_bt[:, 0:2, :], ps[:, M1, 0:2 * P].rearrange("p (b e) -> p b e", b=2), ACT.Copy)
                    for n in (0, 2):
                        A(b_b3[n * TS:(n + 1) * TS, :], ps[0:TS, M1, 2 * P:3 * P], ACT.Copy)
                    A(b_bt[0:TS, 2, :], ps[0:TS, M1, 2 * P:3 * P], ACT.Copy).then_inc(b_cbx_out, 1)
                if j in (2, 4, 6, 8):
                    k = (j - 2) // 2
                    wait(act, b_dlog, u.times(4).plus(k + 1))
                    A(b_dec[:], b_dec[:], ACT.Exp, scale=-1.0).then_inc(b_dexp, 1)
                    wait(act, b_xwr, u.times(4).plus(k + 1))
                    A(b_x3[0:TS, :], b_xw[0:TS, 2, :], ACT.Copy)
                    A(b_x3[TS:2 * TS, :], b_xw[0:TS, 2, :], ACT.Copy).then_inc(b_xhigh, 1)
                if j in (3, 5, 7, 9):
                    k = (j - 3) // 2
                    n = u.times(4).plus(k)
                    wait(act, b_yst, n.times(2).plus(2))
                    wait(act, b_sp_out, n.times(16))
                    A(b_sp[:], ps[:, M3, 0:P], ACT.Copy).then_inc(b_spr, 1)
                    wait(act, b_yg, n.plus(1))
                    A(b_io[:, p, 2 + k, :], b_io[:, p, 6 + k, :], ACT.Square).then_inc(b_gsq, 1)

            def b_group_norm(u, p):
                wait(act, b_gvar, u.plus(1))
                A(b_r[:], b_r[:], ACT.Sqrt).then_inc(b_groot, 1)
                for k in range(4):
                    wait(act, b_gn, u.times(4).plus(k + 1))
                    A(b_out_hi[:, b_place(u, p) + k, :], work[:, k % 2, :], ACT.Copy).then_inc(b_ghi, 1)

            def b_group(u, p, c, mixed):
                for j in range(10):
                    split(c.plus(j + 2))
                    b_first_tap(u, p, j)
                    if mixed is not None and j < 9:
                        b_mix(mixed, 1 - p, j + 1)
                    b_tanh_of(u, j)
                    if mixed is None:
                        gates_b(j)
                if mixed is None:
                    gate_columns_b()
                else:
                    b_group_norm(mixed, 1 - p)

            b_group(Count(0), 0, Count(C_BIN), None)
            b_group(Count(1), 1, Count(C_BIN + 10), Count(0))
            with act.Fori(0, 2) as i:
                for n in range(2):
                    b_group(Count(2 + n, (i, 2)), n, Count(C_BIN + 20 + 10 * n, (i, C_BTURN)), Count(1 + n, (i, 2)))
                out_part(Count(C_BIN + 40, (i, C_BTURN)))
            b_group(Count(6), 0, Count(C_BIN + 76), Count(5))
            b_group(Count(7), 1, Count(C_BIN + 86), Count(6))
            for j in range(10):
                if j < C_PART:
                    split(Count(C_BIN + 96 + j + 2))
                if j < 9:
                    b_mix(Count(7), 1, j + 1)
            b_group_norm(Count(7), 1)
            out_part(Count(C_BIN + 104), ED_BIN + 3 * KT, 3 * KT, 3)
            ffn(1, C_F1, EA_F1, ED_F1, 3)
            norm(4)

        @block.vector
        def _(dve):
            own = Own(dve, dve_own)
            V = nc.vector
            STT, TT, TS_ = V.scalar_tensor_tensor, V.tensor_tensor, V.tensor_scalar

            def split(c, cols=CH):
                wait(dve, w_high, c.plus(1))
                s = c.base % 2
                TT(w_lo[:, s, 0:cols], w_raw[:, s, 0:cols], w_hi[:, s, 0:cols].bitcast(F32), ALU.subtract).then_inc(w_low, 1)

            def norm(k):
                wait(dve, mean_ready, k + 1)
                TS_(rstd[:], ps[:, M0, 0:T], EPS, None, ALU.add).then_inc(var_ready, 1)
                wait(dve, root_ready, k + 1)
                V.reciprocal(rstd[:], rstd[:]).then_inc(rstd_ready, 1)
                wait(dve, rstd_ready, k + 1)

            def input_low(k, t):
                wait(dve, hn_hi_ready, t.plus(KT * k + 1))
                t = t.value
                w = norm_w[:, k, t:t + 1] if isinstance(t, int) else norm_w[:, k, bass.ds(t, 1)]
                STT(hn_lo[:, t, :], x[:, t, :], w, hn_hi[:, t, :].bitcast(F32), ALU.mult, ALU.subtract).then_inc(hn_lo_ready, 1)

            def down(c0, n0, last=False, k=None):
                def four(i, tail):
                    for j in range(4):
                        for q in range(2):
                            ahead = tail and j == 3
                            if q == 1:
                                wait(dve, chunk_done, c0.plus((j + 1) * 2).add(i, 8))
                                t = Count(j).add(i, 4).value
                                TT(x[:, t, :], x[:, t, :], ps[:, (n0 + j) % 4, 0:T], ALU.add).then_inc(res_added, 1)
                            if not (ahead and last):
                                split(c0.plus(j * 2 + q + 2).add(i, 8), CH if ahead else DCH)
                        if k is not None:
                            input_low(k, Count(j).add(i, 4))
                with dve.Fori(0, KT // 4 - 1) as i:
                    four(i, False)
                four(KT // 4 - 1, True)

            def out_chunk(c, n0, m, t, k=None):
                wait(dve, chunk_done, c.plus(1))
                for e in range(2):
                    xt = x[:, t.plus(e).value, :]
                    TT(xt, xt, ps[:, (n0 + 2 * m + e) % 4, 0:T], ALU.add).then_inc(res_added, 1)
                split(c.plus(2))
                for e in range(2):
                    if k is not None:
                        input_low(k, t.plus(e))

            def out_part(c, n0, k=None):
                with dve.Fori(0, C_PART // 2) as i:
                    for m in range(2):
                        out_chunk(c.plus(m).add(i, 2), n0, m, Count(2 * m, (i, 4)), k)

            split(Count(0))
            dve.wait_ge(norm_w_in, 16)
            for t in range(KT):
                input_low(0, Count(t))
            split(Count(1))
            dve.wait_ge(consts_in, N_CONSTS)
            TS_(b_conv[:], b_conv[:], 0.5, None, ALU.mult)
            gate_taps = f_conv[:].rearrange("p l (t two) k -> p l t two k", two=2)[:, :, :, 0, :]
            TS_(gate_taps, gate_taps, 0.5, None, ALU.mult)
            TS_(b_normw[:], b_normw[:], 0.5, None, ALU.mult)
            V.memset(a_dec[:], 0.0)

            split(Count(2))
            row = lambda n: a_rows[:, n, :]
            m0 = a_small[:, 2:2 + NB]

            def gates(j):
                if j == 0:
                    dve.wait_ge(ga_exp, 1)
                    TS_(row(2), row(3), 1.0, None, ALU.add).then_inc(ga_onep, 1)
                    dve.wait_ge(ga_onep, 1)
                    own.link(TS_(row(5), row(2), -1.0, None, ALU.add))
                    own.link(TT(row(5), row(3), row(5), ALU.subtract))
                    own.link(V.reciprocal(row(6), row(2)))
                    own.link(TT(row(5), row(5), row(6), ALU.mult))
                if j == 1:
                    dve.wait_ge(ga_ln, 1)
                    own.link(TT(row(4), row(4), row(5), ALU.add))
                    own.link(STT(row(1), row(1), 0.0, row(4), ALU.min, ALU.subtract))
                    own.link(V.tensor_tensor_scan(row(3), seg_keep[0:8, :], row(1), 0.0, ALU.mult, ALU.add))
                    own.link(TT(row(4), row(0), row(3), ALU.subtract))
                if j == 2:
                    own.link(V.tensor_copy(row(2), row(4)))
                    own.mark(TS_(a_rows[:, 2, 0:1], a_rows[:, 4, 0:1], 0.0, None, ALU.max))
                    own.link(TT(packed(row(2))[:, :, 0], packed(row(4))[:, :, 0], m0, ALU.max))
                    own.link(V.tensor_tensor_scan(row(5), seg_drop[:], row(2), 0.0, ALU.add, ALU.max))
                    own.link(TT(row(7), row(3), row(5), ALU.add))
                    TS_(a_rows[:, 6, 0:TP], a_rows[:, 4, 0:TP], a_rows[:, 5, TP - 1:TP], None, ALU.subtract)
                    m_end = packed(row(5))[:, :, SL - 1:SL].to_broadcast([8, NB, SL])
                    TT(packed(row(6)), packed(row(4)), m_end, ALU.subtract)
                    TT(packed(row(8)), m0.unsqueeze(2).to_broadcast([8, NB, SL]), packed(row(5)), ALU.subtract)
                    V.tensor_copy(a_mnew[:, 0:1], a_rows[:, 7, TP - 1:TP])
                    V.tensor_copy(a_mnew[:, 1:], packed(row(7))[:, :, SL - 1]).then_inc(ga_logs, 1)

            A_STEPS = 8

            def a_link(u, k, ins):
                ins.then_inc(a_steps, 1)
                wait(dve, a_steps, u.times(A_STEPS).plus(k))

            def a_mix(u, p, j):
                h = u.value
                q = a_io[:, p, 0, TP:T]
                if j == 1:
                    wait(dve, a_scores, u.plus(1))
                    STT(a_dec[:, 0:TP], ps[:, M1, 0:TP], a_acol[:, h, 0:1], future[:, 0:TP], ALU.subtract, ALU.max)
                    STT(a_dec[:, TP:TP + P], ps[:, M1, P:TP], a_acol[:, h, 1:2], future[:, TP:TP + P], ALU.subtract, ALU.max)
                    STT(a_dec[0:TS, TP + P:SC], ps[0:TS, M1, TP:T], a_acol[0:TS, h, 2:3], future[0:TS, TP + P:SC],
                        ALU.subtract, ALU.max).then_inc(a_dlog, 1)
                    wait(dve, a_num, u)
                    a_link(u, 1, V.tensor_copy(a_wi[:], ps[:, M1, T:T + TS]))
                    a_link(u, 2, TT(a_qs[:], q, a_wi[:], ALU.mult))
                    by_batch = lambda t: t.rearrange("p (b l) -> p b l", l=SL)
                    TT(by_batch(a_nq[:]), by_batch(a_qs[:]), a_n[:, h, :].unsqueeze(2).to_broadcast([P, NB, SL]), ALU.mult)
                    wait(dve, a_dexp, u.plus(1))
                    TT(a_prob[:, 0:TP + P], ps[:, M0, 0:TP + P], a_dec[:, 0:TP + P], ALU.mult)
                    TT(a_prob[0:TS, TP + P:SC], ps[0:TS, M0, TP + P:SC], a_dec[0:TS, TP + P:SC], ALU.mult).then_inc(a_probs, 1)
                if j == 2:
                    wait(dve, a_v1_tok, u.plus(1))
                    TT(a_k3[2 * TS:3 * TS, :], a_kw[0:TS, 2, :], a_k3[0:TS, :].bitcast(F32), ALU.subtract)
                    TT(a_v3[TS:2 * TS, :], a_vt[0:TS, 2, :], a_v3[0:TS, :].bitcast(F32), ALU.subtract).then_inc(a_klow, 1)
                    wait(dve, a_otanh, u.times(2).plus(2))
                    a_link(u, 3, TS_(a_io[:, p, 4:6, :], a_io[:, p, 4:6, :], 0.5, 0.5, ALU.mult, ALU.add))
                if j == 3:
                    wait(dve, a_num, u.plus(1))
                    wait(dve, a_v1_tok, u.plus(1))
                    a_link(u, 4, STT(a_em[:], ps[:, M2, 0:T], -1.0, a_em[:], ALU.mult, ALU.max))
                    a_link(u, 5, TT(a_em[:], a_em[:], ps[:, M2, 0:T], ALU.max))
                    a_link(u, 6, V.reciprocal(a_em[:], a_em[:]))
                    a_link(u, 7, TT(a_io[:, p, 4:6, :], a_io[:, p, 4:6, :], a_em[:].unsqueeze(1).to_broadcast([P, 2, T]), ALU.mult))
                    for e in range(2):
                        TT(a_h[:, e, :], ps[:, M0 + e, 0:T], a_io[:, p, 4 + e, :], ALU.mult).then_inc(a_htmp, 1)
                    for e in range(2):
                        n = u.times(2).plus(e)
                        wait(dve, a_hhi, n.plus(1))
                        TT(a_out_lo[:, n.value, :], a_h[:, e, :], a_out_hi[:, n.value, :].bitcast(F32),
                           ALU.subtract).then_inc(a_hlo, 1)
                last_step = a_wi[:].rearrange("p (b l) -> p b l", l=SL)[:, :, SL - 1]

                def c_add(n):
                    wait(dve, a_cupd, u.times(4).plus(n + 1))
                    for e in range(2):
                        b = 2 * n + e
                        m = STT(a_c[:, p, b, :], a_c[:, p, b, :], a_wi[:, SL * b + SL - 1:SL * (b + 1)],
                                ps[:, M0 + n % 3, e * A_DV:(e + 1) * A_DV], ALU.mult, ALU.add)
                    m.then_inc(a_cadd, 1)
                if j == 4:
                    wait(dve, a_cupd, u.times(4).plus(1))
                    wait(dve, a_cp_ready, u.plus(1))
                    a_link(u, 8, TT(a_nnew[:, h, 1:1 + NB], a_n[:, h, :], last_step, ALU.mult))
                    TT(a_nnew[:, h, 1:1 + NB], a_nnew[:, h, 1:1 + NB], ps[:, M3, A_DV + 1:A_DV + 1 + NB], ALU.add)
                    for n in range(3):
                        c_add(n)
                if j == 5:
                    c_add(3)

            def a_take(u, p, j):
                c = u.times(6).plus(C_AIN + j)
                if j == 0 and u.base > 0:
                    wait(dve, a_v1, u.plus(-1))
                wait(dve, chunk_done, c.plus(1))
                STT(a_io[:, p, j, :], ps[:, c.base % 4, 0:T], A_DK ** -0.5 if j == 1 else 1.0, rstd[:], ALU.mult,
                    ALU.mult).then_inc(proj_taken, 1)

            def a_head(u, p, mixed):
                for j in range(6):
                    if mixed is not None:
                        a_mix(mixed, 1 - p, j)
                    if mixed is None and j == 0:
                        split(Count(C_AIN + 2))
                        norm(0)
                        TT(a_rows[:, 0, :], ps[0:8, 0, 0:T], rstd[0:8, :], ALU.mult)
                        TT(a_rows[:, 1, :], ps[32:40, 0, 0:T], rstd[32:40, :], ALU.mult).then_inc(proj_taken, 1)
                    a_take(u, p, j)
                    if not (mixed is None and j == 0):
                        split(u.times(6).plus(C_AIN + j + 2))
                    if mixed is None:
                        gates(j)

            a_head(Count(0), 0, None)
            dve.wait_ge(ga_done, 1)
            dve.wait_ge(a_n_in, 16)
            a_head(Count(1), 1, Count(0))
            with dve.Fori(0, 3) as i:
                for n in range(2):
                    a_head(Count(2 + n, (i, 2)), n, Count(1 + n, (i, 2)))
            for j in range(C_PART):
                if j < 6:
                    a_mix(Count(7), 1, j)
                out_chunk(Count(C_AOUT + j), N_AOUT, j, Count(2 * j))
            out_part(Count(C_AOUT + C_PART), N_AOUT, 1)

            def ffn(layer, c0, n0, ea0, k):
                first = 2 * FT * layer
                if layer == 0:
                    for s in a_c_out:
                        dve.wait_ge(s, 16 * A_HEADS // 2)
                    dve.wait_ge(a_cp_out, 16 * A_HEADS)
                    dve.wait_ge(a_nm_out, 32)
                else:
                    dve.wait_ge(b_s_out, 16 * 32)
                    dve.wait_ge(b_sp_out, 16 * 32)
                    dve.wait_ge(b_new_out, 16 * B_GROUPS)
                wait(dve, mean_ready, k + 1)
                for s in range(4):
                    V.memset(f_pad[:, s, 0:2], 0.0).then_inc(f_conved, 1)
                norm(k)

                def half(h):
                    last = layer == 1 and h == 1
                    def pair(i, par):
                        m = Count(first // 2 + par).add(h, FH).add(i, 2)
                        for j in range(2):
                            s = 2 * par + j
                            n = Count(s).add(h, 2 * FH).add(i, 4)
                            c = Count(c0 + s).add(h, C_FHALF).add(i, 4)
                            wait(dve, chunk_done, c.plus(1))
                            wait(dve, f_prefix, n.plus(first + 1))
                            src = ps[:, (c0 + s) % 4, 0:T]
                            TT(f_pad[:, s, 2:2 + TP], src[:, 0:TP], rstd[:, 0:TP], ALU.mult)
                            TT(f_samples(f_pad[:, s, :])[:, :, 2:], packed(src), packed(rstd), ALU.mult).then_inc(proj_taken, 1)
                            split(c.plus(2))
                            g, v, prod = f_u[:, 2 * par, :], f_u[:, 2 * par + 1, :], f_act[:, par, :]
                            if j == 1:
                                wait(dve, f_gated, m.plus(1))
                                STT(prod[:, 0:TP], prod[:, 0:TP], 1.0, g[:, 0:TP], ALU.add, ALU.mult)
                                STT(packed(prod), packed(prod), 1.0, f_samples(g)[:, :, 0:SL], ALU.add,
                                    ALU.mult).then_inc(f_silu, 1)
                            wait(dve, proj_taken, n.plus(ea0 + 1))
                            wait(dve, f_tap0, n.plus(first + 1))
                            w = lambda tap: f_conv[:, layer, n.value, tap:tap + 1]
                            STT(f_u[:, s, 0:FP - 2], f_pad[:, s, 1:FP - 1], w(1), f_u[:, s, 0:FP - 2], ALU.mult,
                                ALU.add).then_inc(f_tap1, 1)
                            wait(dve, f_tap1, n.plus(first + 1))
                            STT(f_u[:, s, 0:FP - 2], f_pad[:, s, 2:FP], w(2), f_u[:, s, 0:FP - 2], ALU.mult,
                                ALU.add).then_inc(f_conved, 1)
                        wait(dve, f_silu, m.plus(1))
                        wait(dve, f_conved, m.times(2).plus(2 + 4 * (layer + 1)))
                        TT(prod[:, 0:TP], prod[:, 0:TP], v[:, 0:TP], ALU.mult)
                        TT(packed(prod), packed(prod), f_samples(v)[:, :, 0:SL], ALU.mult).then_inc(f_prod, 1)
                        wait(dve, f_ahi, m.plus(1))
                        t = Count(par).add(i, 2).value
                        TT(act_lo[:, t, :], f_act[:, par, :], act_hi[:, t, :].bitcast(F32), ALU.subtract).then_inc(f_alo, 1)

                    with dve.Fori(0, FH // 2) as i:
                        for par in range(2):
                            pair(i, par)
                    down(Count(c0 + 2 * FH).add(h, C_FHALF), n0 + 2 * FH, last, 2 if layer == 0 and h == 1 else None)

                half(0)
                half(1)

            ffn(0, C_F0, N_F0, EA_F0, 1)

            dve.wait_ge(f_new_out, 16)
            wait(dve, mean_ready, 3)
            for s in range(2):
                V.memset(b_pad[:, s, 0:3], 0.0).then_inc(b_conved, 1)
            V.memset(b_cb[:], 0.0)
            V.memset(b_dec[:], 0.0)
            split(Count(C_BGATE + 2))
            norm(2)
            TT(b_rows[:, 1, :], ps[0:64, (N_BIN - 1) % 4, 0:T], rstd[0:64, :], ALU.mult).then_inc(proj_taken, 1)
            brow = lambda n: b_rows[:, n, :] if n < 3 else b_tmp[:, n - 3, :]

            def gates_b(j):
                if j == 5:
                    dve.wait_ge(gb_exp, 1)
                    TS_(brow(3), brow(2), 1.0, None, ALU.add).then_inc(gb_onep, 1)
                    dve.wait_ge(gb_onep, 1)
                    own.link(TS_(brow(0), brow(3), -1.0, None, ALU.add))
                    own.link(TT(brow(0), brow(2), brow(0), ALU.subtract))
                    own.link(V.reciprocal(brow(2), brow(3)))
                    own.link(TT(brow(0), brow(0), brow(2), ALU.mult))
                if j == 6:
                    dve.wait_ge(gb_ln, 1)
                    own.link(TT(brow(4), brow(4), brow(0), ALU.add))
                    own.link(STT(brow(1), brow(1), 0.0, brow(4), ALU.max, ALU.add))
                    own.link(TS_(brow(4), brow(1), b_rsum[:, TS:TS + 1], None, ALU.mult))
                    own.link(V.tensor_tensor_scan(brow(0), seg_keep[:], brow(4), 0.0, ALU.mult, ALU.add))
                if j == 9:
                    dve.wait_ge(gb_high, 1)
                    TT(b_nac2[64:P, :], b_rows[:, 0, :], b_nac2[0:64, :].bitcast(F32), ALU.subtract).then_inc(gb_low, 1)
                if j == 7:
                    own.link(TS_(b_rows[:, 2, 0:TP], b_rows[:, 0, 0:TP], -1.0, b_rows[:, 0, TP - 1:TP], ALU.mult, ALU.add))
                    end = packed(brow(0))[:, :, SL - 1:SL].to_broadcast([64, NB, SL])
                    TT(packed(brow(2)), end, packed(brow(0)), ALU.subtract).then_inc(gb_logs, 1)

            def b_take(u, p, c, j):
                wait(dve, chunk_done, c.plus(j + 1))
                src = ps[:, (N_BIN + 10 * p + j) % 4, 0:T]
                if j < 6:
                    wait(dve, b_prefix, u.times(6).plus(j + 1))
                    TT(b_pad[:, j % 2, 3:3 + TP], src[:, 0:TP], rstd[:, 0:TP], ALU.mult)
                    TT(b_samples(b_pad[:, j % 2, :])[:, :, 3:], packed(src), packed(rstd), ALU.mult).then_inc(proj_taken, 1)
                else:
                    TT(b_io[:, p, j, :], src, rstd[:], ALU.mult).then_inc(proj_taken, 1)

            def b_post(u, p, j):
                n = u.times(6).plus(j)
                if j < 6:
                    wait(dve, proj_taken, u.times(10).plus(EA_BIN + j + 1))
                    pad, out = b_pad[:, j % 2, :], b_u[:, 0:BP - 3]
                    w = lambda tap: b_conv[:, n.value, tap:tap + 1]
                    wait(dve, b_tap0, n.plus(1))
                    STT(out, pad[:, 1:BP - 2], w(1), out, ALU.mult, ALU.add).then_inc(b_taps, 1)
                    wait(dve, b_taps, n.times(2).plus(1))
                    STT(out, pad[:, 2:BP - 1], w(2), out, ALU.mult, ALU.add).then_inc(b_taps, 1)
                    wait(dve, b_taps, n.times(2).plus(2))
                    STT(out, pad[:, 3:BP], w(3), out, ALU.mult, ALU.add).then_inc(b_conved, 1)
                    wait(dve, b_tanh, n.plus(1))
                    STT(b_io[:, p, j, 0:TP], b_th[:, 0:TP], 1.0, b_u[:, 0:TP], ALU.add, ALU.mult)
                    STT(packed(b_io[:, p, j, :]), b_samples(b_th)[:, :, 0:SL], 1.0, b_samples(b_u)[:, :, 0:SL], ALU.add,
                        ALU.mult).then_inc(b_silu, 1)
                else:
                    wait(dve, b_ztanh, u.times(4).plus(j - 6 + 1))
                    STT(b_io[:, p, j, :], b_th[:, 0:T], 1.0, b_io[:, p, j, :], ALU.add, ALU.mult).then_inc(b_zready, 1)

            B_STEPS = 4 * 3 + 1

            def b_link(u, k, ins):
                ins.then_inc(b_steps, 1)
                wait(dve, b_steps, u.times(B_STEPS).plus(k))

            def heads(ap):
                return ap.rearrange("p (h e) -> p h e", e=64)

            def b_mix(u, p, j):
                uv = u.value
                if j == 1:
                    wait(dve, b_cbx, u.plus(1))
                    wait(dve, b_xwr, u.times(4))
                    wait(dve, b_yst, u.times(8))
                    TT(heads(b_xdt[:, 0, :]), heads(ps[:, M2, :]), b_dtc[:, uv, 0, :].unsqueeze(2).to_broadcast([P, 8, 64]), ALU.mult)
                    TT(heads(b_xdt[:, 1, :]), heads(ps[:, M3, :]), b_dtc[:, uv, 1, :].unsqueeze(2).to_broadcast([P, 8, 64]),
                       ALU.mult).then_inc(b_xt_out, 1)
                    wait(dve, b_cbx_out, u.plus(1))
                    TT(b_b3[TS:2 * TS, :], b_bt[0:TS, 2, :], b_b3[0:TS, :].bitcast(F32), ALU.subtract).then_inc(b_blow, 1)
                if j == 2:
                    wait(dve, b_xs, u.plus(1))
                    TT(heads(b_xdt[0:TS, 2, :]), heads(ps[0:TS, M2, :]),
                       b_dtc[0:TS, uv, 2, :].unsqueeze(2).to_broadcast([TS, 8, 64]), ALU.mult).then_inc(b_xs_out, 1)
                if j in (2, 4, 6, 8):
                    k = (j - 2) // 2
                    n = u.times(4).plus(k)
                    wait(dve, b_rowsr, n.plus(1))
                    wait(dve, b_yst, n.times(2))
                    wait(dve, b_decayed, n)
                    V.tensor_copy(b_ea[:], ps[:, M1, T:T + TS])
                    for e in range(2):
                        col = lambda b, w: b_nac[0:w, uv, b, 2 * k + e:2 * k + e + 1]
                        STT(b_dec[:, e, 0:TP], ps[:, M0 + e, 0:TP], col(0, P), future[:, 0:TP], ALU.subtract, ALU.max)
                        STT(b_dec[:, e, TP:TP + P], ps[:, M0 + e, P:TP], col(1, P), future[:, TP:TP + P], ALU.subtract, ALU.max)
                        m = STT(b_dec[0:TS, e, TP + P:SC], ps[0:TS, M0 + e, TP:T], col(2, TS), future[0:TS, TP + P:SC],
                                ALU.subtract, ALU.max)
                    m.then_inc(b_dlog, 1)

            def b_weights(u, j):
                if j in (2, 4, 6, 8):
                    n = u.times(4).plus((j - 2) // 2)
                    wait(dve, b_cbx_out, u.plus(1))
                    wait(dve, b_dexp, n.plus(1))
                    TT(b_dec[:], b_dec[:], b_cb[:].unsqueeze(1).to_broadcast([P, 2, SC]), ALU.mult).then_inc(b_wts, 1)
                    wait(dve, b_xhigh, n.plus(1))
                    TT(b_x3[2 * TS:3 * TS, :], b_xw[0:TS, 2, :], b_x3[0:TS, :].bitcast(F32), ALU.subtract).then_inc(b_xlow, 1)

            def b_outputs(u, p, j):
                if j in (3, 5, 7, 9):
                    k = (j - 3) // 2
                    n = u.times(4).plus(k)
                    wait(dve, b_yst, n.times(2).plus(1))
                    b_link(u, 3 * k + 1, TT(b_yi[:], ps[:, M2, T:T + TS], b_ea[:], ALU.mult))
                    y = b_io[:, p, 2 + k, :]
                    b_link(u, 3 * k + 2, STT(y, b_io[:, p, 2 + k, :], b_skip[:, n.value, 0:1], ps[:, M2, 0:T], ALU.mult, ALU.add))
                    b_link(u, 3 * k + 3, TT(y[:, TP:T], y[:, TP:T], b_yi[:], ALU.add))
                    wait(dve, b_zready, n.plus(1))
                    TT(b_io[:, p, 6 + k, :], y, b_io[:, p, 6 + k, :], ALU.mult).then_inc(b_yg, 1)
                    wait(dve, b_yst, n.times(2).plus(2))
                    wait(dve, b_decayed, n.plus(1))
                    for half in range(2):
                        s = b_s[:, 4 * half:4 * half + 4, :]
                        TT(s, s, ps[:, M0 + half, :].rearrange("p (b n) -> p b n", b=4), ALU.add).then_inc(b_sadd, 1)

            def b_group_norm(u, p):
                wait(dve, b_gms, u.plus(1))
                TS_(b_r[:], ps[:, M2, 0:T], EPS, None, ALU.add).then_inc(b_gvar, 1)
                wait(dve, b_groot, u.plus(1))
                b_link(u, 13, V.reciprocal(b_r[:], b_r[:]))
                for k in range(4):
                    n = u.times(4).plus(k)
                    if k > 1:
                        wait(dve, b_glo, n.plus(-1))
                    STT(work[:, k % 2, :], b_io[:, p, 6 + k, :], b_normw[:, n.value, 0:1], b_r[:], ALU.mult,
                        ALU.mult).then_inc(b_gn, 1)
                    wait(dve, b_ghi, n.plus(1))
                    t = b_place(u, p) + k
                    TT(b_out_lo[:, t, :], work[:, k % 2, :], b_out_hi[:, t, :].bitcast(F32),
                       ALU.subtract).then_inc(b_glo, 1)

            def b_group(u, p, c, mixed):
                for j in range(10):
                    mixes, even = mixed is not None and j < 9, j % 2 == 1
                    b_take(u, p, c, j)
                    if mixes and even:
                        b_mix(mixed, 1 - p, j + 1)
                    split(c.plus(j + 2))
                    if mixes and even:
                        b_weights(mixed, j + 1)
                    if mixes and j == 0:
                        b_mix(mixed, 1 - p, 1)
                    if mixes and not even:
                        b_outputs(mixed, 1 - p, j + 1)
                    b_post(u, p, j)
                    if mixed is None:
                        gates_b(j)
                if mixed is None:
                    dve.wait_ge(gb_done, 1)
                else:
                    b_group_norm(mixed, 1 - p)

            b_group(Count(0), 0, Count(C_BIN), None)
            b_group(Count(1), 1, Count(C_BIN + 10), Count(0))
            with dve.Fori(0, 2) as i:
                for n in range(2):
                    b_group(Count(2 + n, (i, 2)), n, Count(C_BIN + 20 + 10 * n, (i, C_BTURN)), Count(1 + n, (i, 2)))
                out_part(Count(C_BIN + 40, (i, C_BTURN)), N_BIN)
            b_group(Count(6), 0, Count(C_BIN + 76), Count(5))
            b_group(Count(7), 1, Count(C_BIN + 86), Count(6))
            for j in range(10):
                if j % 2 == 1 and j < 9:
                    b_mix(Count(7), 1, j + 1)
                if j < C_PART:
                    out_chunk(Count(C_BIN + 96 + j), N_BIN, j, Count(2 * j))
                if j % 2 == 1 and j < 9:
                    b_weights(Count(7), j + 1)
                if j == 0:
                    b_mix(Count(7), 1, 1)
                if j % 2 == 0:
                    b_outputs(Count(7), 1, j + 1)
            b_group_norm(Count(7), 1)
            out_part(Count(C_BIN + 104), N_BIN, 3)
            ffn(1, C_F1, N_F1, EA_F1, 3)
            norm(4)
            for t in range(KT):
                STT(x[:, t, :], x[:, t, :], norm_w[:, 4, t:t + 1], rstd[:], ALU.mult, ALU.mult).then_inc(y_ready, 1)

        @block.gpsimd
        def _(pool):
            G = nc.gpsimd
            own = Own(pool, pool_own)

            def until(sem, count):
                wait(pool, sem, count)
                if isinstance(count, Count) and count.terms:
                    pool.sem_inc(pool_passed, 1)

            def add_square(r, buf):
                until(squared, r.plus(1))
                until(sq_added, r)
                G.tensor_tensor(sumsq[:], sumsq[:], work[:, buf, :], ALU.add).then_inc(sq_added, 1)

            def residual(norms, sq0, used=None):
                until(mean_ready, norms)
                if used is not None:
                    until(*used)
                own.link(G.memset(sumsq[:], 0.0))
                with pool.Fori(0, KT // 2) as i:
                    for j in range(2):
                        add_square(sq0.plus(j).add(i, 2), j)

            own.link(G.memset(sumsq[:], 0.0))
            for t in range(KT):
                add_square(Count(t), t % 2)
            pool.dma_start(a_c[:, 0, :, :], d["a_c"][0]).then_inc(a_c_in[0], 16)
            pool.wait_ge(consts_in, N_CONSTS)

            def a_mix(u, p, j):
                if j == 0:
                    until(a_v1, u)
                    G.tensor_copy(a_sel[:], ident[0:8, bass.ds(u.value, 1)].to_broadcast([8, P])).then_inc(a_sel_ready, 1)
                if j == 1 and not (u.base == A_HEADS - 1 and not u.terms):
                    nxt = u.plus(1)
                    until(a_c_out[1 - p], nxt.half().times(16))
                    pool.dma_start(a_c[:, 1 - p, :, :], d["a_c"][nxt.value]).then_inc(a_c_in[1 - p], 16)
                if j == 2:
                    until(a_v1_tok, u.plus(1))
                    until(a_cupd, u.times(4))
                    until(a_klow, u.plus(1))
                    G.tensor_tensor(a_vm[:], a_v3[:].bitcast(F32).unsqueeze(1).to_broadcast([3 * TS, NB, A_DV]),
                                    in_batch[:].unsqueeze(2).to_broadcast([3 * TS, NB, A_DV]), ALU.mult).then_inc(a_vmask, 1)
                if j == 5:
                    until(a_cadd, u.plus(1).times(4))
                    pool.dma_start(o["C_s"][u.value], a_c[:, p, :, :]).then_inc(a_c_out[p], 16)
                    until(a_cp_ready, u.plus(1))
                    pool.dma_start(o["C_p"][u.value], a_cp[:]).then_inc(a_cp_out, 16)

            def head(u, p):
                for j in range(6):
                    a_mix(u, p, j)

            head(Count(0), 0)
            with pool.Fori(0, 3) as i:
                for n in range(2):
                    head(Count(1 + n, (i, 2)), 1 - n)
            head(Count(7), 1)
            pool.dma_start(o["n"], a_nnew[:]).then_inc(a_nm_out, 16)
            pool.dma_start(o["m"], a_mnew[:]).then_inc(a_nm_out, 16)
            residual(1, Count(KT), (a_htmp, Count(2 * A_HEADS)))

            def ffn(layer, k):
                first = 2 * FT * layer
                if layer == 0:
                    for s in a_c_out:
                        pool.wait_ge(s, 16 * A_HEADS // 2)
                    pool.wait_ge(a_cp_out, 16 * A_HEADS)
                    pool.wait_ge(a_nm_out, 32)
                else:
                    pool.wait_ge(b_s_out, 16 * 32)
                    pool.wait_ge(b_sp_out, 16 * 32)
                    pool.wait_ge(b_new_out, 16 * B_GROUPS)
                until(mean_ready, k + 1)
                pool.dma_start(f_old[:], d["f_old"][layer]).then_inc(f_old_in, 16)
                pool.wait_ge(f_old_in, 16 * (layer + 1))

                def half(h):
                    with pool.Fori(0, FH // 2) as i:
                        for s in range(4):
                            n = Count(s).add(h, 2 * FH).add(i, 4)
                            until(f_conved, n.plus(first + 1 + 4 * layer))
                            pad = f_samples(f_pad[:, s, :])
                            G.tensor_copy(pad[:, :, 0:2], f_old[:, n.value, :].rearrange("p (b k) -> p b k", k=2)).then_inc(f_prefix, 1)
                            until(f_tap0, n.plus(first + 1))
                            G.tensor_copy(f_new[:, n.value, 0:2], f_pad[:, s, TP:TP + 2])
                            G.tensor_copy(f_new[:, n.value, 2:].rearrange("p (b k) -> p b k", k=2),
                                          pad[:, :, SL:SL + 2]).then_inc(f_kept, 1)

                with pool.Fori(0, 2) as h:
                    half(h)
                residual(k + 1, Count(KT * (k + 1)))
                pool.wait_ge(f_kept, first + 2 * FT)
                pool.dma_start(o["fconv"][layer], f_new[:]).then_inc(f_new_out, 16)

            ffn(0, 1)

            pool.wait_ge(f_new_out, 16)
            until(mean_ready, 3)

            def load_state(n):
                pool.dma_start(b_sT[:], d["b_sT"][n.value]).then_inc(b_sT_in, 16)

            def b_fill(u, j):
                n = u.times(6).plus(j)
                if j == 0:
                    until(b_old_in, u.plus(1).times(16))
                until(b_conved, n.plus(1))
                G.tensor_copy(b_samples(b_pad[:, j % 2, :])[:, :, 0:3],
                              b_old[:, j, :].rearrange("p (b k) -> p b k", k=3)).then_inc(b_prefix, 1)

            def b_post(u, p, j):
                if j >= 6:
                    return
                n = u.times(6).plus(j)
                pad = b_samples(b_pad[:, j % 2, :])
                if j == 0:
                    until(b_new_out, u.times(16))
                until(b_tap0, n.plus(1))
                G.tensor_copy(b_new[:, j, 0:3], b_pad[:, j % 2, TP:TP + 3])
                G.tensor_copy(b_new[:, j, 3:].rearrange("p (b k) -> p b k", k=3), pad[:, :, SL:SL + 3]).then_inc(b_kept, 1)
                if j == 5:
                    until(b_prefix, n.plus(1))
                    if u.base < B_GROUPS - 1:
                        pool.dma_start(b_old[:], d["b_old"][u.plus(1).value]).then_inc(b_old_in, 16)
                    until(b_kept, n.plus(1))
                    pool.dma_start(o["bconv"][u.value], b_new[:]).then_inc(b_new_out, 16)

            def b_mix(u, p, j):
                uv = u.value
                def select(k):
                    n = u.times(4).plus(k)
                    until(b_rowsr, n)
                    G.tensor_copy(b_sel[:], head_ident[:, bass.ds(u.times(8).plus(2 * k).value, 2)].unsqueeze(2)
                                  .to_broadcast([P, 2, P])).then_inc(b_selr, 1)
                if j == 0:
                    select(0)
                if j == 1:
                    until(b_cbx_out, u.plus(1))
                    until(b_blow, u.plus(1))
                    G.tensor_tensor(b_bm[:], b_b3[:].bitcast(F32).unsqueeze(1).to_broadcast([3 * TS, NB, P]),
                                    in_batch[:].unsqueeze(2).to_broadcast([3 * TS, NB, P]), ALU.mult).then_inc(b_bmask, 1)
                if j in (2, 4, 6, 8):
                    k = (j - 2) // 2
                    n = u.times(4).plus(k)
                    ch = slice(k * P, (k + 1) * P)
                    until(b_xs_out, u.plus(1))
                    until(b_yst, n.times(2))
                    for b in range(3):
                        w = P if b < 2 else TS
                        m = G.tensor_tensor(b_xw[0:w, b, :].rearrange("p (h e) -> p h e", e=64),
                                            b_xdt[0:w, b, ch].rearrange("p (h e) -> p h e", e=64),
                                            b_end[0:w, uv, b, 2 * k:2 * k + 2].unsqueeze(2).to_broadcast([w, 2, 64]), ALU.mult)
                    m.then_inc(b_xwr, 1)
                    if k < 3:
                        select(k + 1)
                    until(b_s_out, n.times(16))
                    pool.dma_start(b_s[:], d["b_s"][n.value]).then_inc(b_s_in, 16)
                    until(b_s_in, n.plus(1).times(16))
                    until(b_dlog, n.plus(1))
                    dec = b_ea[:].rearrange("p (b l) -> p b l", l=SL)[:, :, SL - 1:SL].to_broadcast([P, NB, P])
                    G.tensor_tensor(b_s[:], b_s[:], dec, ALU.mult).then_inc(b_decayed, 1)
                if j in (3, 5, 7, 9):
                    k = (j - 3) // 2
                    n = u.times(4).plus(k)
                    until(b_sadd, n.plus(1).times(2))
                    pool.dma_start(o["ssm_s"][n.value], b_s[:]).then_inc(b_s_out, 16)
                    if not (u.base == B_GROUPS - 1 and k == 3):
                        load_state(n.plus(1))
                    until(b_spr, n.plus(1))
                    pool.dma_start(o["ssm_p"][n.value], b_sp[:]).then_inc(b_sp_out, 16)

            def b_group(u, p, mixed):
                if mixed is not None:
                    b_mix(mixed, 1 - p, 0)
                for j in range(10):
                    b_post(u, p, j)
                    if j < 5:
                        b_fill(u, j + 1)
                    if j == 9 and u.base < B_GROUPS - 1:
                        b_fill(u.plus(1), 0)
                    if mixed is not None and j < 9:
                        b_mix(mixed, 1 - p, j + 1)

            pool.dma_start(b_old[:], d["b_old"][0]).then_inc(b_old_in, 16)
            load_state(Count(0))
            b_fill(Count(0), 0)
            b_group(Count(0), 0, None)
            pool.wait_ge(gb_done, 1)
            b_group(Count(1), 1, Count(0))
            with pool.Fori(0, 2) as i:
                for n in range(2):
                    b_group(Count(2 + n, (i, 2)), n, Count(1 + n, (i, 2)))
            b_group(Count(6), 0, Count(5))
            b_group(Count(7), 1, Count(6))
            for j in range(10):
                b_mix(Count(7), 1, j)
            residual(3, Count(3 * KT), (b_glo, Count(4 * B_GROUPS)))
            ffn(1, 3)
            for t in range(4):
                until(y_ready, 4 * (t + 1))
                pool.dma_start(o["y"][:, 4 * t:4 * t + 4, :], x[:, 4 * t:4 * t + 4, :]).then_inc(y_stored, 16)
            pool.wait_ge(y_stored, 64)
            pool.wait_ge(f_new_out, 32)


def kernel(**inputs):
    import concourse.bacc as bacc
    from concourse.bass_utils import run_bass_kernel_spmd

    a = {k: np.asarray(v) for k, v in inputs.items()}

    def chunks(w, kt):
        k, n = w.shape
        w = w.reshape(k // (kt * P), kt, P, n // P, P).transpose(3, 0, 2, 1, 4)
        return w.reshape(-1, P, kt * P)

    def out_chunks(w):
        c = chunks(w, KT // 2)
        return c.reshape(-1, 2, P, CH // 2).transpose(0, 2, 1, 3).reshape(-1, P, CH)

    def tiles(v, *tail):
        v = v.reshape(v.shape[:-1] + (-1, P))
        v = np.moveaxis(v, (-1, -2), (0, 1))
        return v.reshape(v.shape[:2] + tail) if tail else v

    w = a["a_w_in"][0]
    hk = A_HEADS * A_DK
    q, k, v, og, gates = np.split(w, [hk, 2 * hk, 2 * hk + D_MODEL, 2 * hk + 2 * D_MODEL], axis=1)
    by_head = [z.reshape(D_MODEL, A_HEADS, -1) for z in (q, k, v, og)]
    wa_in = np.concatenate(by_head, axis=2).reshape(D_MODEL, -1)
    wa_gate = np.zeros((D_MODEL, P), np.float32)
    wa_gate[:, 0:8], wa_gate[:, 32:40] = gates[:, :8], gates[:, 8:]
    w = a["b_w_in"][0]
    z, xs, bm, cm, dt = np.split(w, [B_DINNER, 2 * B_DINNER, 2 * B_DINNER + 1024, 2 * B_DINNER + 2048], axis=1)

    def by_group(*parts):
        return np.concatenate([v.reshape(v.shape[:-1] + (B_GROUPS, -1)) for v in parts], axis=-1).reshape(parts[0].shape[:-1] + (-1,))

    def conv_by_group(v):
        xp, bp, cp = np.split(v, [B_DINNER, B_DINNER + 1024], axis=-1)
        return by_group(bp, cp, xp)

    wb_in = by_group(bm, cm, xs, z)
    wb_gate = np.zeros((D_MODEL, P), np.float32)
    wb_gate[:, 0:64] = dt

    def gate_value(v):
        s = v.shape[:-1]
        return np.swapaxes(v.reshape(s + (2, FT, P)), -3, -2).reshape(s + (-1,))

    f_tapb = np.concatenate([a["f_conv_w"], a["f_conv_b"][:, None]], axis=1)
    b_tapb = np.concatenate([a["b_conv_w"][0], a["b_conv_b"]], axis=0)
    x = np.concatenate([a["x_prompt"][0], a["x_sample"].reshape(TS, D_MODEL)], axis=0)
    s_idx, t_idx = np.arange(P)[:, None], np.arange(P)[None, :]
    future = np.zeros((P, SC), np.float32)
    future[:, 0:P] = future[:, TP:TP + P] = np.where(s_idx <= t_idx, 0.0, BIG)
    ss, tt = np.arange(TS)[:, None], np.arange(TS)[None, :]
    future[0:TS, TP + P:SC] = np.where((ss <= tt) & (ss // SL == tt // SL), 0.0, BIG)
    starts = [0] + [TP + SL * b for b in range(NB)]
    seg_keep = np.ones((64, T), np.float32)
    seg_keep[:, starts] = 0.0
    seg_drop = np.zeros((8, T), np.float32)
    seg_drop[:, starts] = -BIG
    ssm = a["state_ssm"][0].reshape(NB, 32, P, P)
    ins = {
        "x": tiles(x).astype(np.float32, copy=False),
        "ident": np.eye(P, dtype=np.float32),
        "mean_mat": np.full((P, P), 1.0 / D_MODEL, np.float32),
        "ones": np.ones((P, P), np.float32),
        "future": future, "seg_keep": seg_keep, "seg_drop": seg_drop,
        "in_batch": np.tile(ss // SL == np.arange(NB)[None, :], (3, 1)).astype(np.float32),
        "head_ident": np.tile(np.eye(64, dtype=np.float32), (2, 1)),
        "norm_w": np.moveaxis(tiles(np.concatenate([a["norm_mix"][0:1], a["norm_ffn"][0:1], a["norm_mix"][1:2],
                                                    a["norm_ffn"][1:2], a["norm_final"][None]])), 1, 2),
        "f_conv": np.moveaxis(tiles(gate_value(f_tapb)), 1, 2),
        "b_conv": tiles(conv_by_group(b_tapb)),
        "b_normw": tiles(a["b_norm_w"][0])[:, :, None],
        "b_skip": np.repeat(a["b_D"][0], 64).reshape(32, P).T[:, :, None],
        "b_small": np.stack([a["b_dt_bias"][0], a["b_A_log"][0]], axis=1),
        "a_small": np.concatenate([a["a_b_if"][0].reshape(2, 8).T, a["state_mlstm_m"][0].T], axis=1),
        "a_n": a["state_mlstm_n"][0].transpose(2, 1, 0),
        "a_c": a["state_mlstm_C"][0].transpose(1, 2, 0, 3),
        "f_old": np.stack([tiles(gate_value(s), NB * 2) for s in a["state_ffn_conv"]]),
        "b_old": np.moveaxis(tiles(conv_by_group(a["state_ssm_conv"][0]), NB * 3).reshape(P, B_GROUPS, 6, NB * 3), 1, 0),
        "b_sT": ssm.transpose(1, 3, 0, 2),
        "b_s": ssm.transpose(1, 2, 0, 3),
        "wa_gate": chunks(wa_gate, KT), "wa_in": chunks(wa_in, KT), 
        "wa_out": np.concatenate([out_chunks(a["a_w_out"][0][h * 1024:(h + 1) * 1024]) for h in range(2)]),
        "wb_gate": chunks(wb_gate, KT), "wb_in": chunks(wb_in, KT),
        "wb_out": np.concatenate([
            out_chunks(np.concatenate([a["b_w_out"][0][g * 512:(g + 1) * 512] for g in pair]))
            for pair in ((1, 2), (3, 4), (5, 6), (0, 7))]),
    }
    for l in range(2):
        ins[f"wf_up{l}"] = chunks(gate_value(a["f_w_up"][l]), KT)
        ins[f"wf_down{l}"] = np.concatenate([chunks(a["f_w_down"][l][h * FH * P:(h + 1) * FH * P], FH // 2) for h in range(2)])
    ins = {n: np.ascontiguousarray(v) for n, v in ins.items()}
    outs = {"y": (P, KT, T), "C_s": (A_HEADS, P, NB, A_DV), "C_p": (A_HEADS, P, A_DV), "n": (P, A_HEADS, 1 + NB),
            "m": (A_HEADS, 1 + NB), "ssm_s": (32, P, NB, P), "ssm_p": (32, P, P),
            "bconv": (B_GROUPS, P, 6, (1 + NB) * 3), "fconv": (2, P, 2 * FT, (1 + NB) * 2)}
    nc = bacc.Bacc("TRN2", target_bir_lowering=False, num_devices=1, dynamic_dma_scratch_size=8192)
    d = {n: nc.dram_tensor(n + "_in", v.shape, F32, kind="ExternalInput").ap() for n, v in ins.items()}
    o = {n: nc.dram_tensor(n + "_out", s, F32, kind="ExternalOutput").ap() for n, s in outs.items()}
    trunk(nc, d, o)
    r = run_bass_kernel_spmd(nc, [{n + "_in": v for n, v in ins.items()}], core_ids=[0]).results[0]
    r = {n: np.asarray(r[n + "_out"]) for n in outs}

    y = r["y"].transpose(2, 1, 0).reshape(T, D_MODEL)
    C_s = r["C_s"].transpose(2, 0, 1, 3)[None]
    n_all = r["n"].transpose(2, 1, 0)
    m_all = r["m"].T
    ssm_s = r["ssm_s"].transpose(2, 0, 1, 3).reshape(NB, B_HEADS, 64, P)[None]
    ssm_p = r["ssm_p"].reshape(1, 1, B_HEADS, 64, P)
    bc = r["bconv"].reshape(B_GROUPS, P, 6, 1 + NB, 3).transpose(3, 4, 0, 2, 1)
    bc = np.concatenate([bc[:, :, :, 2:6].reshape(1 + NB, 3, -1), bc[:, :, :, 0].reshape(1 + NB, 3, -1),
                         bc[:, :, :, 1].reshape(1 + NB, 3, -1)], axis=-1)
    fc = r["fconv"].reshape(2, P, FT, 2, 1 + NB, 2).transpose(0, 4, 5, 3, 2, 1).reshape(2, 1 + NB, 2, 2 * D_FF)
    out = (y[None, :TP], y[TP:].reshape(NB, SL, D_MODEL), r["C_p"][None, None], C_s,
           n_all[None, 0:1], n_all[None, 1:], m_all[None, 0:1], m_all[None, 1:], ssm_p, ssm_s,
           bc[None, 0:1], bc[None, 1:], fc[:, 0:1], fc[:, 1:])
    return tuple(np.ascontiguousarray(v) for v in out)
```
